# Optimizing a Trainium2 kernel written in Bass

```python
import jax, jax.numpy as jnp
from jax import lax
import numpy as np
import math

D_MODEL = 1024
BATCH = 1
SEQ = 256
DEPTH = 2

GDN_HEADS = D_MODEL // 256
GDN_DK = 128
GDN_DV = 128
GDN_CONV = 4
GDN_CHUNK = 64
MOBA_HEADS = D_MODEL // 128
MOBA_DH = 64
MOBA_BLOCK = 256
MOBA_TOPK = 3
MOBA_QCHUNK = 32
ROPE_DIMS = MOBA_DH // 4
ROPE_THETA = 500000.0
GDN_QK_W = GDN_HEADS * GDN_DK
GDN_V_W = GDN_HEADS * GDN_DV
MOBA_W = MOBA_HEADS * MOBA_DH
D_MIX = GDN_V_W + MOBA_W
IN_SPLITS = (GDN_QK_W, GDN_QK_W, GDN_V_W, GDN_HEADS, GDN_HEADS, GDN_V_W, MOBA_W, MOBA_W, MOBA_W)
N_IN = sum(IN_SPLITS)
D_FF = 256 * ((8 * D_MODEL // 3 + 255) // 256)
FFN_CONV = 3
DEEPNORM_ALPHA = (2 * DEPTH) ** 0.25
DEEPNORM_BETA = (8 * DEPTH) ** -0.25
LN_EPS = 1e-5
NORM_EPS = 1e-6


def layer_norm(x, g, b):
    xf = x.astype(jnp.float32)
    mu = xf.mean(-1, keepdims=True)
    var = jnp.square(xf - mu).mean(-1, keepdims=True)
    return ((xf - mu) * lax.rsqrt(var + LN_EPS) * g + b).astype(x.dtype)

def causal_dwconv(x, w):
    k_w = w.shape[0]
    s = x.shape[1]
    xp = jnp.pad(x, ((0, 0), (k_w - 1, 0), (0, 0)))
    return sum(xp[:, j:j + s, :] * w[j] for j in range(k_w))

def l2norm(x):
    return x * lax.rsqrt(jnp.sum(x * x, -1, keepdims=True) + NORM_EPS)

def split_heads(t, n_heads):
    b, s, _ = t.shape
    return t.reshape(b, s, n_heads, -1).transpose(0, 2, 1, 3)

def partial_rotary(x, pos):
    half = ROPE_DIMS // 2
    inv = ROPE_THETA ** (-jnp.arange(half, dtype=jnp.float32) / half)
    ang = pos.astype(jnp.float32)[:, None] * inv[None, :]
    cos = jnp.cos(ang).astype(x.dtype)
    sin = jnp.sin(ang).astype(x.dtype)
    x1, x2, rest = x[..., :half], x[..., half:ROPE_DIMS], x[..., ROPE_DIMS:]
    return jnp.concatenate([x1 * cos - x2 * sin, x2 * cos + x1 * sin, rest], -1)

def gated_delta_rule(q, k, v, g, beta):
    b_, h, s, dk = q.shape
    dv = v.shape[-1]
    c = GDN_CHUNK
    n = s // c
    q = q * dk ** -0.5
    resh = lambda t: t.reshape(b_, h, n, c, *t.shape[3:])
    q, k, v, g, beta = map(resh, (q, k, v, g, beta))
    g = jnp.cumsum(g, axis=-1)
    idx = jnp.arange(c)
    lower_incl = idx[:, None] >= idx[None, :]
    decay = jnp.exp(jnp.where(lower_incl, g[..., :, None] - g[..., None, :], -jnp.inf))
    k_beta = k * beta[..., None]
    a_strict = jnp.where(idx[:, None] > idx[None, :],
                         jnp.einsum('bhncd,bhnmd->bhncm', k_beta, k) * decay, 0.0)
    t_mat = a_strict + jnp.eye(c, dtype=q.dtype)
    rhs = jnp.concatenate([v * beta[..., None], k_beta * jnp.exp(g)[..., None]], -1)
    sol = lax.linalg.triangular_solve(t_mat, rhs, left_side=True, lower=True, unit_diagonal=True)
    u, w = sol[..., :dv], sol[..., dv:]
    attn_intra = jnp.einsum('bhncd,bhnmd->bhncm', q, k) * decay
    q_dec = q * jnp.exp(g)[..., None]
    g_last = g[..., -1]
    k_dec = k * jnp.exp(g_last[..., None] - g)[..., None]

    def step(state, xs):
        q_c, k_c, u_c, w_c, a_c, gl = xs
        v_new = u_c - jnp.einsum('bhcd,bhde->bhce', w_c, state)
        o = jnp.einsum('bhcd,bhde->bhce', q_c, state) + jnp.einsum('bhcm,bhme->bhce', a_c, v_new)
        state = state * jnp.exp(gl)[..., None, None] + jnp.einsum('bhcd,bhce->bhde', k_c, v_new)
        return state, o

    xs = tuple(jnp.moveaxis(t, 2, 0) for t in (q_dec, k_dec, u, w, attn_intra, g_last))
    s0 = jnp.zeros((b_, h, dk, dv), q.dtype)
    _, o = lax.scan(step, s0, xs)
    return jnp.moveaxis(o, 0, 2).reshape(b_, h, s, dv)

def gdn_mixer(q, k, v, a_logit, b_logit, z, conv_w, a_log, dt_bias, norm_g):
    b_, s, _ = q.shape
    qkv = jax.nn.silu(causal_dwconv(jnp.concatenate([q, k, v], -1), conv_w))
    q, k, v = jnp.split(qkv, [GDN_QK_W, 2 * GDN_QK_W], -1)
    f32 = jnp.float32
    qh = l2norm(split_heads(q, GDN_HEADS).astype(f32))
    kh = l2norm(split_heads(k, GDN_HEADS).astype(f32))
    vh = split_heads(v, GDN_HEADS).astype(f32)
    beta = jax.nn.sigmoid(b_logit.astype(f32)).transpose(0, 2, 1)
    g = (-jnp.exp(a_log.astype(f32)) * jax.nn.softplus(a_logit.astype(f32) + dt_bias.astype(f32))).transpose(0, 2, 1)
    o = gated_delta_rule(qh, kh, vh, g, beta).transpose(0, 2, 1, 3)
    o = o * lax.rsqrt(jnp.mean(o * o, -1, keepdims=True) + NORM_EPS) * norm_g.astype(f32)
    o = o * jax.nn.silu(z.reshape(b_, s, GDN_HEADS, GDN_DV).astype(f32))
    return o.reshape(b_, s, GDN_V_W).astype(q.dtype)

def moba_mixer(q, k, v, pos):
    b_, s, _ = q.shape
    h, dh, blk, qc_len = MOBA_HEADS, MOBA_DH, MOBA_BLOCK, MOBA_QCHUNK
    qh = partial_rotary(split_heads(q, h), pos)
    kh = partial_rotary(split_heads(k, h), pos)
    vh = split_heads(v, h)
    nb = -(-s // blk)
    pad = nb * blk - s
    n_sel = min(MOBA_TOPK, nb)
    kb = jnp.pad(kh, ((0, 0), (0, 0), (0, pad), (0, 0))).reshape(b_, h, nb, blk, dh)
    vb = jnp.pad(vh, ((0, 0), (0, 0), (0, pad), (0, 0))).reshape(b_, h, nb, blk, dh)
    k_mean = kb.mean(axis=3)
    nq = s // qc_len
    q_chunks = jnp.moveaxis(qh.reshape(b_, h, nq, qc_len, dh), 2, 0)
    scale = dh ** -0.5
    bi = jnp.arange(b_)[:, None, None, None]
    hi = jnp.arange(h)[None, :, None, None]
    blk_ids = jnp.arange(nb)
    sel_rank = jnp.arange(n_sel)

    def attend(args):
        q_c, ci = args
        t = ci * qc_len + jnp.arange(qc_len)
        own = (ci * qc_len) // blk
        gate = jnp.einsum('bhqd,bhnd->bhqn', q_c, k_mean).astype(jnp.float32)
        gate = jnp.where(blk_ids < own, gate, -jnp.inf)
        _, sel = lax.top_k(gate, n_sel)
        sel_valid = sel_rank < own
        k_sel = kb[bi, hi, sel]
        v_sel = vb[bi, hi, sel]
        s_sel = jnp.einsum('bhqd,bhqjkd->bhqjk', q_c, k_sel).astype(jnp.float32) * scale
        s_sel = jnp.where(sel_valid[:, None], s_sel, -jnp.inf).reshape(b_, h, qc_len, n_sel * blk)
        k_own = lax.dynamic_index_in_dim(kb, own, axis=2, keepdims=False)
        v_own = lax.dynamic_index_in_dim(vb, own, axis=2, keepdims=False)
        s_own = jnp.einsum('bhqd,bhkd->bhqk', q_c, k_own).astype(jnp.float32) * scale
        key_pos = own * blk + jnp.arange(blk)
        s_own = jnp.where(key_pos[None, :] <= t[:, None], s_own, -jnp.inf)
        p = jax.nn.softmax(jnp.concatenate([s_own, s_sel], -1), axis=-1).astype(v_sel.dtype)
        p_own = p[..., :blk]
        p_sel = p[..., blk:].reshape(b_, h, qc_len, n_sel, blk)
        return (jnp.einsum('bhqk,bhkd->bhqd', p_own, v_own)
                + jnp.einsum('bhqjk,bhqjkd->bhqd', p_sel, v_sel))

    o = lax.map(attend, (q_chunks, jnp.arange(nq)))
    o = jnp.moveaxis(o, 0, 2).reshape(b_, h, s, dh)
    return o.transpose(0, 2, 1, 3).reshape(b_, s, MOBA_W)

def hybrid_layer(x, w_in, gdn_conv_w, gdn_a_log, gdn_dt_bias, gdn_norm_g, w_out,
                 ln1_g, ln1_b, w_up, ffn_conv_w, ffn_conv_b, w_down, ln2_g, ln2_b, pos):
    proj = x @ w_in
    offs = np.cumsum(IN_SPLITS)[:-1].tolist()
    q_a, k_a, v_a, a_logit, b_logit, z, q_b, k_b, v_b = jnp.split(proj, offs, -1)
    o_a = gdn_mixer(q_a, k_a, v_a, a_logit, b_logit, z, gdn_conv_w, gdn_a_log, gdn_dt_bias, gdn_norm_g)
    o_b = moba_mixer(q_b, k_b, v_b, pos)
    mix = jnp.concatenate([o_a, o_b], -1) @ w_out
    x = layer_norm(DEEPNORM_ALPHA * x + mix, ln1_g, ln1_b)
    hid = causal_dwconv(x @ w_up, ffn_conv_w) + ffn_conv_b
    gate, val = jnp.split(hid, 2, -1)
    ffn = (jax.nn.silu(gate) * val) @ w_down
    return layer_norm(DEEPNORM_ALPHA * x + ffn, ln2_g, ln2_b)

def first_inputs(seed: int = 0) -> dict:
    key = jax.random.key(seed)
    ks = jax.random.split(key, 16)
    f = jnp.float32
    nrm = lambda k, shape, scale: jax.random.normal(k, shape, f) * scale
    x = jax.random.normal(ks[0], (BATCH, SEQ, D_MODEL), f)
    w_in = nrm(ks[1], (DEPTH, D_MODEL, N_IN), D_MODEL ** -0.5)
    gdn_conv_w = nrm(ks[2], (DEPTH, GDN_CONV, 2 * GDN_QK_W + GDN_V_W), GDN_CONV ** -0.5)
    gdn_a_log = jnp.log(jax.random.uniform(ks[3], (DEPTH, GDN_HEADS), f, 1.0, 16.0))
    dt = jnp.exp(jax.random.uniform(ks[4], (DEPTH, GDN_HEADS), f, float(np.log(1e-3)), float(np.log(1e-1))))
    gdn_dt_bias = dt + jnp.log(-jnp.expm1(-dt))
    gdn_norm_g = 1.0 + nrm(ks[5], (DEPTH, GDN_DV), 0.02)
    w_out = nrm(ks[6], (DEPTH, D_MIX, D_MODEL), DEEPNORM_BETA * D_MIX ** -0.5)
    ln1_g = 1.0 + nrm(ks[7], (DEPTH, D_MODEL), 0.02)
    ln1_b = nrm(ks[8], (DEPTH, D_MODEL), 0.02)
    w_up = nrm(ks[9], (DEPTH, D_MODEL, 2 * D_FF), D_MODEL ** -0.5)
    ffn_conv_w = nrm(ks[10], (DEPTH, FFN_CONV, 2 * D_FF), FFN_CONV ** -0.5)
    ffn_conv_b = nrm(ks[11], (DEPTH, 2 * D_FF), 0.01)
    w_down = nrm(ks[12], (DEPTH, D_FF, D_MODEL), DEEPNORM_BETA * D_FF ** -0.5)
    ln2_g = 1.0 + nrm(ks[13], (DEPTH, D_MODEL), 0.02)
    ln2_b = nrm(ks[14], (DEPTH, D_MODEL), 0.02)
    return {'x': x, 'w_in': w_in, 'gdn_conv_w': gdn_conv_w, 'gdn_a_log': gdn_a_log,
            'gdn_dt_bias': gdn_dt_bias, 'gdn_norm_g': gdn_norm_g, 'w_out': w_out,
            'ln1_g': ln1_g, 'ln1_b': ln1_b, 'w_up': w_up, 'ffn_conv_w': ffn_conv_w,
            'ffn_conv_b': ffn_conv_b, 'w_down': w_down, 'ln2_g': ln2_g, 'ln2_b': ln2_b}

def first_block(x, w_in, gdn_conv_w, gdn_a_log, gdn_dt_bias, gdn_norm_g, w_out,
              ln1_g, ln1_b, w_up, ffn_conv_w, ffn_conv_b, w_down, ln2_g, ln2_b):
    pos = jnp.arange(x.shape[1], dtype=jnp.int32)
    for l in range(DEPTH):
        x = hybrid_layer(x, w_in[l], gdn_conv_w[l], gdn_a_log[l], gdn_dt_bias[l], gdn_norm_g[l],
                         w_out[l], ln1_g[l], ln1_b[l], w_up[l], ffn_conv_w[l], ffn_conv_b[l],
                         w_down[l], ln2_g[l], ln2_b[l], pos)
    return x


DEPTH_2 = 1

HEAD_DIM = 64
N_DIFF_HEADS = D_MODEL // 2 // (2 * HEAD_DIM)
DIFF_WIDTH = N_DIFF_HEADS * 2 * HEAD_DIM
N_DIL_HEADS = D_MODEL // 2 // HEAD_DIM
DIL_WIDTH = N_DIL_HEADS * HEAD_DIM
MIX_WIDTH = DIFF_WIDTH + DIL_WIDTH
DIL_PATTERNS = ((128, 1), (512, 4), (2048, 16))
N_BUCKETS = 32
REL_MAX_DIST = 1024
Q_BLOCK = 128
N_EXPERTS = 16
EC_K = 2
D_FF_2 = 256 * ((8 * D_MODEL // 3 + 255) // 256)
SUBLN_EPS = 1e-5
NEG = -1e30


def rms_norm(x, g, eps=NORM_EPS):
    xf = x.astype(jnp.float32)
    y = xf * lax.rsqrt(jnp.mean(xf * xf, axis=-1, keepdims=True) + eps)
    return (y * g.astype(jnp.float32)).astype(x.dtype)

def t5_bucket(rel):
    half = N_BUCKETS // 2
    max_exact = half // 2
    n = jnp.abs(rel)
    nf = jnp.maximum(n, 1).astype(jnp.float32)
    large = max_exact + (jnp.log(nf / max_exact) / math.log(REL_MAX_DIST / max_exact)
                         * (half - max_exact)).astype(jnp.int32)
    large = jnp.minimum(large, half - 1)
    return jnp.where(rel > 0, half, 0) + jnp.where(n < max_exact, n, large)

def diff_attention(qa, ka, va, lam, lambda_init, subln_g, bias_a):
    B, S = qa.shape[:2]
    H = N_DIFF_HEADS
    q = qa.reshape(B, S, H, 2, HEAD_DIM) * (HEAD_DIM ** -0.5)
    k = ka.reshape(B, S, H, 2, HEAD_DIM)
    k1 = k[:, :, :, 0].transpose(0, 2, 1, 3)
    k2 = k[:, :, :, 1].transpose(0, 2, 1, 3)
    v = va.reshape(B, S, H, 2 * HEAD_DIM).transpose(0, 2, 1, 3)
    n_blk = S // Q_BLOCK

    def to_qblocks(t):
        return t.reshape(B, n_blk, Q_BLOCK, H, HEAD_DIM).transpose(1, 0, 3, 2, 4)

    q1b = to_qblocks(q[:, :, :, 0])
    q2b = to_qblocks(q[:, :, :, 1])
    kpos = jnp.arange(S, dtype=jnp.int32)

    def block(args):
        j, q1, q2 = args
        qpos = j * Q_BLOCK + jnp.arange(Q_BLOCK, dtype=jnp.int32)
        bias = jnp.take(bias_a, t5_bucket(kpos[None, :] - qpos[:, None]), axis=0)
        bias = bias.transpose(2, 0, 1).astype(jnp.float32)[None]
        s1 = jnp.einsum('bhqd,bhkd->bhqk', q1, k1).astype(jnp.float32) + bias
        s2 = jnp.einsum('bhqd,bhkd->bhqk', q2, k2).astype(jnp.float32) + bias
        p = jax.nn.softmax(s1, axis=-1) - lam * jax.nn.softmax(s2, axis=-1)
        return jnp.einsum('bhqk,bhkd->bhqd', p.astype(v.dtype), v)

    o = lax.map(block, (jnp.arange(n_blk, dtype=jnp.int32), q1b, q2b))
    o = o.transpose(1, 0, 3, 2, 4).reshape(B, S, H, 2 * HEAD_DIM)
    o = rms_norm(o, subln_g, SUBLN_EPS) * (1.0 - lambda_init)
    return o.reshape(B, S, DIFF_WIDTH)

def dilated_pattern(q, k, v, window, dil, bias_b):
    B, S, H, Dh = q.shape
    half = window // (2 * dil)
    blk = half
    unit = dil * blk
    sp = -(-S // unit) * unit
    m_len = sp // dil
    nb = m_len // blk

    def to_blocks(t):
        t = jnp.pad(t, ((0, 0), (0, sp - S), (0, 0), (0, 0)))
        t = t.reshape(B, m_len, dil, H, Dh).transpose(0, 2, 3, 1, 4)
        return t.reshape(B, dil, H, nb, blk, Dh)

    def with_neighbours(t):
        tp = jnp.pad(t, ((0, 0), (0, 0), (0, 0), (1, 1), (0, 0), (0, 0)))
        return jnp.concatenate([tp[:, :, :, :-2], tp[:, :, :, 1:-1], tp[:, :, :, 2:]], axis=4)

    qb = to_blocks(q * (Dh ** -0.5))
    kn = with_neighbours(to_blocks(k))
    vn = with_neighbours(to_blocks(v))
    off = (jnp.arange(3 * blk, dtype=jnp.int32)[None, :] - blk
           - jnp.arange(blk, dtype=jnp.int32)[:, None])
    in_band = jnp.abs(off) <= half
    m_key = (jnp.arange(nb, dtype=jnp.int32)[:, None] * blk
             + jnp.arange(3 * blk, dtype=jnp.int32)[None, :] - blk)
    pos_key = m_key[None] * dil + jnp.arange(dil, dtype=jnp.int32)[:, None, None]
    key_ok = (m_key >= 0)[None] & (pos_key < S)
    mask = key_ok[:, :, None, :] & in_band[None, None]
    bias = jnp.take(bias_b, t5_bucket(off * dil), axis=0).transpose(2, 0, 1).astype(jnp.float32)
    s = jnp.einsum('brhnqd,brhnkd->brhnqk', qb, kn).astype(jnp.float32) + bias[None, None, :, None]
    s = jnp.where(mask[None, :, None], s, NEG)
    lse = jax.nn.logsumexp(s, axis=-1)
    p = jnp.exp(s - lse[..., None])
    o = jnp.einsum('brhnqk,brhnkd->brhnqd', p.astype(v.dtype), vn)
    o = o.reshape(B, dil, H, m_len, Dh).transpose(0, 3, 1, 2, 4).reshape(B, sp, H, Dh)[:, :S]
    lse = lse.reshape(B, dil, H, m_len).transpose(0, 3, 1, 2).reshape(B, sp, H)[:, :S]
    return o, lse

def dilated_attention(qd, kd, vd, bias_b):
    B, S = qd.shape[:2]
    q = qd.reshape(B, S, N_DIL_HEADS, HEAD_DIM)
    k = kd.reshape(B, S, N_DIL_HEADS, HEAD_DIM)
    v = vd.reshape(B, S, N_DIL_HEADS, HEAD_DIM)
    outs, lses = [], []
    for window, dil in DIL_PATTERNS:
        o, lse = dilated_pattern(q, k, v, window, dil, bias_b)
        outs.append(o)
        lses.append(lse)
    w = jax.nn.softmax(jnp.stack(lses, axis=0), axis=0)
    o = jnp.sum(w[..., None] * jnp.stack(outs, axis=0).astype(jnp.float32), axis=0)
    return o.astype(qd.dtype).reshape(B, S, DIL_WIDTH)

def expert_choice_ffn(h, w_router, w_gate, w_up, w_down):
    B, S, D = h.shape
    cap = EC_K * S // N_EXPERTS
    aff = jax.nn.softmax((h @ w_router).astype(jnp.float32), axis=-1)
    g, idx = lax.top_k(aff.transpose(0, 2, 1), cap)
    g = g.transpose(1, 0, 2)
    idx = idx.transpose(1, 0, 2)
    b_rows = jnp.arange(B, dtype=jnp.int32)[:, None]

    def run_expert(args):
        wg, wu, wd, ie, ge = args
        xe = h[b_rows, ie]
        he = jax.nn.silu(xe @ wg) * (xe @ wu)
        return (he @ wd) * ge[..., None].astype(h.dtype)

    ye = lax.map(run_expert, (w_gate, w_up, w_down, idx, g))
    b_idx = jnp.arange(B, dtype=jnp.int32)[None, :, None]
    return jnp.zeros_like(h).at[b_idx, idx].add(ye)

def second_inputs(seed: int = 0) -> dict:
    key = jax.random.key(seed)
    ks = jax.random.split(key, 16)
    f = jnp.float32
    n_in = 3 * DIFF_WIDTH + 3 * DIL_WIDTH
    nrm = lambda k, shape, s: jax.random.normal(k, shape, f) * s
    return {
        'x': nrm(ks[0], (BATCH, SEQ, D_MODEL), 1.0),
        'norm1_g': 1.0 + nrm(ks[1], (DEPTH_2, D_MODEL), 0.02),
        'w_in': nrm(ks[2], (DEPTH_2, D_MODEL, n_in), D_MODEL ** -0.5),
        'lam_q1': nrm(ks[3], (DEPTH_2, HEAD_DIM), 0.1),
        'lam_k1': nrm(ks[4], (DEPTH_2, HEAD_DIM), 0.1),
        'lam_q2': nrm(ks[5], (DEPTH_2, HEAD_DIM), 0.1),
        'lam_k2': nrm(ks[6], (DEPTH_2, HEAD_DIM), 0.1),
        'subln_g': 1.0 + nrm(ks[7], (DEPTH_2, 2 * HEAD_DIM), 0.02),
        'w_out': nrm(ks[8], (DEPTH_2, MIX_WIDTH, D_MODEL), MIX_WIDTH ** -0.5),
        'rel_bias': nrm(ks[9], (N_BUCKETS, N_DIFF_HEADS + N_DIL_HEADS), 0.2),
        'norm2_g': 1.0 + nrm(ks[10], (DEPTH_2, D_MODEL), 0.02),
        'w_router': nrm(ks[11], (DEPTH_2, D_MODEL, N_EXPERTS), D_MODEL ** -0.5),
        'w_gate': nrm(ks[12], (DEPTH_2, N_EXPERTS, D_MODEL, D_FF_2), D_MODEL ** -0.5),
        'w_up': nrm(ks[13], (DEPTH_2, N_EXPERTS, D_MODEL, D_FF_2), D_MODEL ** -0.5),
        'w_down': nrm(ks[14], (DEPTH_2, N_EXPERTS, D_FF_2, D_MODEL), D_FF_2 ** -0.5),
        'norm_f_g': 1.0 + nrm(ks[15], (D_MODEL,), 0.02),
    }

def second_block(x, norm1_g, w_in, lam_q1, lam_k1, lam_q2, lam_k2, subln_g, w_out, rel_bias,
              norm2_g, w_router, w_gate, w_up, w_down, norm_f_g):
    splits = [DIFF_WIDTH, 2 * DIFF_WIDTH, 3 * DIFF_WIDTH,
              3 * DIFF_WIDTH + DIL_WIDTH, 3 * DIFF_WIDTH + 2 * DIL_WIDTH]
    bias_a = rel_bias[:, :N_DIFF_HEADS]
    bias_b = rel_bias[:, N_DIFF_HEADS:]
    for l in range(DEPTH_2):
        lambda_init = 0.8 - 0.6 * math.exp(-0.3 * l)
        h = rms_norm(x, norm1_g[l])
        proj = h @ w_in[l]
        qa, ka, va, qd, kd, vd = jnp.split(proj, splits, axis=-1)
        lam = (jnp.exp(jnp.sum(lam_q1[l].astype(jnp.float32) * lam_k1[l].astype(jnp.float32)))
               - jnp.exp(jnp.sum(lam_q2[l].astype(jnp.float32) * lam_k2[l].astype(jnp.float32)))
               + lambda_init)
        oa = diff_attention(qa, ka, va, lam, lambda_init, subln_g[l], bias_a)
        od = dilated_attention(qd, kd, vd, bias_b)
        x = x + jnp.concatenate([oa, od], axis=-1) @ w_out[l]
        x = x + expert_choice_ffn(rms_norm(x, norm2_g[l]), w_router[l], w_gate[l], w_up[l], w_down[l])
    return rms_norm(x, norm_f_g)


def setup_inputs(seed=0):
    out = dict(first_inputs(seed))
    for name, value in second_inputs(seed + 1).items():
        if name != "x":
            out[name + "_2"] = value
    return out


def reference(
    x, w_in, gdn_conv_w, gdn_a_log, gdn_dt_bias, gdn_norm_g, w_out, ln1_g, ln1_b, w_up,
    ffn_conv_w, ffn_conv_b, w_down, ln2_g, ln2_b, norm1_g_2, w_in_2, lam_q1_2, lam_k1_2,
    lam_q2_2, lam_k2_2, subln_g_2, w_out_2, rel_bias_2, norm2_g_2, w_router_2, w_gate_2, w_up_2,
    w_down_2, norm_f_g_2,
):
    x = first_block(
        x, w_in, gdn_conv_w, gdn_a_log, gdn_dt_bias, gdn_norm_g, w_out, ln1_g, ln1_b, w_up,
        ffn_conv_w, ffn_conv_b, w_down, ln2_g, ln2_b,
    )
    return second_block(
        x, norm1_g_2, w_in_2, lam_q1_2, lam_k1_2, lam_q2_2, lam_k2_2, subln_g_2, w_out_2,
        rel_bias_2, norm2_g_2, w_router_2, w_gate_2, w_up_2, w_down_2, norm_f_g_2,
    )


_drawn_inputs = setup_inputs


def setup_inputs(seed=0):
    import zlib

    import numpy as np

    out = dict(_drawn_inputs(seed))
    spreads = {}
    factors = {'gdn_norm_g': 5.669,
     'ffn_conv_b': 5.227,
     'norm1_g_2': 2.776,
     'lam_q2_2': 5.885,
     'lam_k2_2': 4.862,
     'subln_g_2': 4.244,
     'norm2_g_2': 3.745,
     'norm_f_g_2': 2.871}
    for name, (base, spread) in spreads.items():
        noise = np.random.default_rng([zlib.crc32(name.encode()), seed]).standard_normal(out[name].shape)
        drawn = base * np.exp(spread * noise) if base else spread * noise
        out[name] = __import__('jax').numpy.asarray(drawn.astype(out[name].dtype))
    for name, factor in factors.items():
        out[name] = (out[name] * factor).astype(out[name].dtype)
    return out
```

```python
import numpy as np
from contextlib import ExitStack

import concourse.bass as bass
from concourse import mybir

F32 = mybir.dt.float32
U32 = mybir.dt.uint32
ACT = mybir.ActivationFunctionType
ALU = mybir.AluOpType
AX = mybir.AxisListType

P = 128
S = 256
T = S // P
D = 1024
KT = D // P
DEPTH = 2
H = 4
DK = 128
QKV = 3 * H * DK
CHUNK = 64
FF = 2816
FT = FF // P
TAPS, FTAPS = 4, 3
ROPE_HALF, ROPE_THETA, DH = 8, 500000.0, 64
NE, CAP = 16, 32
BUCKETS, BIAS_HEADS = 32, 12
ALPHA = (2 * DEPTH) ** 0.25
LN_EPS, NORM_EPS, SUBLN_EPS = 1e-5, 1e-6, 1e-5
LAMBDA_INIT = 0.2
NEG = -1e30

RING = 4
SBUF_FLOATS = 53200
SLOT = 4096
OFF = {"q": 0, "k": 512, "v": 1024, "ab": 1536, "z": 1544, "qb": 2056, "kb": 2568, "vb": 3080}
UNITS_IN = ["q", "k", "v", "ab", "qb", "kb", "z", "vb"]
U_OUT, U_UP, U_DOWN = 8, 10, 21
DOWN_TILES = [4, 3, 3, 3, 3, 3, 3]
UNITS = 28
ROW_UNITS = 2 + len(DOWN_TILES)
UNITS_IN_2 = [0, 512, 1024, 1536, 2048, 2560]
GU_RING, D_RING = 4, 11
HALF = FF // 2
HT = HALF // P
PIECES = [(0, 512), (512, 512), (1024, 384)]
HID_BANKS, OUT_BANKS = (3, 4, 6), (6, 7, 3, 4)


def constants():
    i = np.arange(P)[:, None]
    j = np.arange(P)[None, :]
    same = (i // CHUNK) == (j // CHUNK)
    neg = lambda ok: np.where(ok, 0.0, NEG)
    parts = {
        "ident": (i == j) * 1.0,
        "ones": np.ones((P, P)),
        "cum": (same & (i <= j)) * 1.0,
        "neg_strict": neg(same & (i > j)),
        "neg_incl_t": neg(same & (i <= j)),
    }
    for n in range(6):
        s = 1 << n
        parts[f"level{n}"] = ((i // (2 * s) == j // (2 * s)) & (i % (2 * s) >= s) & (j % (2 * s) < s)) * 1.0
    rot = np.zeros((P, P))
    cos, sin = np.ones((P, S)), np.zeros((P, S))
    inv = np.float32(ROPE_THETA) ** (-np.arange(ROPE_HALF, dtype=np.float32) / np.float32(ROPE_HALF))
    ang = np.arange(S, dtype=np.float32)[:, None] * inv[None, :].astype(np.float32)
    for h in range(P // DH):
        for c in range(ROPE_HALF):
            a, b = h * DH + c, h * DH + ROPE_HALF + c
            rot[b, a], rot[a, b] = -1.0, 1.0
            cos[[a, b]] = np.cos(ang[:, c])
            sin[[a, b]] = np.sin(ang[:, c])
    parts["rot"], parts["cos"], parts["sin"] = rot, cos, sin
    jj = np.arange(3 * P)[None, :]
    parts["causal"] = neg(jj <= i + P)
    parts["tok_row"] = np.broadcast_to(np.arange(S)[None, :], (P, S))
    parts["tok_col"] = np.concatenate([i, i + P], 1)
    own = (np.arange(NE)[:, None] == (np.arange(NE * CAP) // CAP)[None, :]) * 1.0
    parts["own"] = np.concatenate([own, np.zeros((P - NE, NE * CAP))])
    at, cols = {}, 0
    for name, a in parts.items():
        at[name] = (cols, a.shape[1])
        cols += a.shape[1]
    return np.ascontiguousarray(np.concatenate([np.asarray(a, np.float32) for a in parts.values()], 1)), at


def bias_tables():
    rel = np.arange(-(S - 1), S + 1)
    n = np.abs(rel)
    half, exact = BUCKETS // 2, BUCKETS // 4
    nf = np.maximum(n, 1).astype(np.float32)
    large = exact + (np.log(nf / np.float32(exact)) / np.float32(np.log(1024 / exact)) * np.float32(half - exact)).astype(np.int32)
    bucket = np.where(rel > 0, half, 0) + np.where(n < exact, n, np.minimum(large, half - 1))
    count = (n <= 64) * 1 + (rel % 4 == 0) * 1 + (rel % 16 == 0) * 1
    table = np.zeros((BUCKETS + 1, 2 * S), np.float32)
    table[bucket, np.arange(2 * S)] = 1.0
    table[BUCKETS] = np.where(count > 0, np.log(np.maximum(count, 1)), NEG)
    takes = np.zeros((1, BIAS_HEADS), np.float32)
    takes[0, H:] = 1.0
    return table, takes


PER = dict(
    x_rows=4, xT_ready=8, x_tr=8, conv_rows=64, small=48, ln1=32, ln2=32, cw_tr=1, cw_ready=1,
    proj=14, tap=6, taps=6, silu=6, act_evac=8, ab_mm=1, ab_pre=1, ab_act=1, g_ready=1,
    sq=4, l2_mm=4, l2_sum=4, l2_rs=4, qk_norm=4, cum_mm=1, cum_read=1, arg_ready=1, dec=1, rows_tr=4, rows_a=1, rows_v=1,
    kk_mm=1, a_ready=1, x_mm=12, x_evac=12, ed_mm=12, e_ready=12, lvl=12, sol_mm=2, u_ready=1, w_ready2=1,
    qdec=1, pv_mm=3, vnew=4, st_mm=3, state=3, o_step=4, o_sq=2, o_sum=2, o_rs=2, o_rows=2, zg=1, o_tr=2, mix_o=2,
    rot_mm=4, rotated=4, at_s=8, at_read=8, at_exp=8, at_prob=8, at_tr=8, at_pt=8, at_pv=4, at_out=4,
    mo_mm=1, y_stat=4, y_rs=4, up=22, up_act=22, up_dve=22, up_silu=22, hid=22, dn_mm=1,
)


def build(nc, a, out, scratch, CAT, STOP=None):
    ctx = ExitStack()
    with ctx:
        free = SBUF_FLOATS
        arena = ctx.enter_context(nc.sbuf_tensor("arena", [P, free], F32))
        ps = [ctx.enter_context(nc.psum_tensor(f"bank{i}", [P, 512], F32)) for i in range(8)]
        sems = {}

        def sem(name):
            if name not in sems:
                sems[name] = ctx.enter_context(nc.semaphore(name))
            return sems[name]

        def at(l, name, k):
            return l * PER[name] + k

        class Region:
            def __init__(self, lo, hi):
                self.at, self.hi = lo, hi

            def take(self, *dims):
                n = int(np.prod(dims))
                assert self.at + n <= self.hi, (dims, self.at, n, self.hi)
                v = arena[:, self.at:self.at + n]
                self.at += n
                if len(dims) == 2:
                    v = v.rearrange("p (x y) -> p x y", y=dims[1])
                if len(dims) == 3:
                    v = v.rearrange("p (x y z) -> p x y z", y=dims[1], z=dims[2])
                if len(dims) == 4:
                    v = v.rearrange("p (x y z w) -> p x y z w", y=dims[1], z=dims[2], w=dims[3])
                return v

        NC = sum(n for _, n in CAT.values())
        keep = Region(0, free)
        const = keep.take(NC)
        C = lambda name: const[:, CAT[name][0]:CAT[name][0] + CAT[name][1]]
        ident, ones = C("ident"), C("ones")
        x = keep.take(T, D)
        xT = keep.take(KT, S)
        mixT = keep.take(KT, S)
        st6 = keep.take(T, 2, 6)
        mv = keep.take(T, 2)
        rs = keep.take(T, 1)
        mx, sm, rc = keep.take(2, 2), keep.take(2, 2), keep.take(2, 2)
        lo_ring = keep.at
        ring = keep.take(RING, SLOT)
        lo_free = keep.at
        gu = Region(lo_ring, free).take(GU_RING, 2, FF)
        dreg = Region(lo_ring + GU_RING * 2 * FF, free)
        dring = dreg.take(D_RING, D)
        c_lo = dreg.at

        def slot(u, n=None):
            v = ring[:, u % RING, :]
            return v if n is None else v.rearrange("p (k n) -> p k n", n=n)

        A = Region(lo_free, free)
        ln_g, ln_b = A.take(D), A.take(D)
        convrow = A.take(3, P)
        cw = A.take(48 + 88 + 88)
        dtb, alog, ng = A.take(H), A.take(H), A.take(P)
        mark = A.at
        qkv = A.take(12, S)
        qbT, kbT = A.take(4, S), A.take(4, S)
        vb, zg = A.take(T, 512), A.take(T, 512)
        small = A.take(200)
        so = [0]

        def tiny(*dims):
            n = int(np.prod(dims))
            v = small[:, so[0]:so[0] + n]
            so[0] += n
            assert so[0] <= 200
            return v if len(dims) == 1 else v.rearrange("p (x y) -> p x y", y=dims[1])
        ar, br, nab, eb, ea, el, g, beta = (tiny(T, H) for _ in range(8))
        eal = tiny(H)
        gcol, ngcol, egc, beg, gl, ekd, o_ss, o_rs = (tiny(T * H) for _ in range(8))
        gdn = A.at
        l2 = A.take(4, 512)
        gb = A.take(8, P)
        decS = A.take(8, P)
        decT = A.take(8, P)
        egb = A.take(8, P)
        bk, kdec, bv = A.take(8, P), A.take(8, P), A.take(8, P)
        Am, Dm, Em = A.take(8, P), A.take(8, P), A.take(8, P)
        Lm, Xm = l2.rearrange("p x y -> p (x y)")[:, 0:1024].rearrange("p (x y) -> p x y", y=P), l2.rearrange("p x y -> p (x y)")[:, 1024:2048].rearrange("p (x y) -> p x y", y=P)
        attT = decT
        uu, vnew, wT = gb, gb, decS
        state = A.take(H, P)
        G = Region(gdn, free)
        att_e = G.take(2, 2, S)
        att_pt = G.take(2, 4, S)
        rtmp = G.take(512)
        Fr = Region(mark, free)
        hidT = Fr.take(FT, S)
        facc = Fr.take(3, 2, S)
        a_end = A.at

        bg = Region(c_lo, free)
        hrows = bg.take(T, D)
        gbc = bg.take(D)
        xeT = bg.take(KT, NE * CAP)
        oneT = bg.take(T, NE * CAP)
        c_tiny = bg.take(320)
        c_end = bg.at
        B = Region(lo_free, c_lo)
        qaT, kaT, qdT, kdT = (B.take(4, S) for _ in range(4))
        va, vd = B.take(T, 512), B.take(T, 512)
        bE = B.take(2, 2, S)
        bPT = B.take(2, 4, S)
        bias12 = Region(c_lo + T * D + D, free).take(BIAS_HEADS, 3 * P)
        oa = B.take(T, 512)
        pro = Region(lo_free, free)
        tb_sb = pro.take(BIAS_HEADS, 2 * S)
        btab = pro.take(2 * S)
        brel = pro.take(BIAS_HEADS)
        brep = pro.take(BIAS_HEADS, P)
        E2 = mixT.rearrange("p x y -> p (x y)")
        sg = E2[:, 0:HALF]
        xe = xT.rearrange("p x y -> p (x y)")[:, 0:KT * CAP].rearrange("p (k s) -> p k s", s=CAP)
        pg = xT.rearrange("p x y -> p (x y)")[:, 256:512]
        hT = xT.rearrange("p x y -> p (x y)")[:, 512:512 + (HT + 1) * 64].rearrange("p (k s) -> p k s", s=64)
        yq = xT.rearrange("p x y -> p (x y)")[:, 1280:1536]
        hh = hrows.rearrange("p x y -> p (x y)")[:, 0:6 * P].rearrange("p (m n) -> p m n", n=P)
        to = [0]

        def ct(*dims):
            n = int(np.prod(dims))
            v = c_tiny[:, to[0]:to[0] + n]
            to[0] += n
            assert to[0] <= 320
            return v if len(dims) == 1 else v.rearrange("p (x y) -> p x y", y=dims[1])
        wr = ct(KT, NE)
        topidx = ct(CAP)[0:NE, :].bitcast(U32)
        ssq, rsb = ct(T), ct(T)
        neglam = ct(1)
        subg = Region(B.at, c_lo).take(P)
        lamv = Region(B.at + P, c_lo).take(4, DH)
        lame = Region(B.at + P + 256, c_lo).take(8)
        rl, rmax, rsum = ct(T, NE), ct(T), ct(T)
        affT = oneT.rearrange("p x y -> p (x y)")[0:NE, 0:S]
        affW = oneT.rearrange("p x y -> p (x y)")[0:NE, S:2 * S]
        topv = xeT.rearrange("p x y -> p (x y)")[0:NE, 0:CAP]
        topf = xeT.rearrange("p x y -> p (x y)")[0:NE, 64:64 + CAP]
        spread = xeT.rearrange("p x y -> p (x y)")[0:NE, 512:1024]
        rep = xeT.rearrange("p x y -> p (x y)")[0:NE, 1024:1280]
        idx4, g4 = ct(NE), ct(NE)

        block = ctx.enter_context(nc.Block())
        stop_a = STOP == "a"

        @block.sync
        def _(sp):
            sp.dma_start(const, a["consts"]).then_inc(sem("const_in"), 16)
            sp.dma_start(x, a["x"][0].rearrange("(t p) n -> p t n", p=P)).then_inc(sem("x_in"), 16)
            sp.sem_inc(sem("rows_used"), ROW_UNITS)

            def used(l, u):
                if u in (0, 1, 2):
                    return "proj", at(l, "proj", 2 * (u + 1))
                if u == 3:
                    return "ab_mm", at(l, "ab_mm", 1)
                if u < U_OUT:
                    return "proj", at(l, "proj", 2 * u)
                if U_UP <= u < U_DOWN:
                    return "up", at(l, "up", 2 * (u - U_UP + 1))
                return "rows_used", (l + 1) * ROW_UNITS + (u - U_OUT + 1 if u < U_UP else u - U_DOWN + 3)

            def stream(l, u, halves, before=None):
                name, value = before or (used(l, u - RING) if u >= RING else used(l - 1, UNITS + u - RING))
                sp.wait_ge(sem(name), value)
                for to_, from_ in halves:
                    sp.dma_start(to_, from_).then_inc(sem(f"slot_in{u % RING}"), 16)

            def columns(w, l, c, n, u):
                v = w[bass.ds(l, 1), :, c:c + n].rearrange("o (k p) n -> p (o k) n", p=P)
                s = slot(u, 512)[:, :, 0:n]
                return [(s[:, 0:4], v[:, 0:4]), (s[:, 4:8], v[:, 4:8])]

            def rows(w, l, k0, n, u):
                v = w[bass.ds(l, 1), k0 * P:(k0 + n) * P, :].rearrange("o (k p) n -> p (o k) n", p=P)
                s = slot(u, 1024)
                h = n // 2
                return [(s[:, 0:h], v[:, 0:h]), (s[:, h:n], v[:, h:n])]

            def bcast(w, l, n):
                return w[bass.ds(l, 1), :].broadcast_to([P, n])

            with sp.Fori(0, DEPTH) as l:
                for u, name in enumerate(UNITS_IN):
                    stream(l, u, columns(a["w_in"], l, OFF[name], 8 if name == "ab" else 512, u))
                    if u == RING - 1:
                        sp.wait_ge(sem("x_rows"), at(l, "x_rows", 2))
                        c = a["gdn_conv_w"][bass.ds(l, 1)].rearrange("o j (t p) -> (o j t) p", p=P)
                        sp.dma_start(convrow[0:48, 0, :], c).then_inc(sem("conv_rows"), 16)
                        f = a["ffn_conv_w"][bass.ds(l, 1)].rearrange("o j (t p) -> (o j t) p", p=P)
                        sp.dma_start(convrow[0:88, 1, :], f[0:88, :]).then_inc(sem("conv_rows"), 16)
                        sp.dma_start(convrow[0:44, 2, :], f[88:132, :]).then_inc(sem("conv_rows"), 8 * 2)
                        sp.dma_start(convrow[44:88, 2, :], a["ffn_conv_b"][bass.ds(l, 1)].rearrange("o (t p) -> (o t) p", p=P)).then_inc(sem("conv_rows"), 16)
                        sp.dma_start(dtb, bcast(a["gdn_dt_bias"], l, H)).then_inc(sem("small"), 16)
                        sp.dma_start(alog, bcast(a["gdn_a_log"], l, H)).then_inc(sem("small"), 16)
                        sp.dma_start(ng, bcast(a["gdn_norm_g"], l, P)).then_inc(sem("small"), 16)
                        sp.dma_start(ln_g, bcast(a["ln1_g"], l, D)).then_inc(sem("ln1"), 16)
                        sp.dma_start(ln_b, bcast(a["ln1_b"], l, D)).then_inc(sem("ln1"), 16)
                for i in range(2):
                    stream(l, U_OUT + i, rows(a["w_out"], l, 4 * i, 4, U_OUT + i))
                for i in range(11):
                    u = U_UP + i
                    s = slot(u, 512)
                    g_ = a["w_up"][bass.ds(l, 1), :, 256 * i:256 * i + 256].rearrange("o (k p) n -> p (o k) n", p=P)
                    v_ = a["w_up"][bass.ds(l, 1), :, FF + 256 * i:FF + 256 * i + 256].rearrange("o (k p) n -> p (o k) n", p=P)
                    stream(l, u, [(s[:, :, 0:256], g_), (s[:, :, 256:512], v_)])
                    if i == RING - 1:
                        sp.wait_ge(sem("x_rows"), at(l, "x_rows", 4))
                        sp.dma_start(ln_g, bcast(a["ln2_g"], l, D)).then_inc(sem("ln2"), 16)
                        sp.dma_start(ln_b, bcast(a["ln2_b"], l, D)).then_inc(sem("ln2"), 16)
                k0 = 0
                for i, n in enumerate(DOWN_TILES):
                    stream(l, U_DOWN + i, rows(a["w_down"], l, k0, n, U_DOWN + i))
                    k0 += n
            if stop_a:
                sp.wait_ge(sem("x_rows"), 2 + 2 * PER["x_rows"])
                sp.dma_start(out[0].rearrange("(t p) n -> p t n", p=P), x).then_inc(sem("stored"), 16)
                sp.wait_ge(sem("stored"), 16)
                return
            for u, c in enumerate(UNITS_IN_2):
                stream(DEPTH, u, columns(a["w_in_2"], 0, c, 512, u), ("b_proj", 2 * (u - RING + 1)) if u >= RING else None)
            for i in range(2):
                stream(DEPTH, 6 + i, rows(a["w_out_2"], 0, 4 * i, 4, 6 + i), ("b_proj", 2 * (3 + i)))
            sp.wait_ge(sem("rows_used"), (DEPTH + 1) * ROW_UNITS + 2)
            sp.wait_ge(sem("att_over"), 1)
            sp.sem_inc(sem("gu_free"), GU_RING)
            sp.sem_inc(sem("d_free"), D_RING)
            with sp.Fori(0, NE) as e:
                for k in range(KT):
                    sp.wait_ge(sem("gu_free"), e * KT + k + 1)
                    for n, w in enumerate(("w_gate_2", "w_up_2")):
                        sp.dma_start(gu[:, k % GU_RING, n, :], a[w][0, bass.ds(e, 1), k * P:(k + 1) * P, :].rearrange("o p n -> (o p) n")
                                     ).then_inc(sem(f"gu_in{k % GU_RING}"), 16)
                for k in range(FT):
                    sp.wait_ge(sem("d_free"), e * FT + k + 1)
                    sp.dma_start(dring[:, k % D_RING, :], a["w_down_2"][0, bass.ds(e, 1), k * P:(k + 1) * P, :].rearrange("o p n -> (o p) n")
                                 ).then_inc(sem(f"d_in{k % D_RING}"), 16)
            sp.wait_ge(sem("final_rows"), T)
            sp.dma_start(out[0].rearrange("(t p) n -> p t n", p=P), x).then_inc(sem("stored"), 16)
            sp.wait_ge(sem("stored"), 16)

        @block.gpsimd
        def _(pool):
            pool.dma_start(btab[0:BUCKETS + 1, :], a["bias_table"]).then_inc(sem("bias_in"), 16)
            pool.dma_start(brel[0:BUCKETS, :], a["rel_bias_2"]).then_inc(sem("bias_in"), 16)
            pool.dma_start(brel[BUCKETS:BUCKETS + 1, :], a["takes"]).then_inc(sem("bias_in"), 16)
            pool.wait_ge(sem("bias_sb"), BIAS_HEADS)
            pool.dma_start(scratch.rearrange("h (p n) -> p h n", p=P), tb_sb).then_inc(sem("bias_out"), 16)
            pool.wait_ge(sem("bias_out"), 16)
            pool.sem_inc(sem("layers_may"), 1)

            if stop_a:
                return
            pool.wait_ge(sem("x_rows"), at(DEPTH, "x_rows", 2))
            pool.dma_start(gbc, a["norm1_g_2"].broadcast_to([P, D])).then_inc(sem("g1"), 16)
            for h in range(BIAS_HEADS):
                v = scratch[h:h + 1, P - 1:P - 1 + P * (2 * S - 1)].rearrange("o (p n) -> (o p) n", p=P)[:, 0:3 * P]
                pool.dma_start(bias12[:, h, :], v).then_inc(sem("bias_back"), 16)
            pool.dma_start(subg, a["subln_g_2"].broadcast_to([P, P])).then_inc(sem("b_small"), 16)
            for n, name in enumerate(("lam_q1_2", "lam_k1_2", "lam_q2_2", "lam_k2_2")):
                pool.dma_start(lamv[:, n, :], a[name].broadcast_to([P, DH])).then_inc(sem("b_small"), 16)
            pool.dma_start(wr, a["w_router_2"][0].rearrange("(k p) e -> p k e", p=P)).then_inc(sem("b_small"), 16)
            pool.wait_ge(sem("h1_rows"), T)
            pool.dma_start(gbc, a["norm2_g_2"].broadcast_to([P, D])).then_inc(sem("g2"), 16)
            pool.wait_ge(sem("h2_rows"), T)
            pool.dma_start(gbc, a["norm_f_g_2"].broadcast_to([P, D])).then_inc(sem("g3"), 16)

        LAYER_PAIRS = [("causal", n) for n in range(4)]
        SECOND_PAIRS = [("diff", n) for n in range(4)] + [("dil", n) for n in range(4)]
        SC, TR, PV = ((2, 3), (4, 5)), (6, 7), (0, 1)

        def attention_operands(kind):
            if kind == "causal":
                return qbT, kbT, vb, att_e, att_pt
            return (qaT, kaT, va, bE, bPT) if kind == "diff" else (qdT, kdT, vd, bE, bPT)

        @block.tensor
        def _(pe):
            mm, tr = nc.tensor.matmul, nc.tensor.transpose

            def unit_in(l, u):
                pe.wait_ge(sem(f"slot_in{u % RING}"), l * (UNITS // RING * 32) + 32 * (u // RING + 1))

            def transpose_x(l, n, src, rows_name="x_rows"):
                for t in range(T):
                    pe.wait_ge(sem(rows_name), at(l, "x_rows", 2 * n + t + 1) if rows_name == "x_rows" else t + 1)
                    for kh in range(2):
                        for k in range(4):
                            last = tr(ps[4 + 2 * t + kh][:, k * P:(k + 1) * P], src[:, t, (4 * kh + k) * P:(4 * kh + k + 1) * P], ident)
                        last.then_inc(sem("x_tr"), 1)

            def channels(l, u, j0, bank):
                w = slot(u, 512)
                for j in range(2):
                    for k in range(KT):
                        last = mm(ps[bank][:, j * S:(j + 1) * S], w[:, k, (j0 + j) * P:(j0 + j + 1) * P], xT[:, k, :], start=(k == 0), stop=(k == KT - 1))
                return last

            def tokens(u, t, bank):
                w = slot(u, 512)
                for k in range(KT):
                    last = mm(ps[bank][:, :], xT[:, k, t * P:(t + 1) * P], w[:, k, :], start=(k == 0), stop=(k == KT - 1))
                return last

            def rows_product(l, lhsT, u0, tiles, banks=(0, 1, 2, 3)):
                k, K = 0, sum(tiles)
                for i, n in enumerate(tiles):
                    unit_in(l, u0 + i)
                    w = slot(u0 + i, 1024)
                    for kk in range(n):
                        for t in range(T):
                            for nh in range(2):
                                last = mm(ps[banks[2 * t + nh]][:, :], lhsT[:, k, t * P:(t + 1) * P], w[:, kk, nh * 512:(nh + 1) * 512],
                                          start=(k == 0), stop=(k == K - 1))
                        k += 1
                    last.then_inc(sem("rows_used"), 1)

            def attention(l, pairs):
                n = 2 * len(pairs)
                for i in range(n + 2):
                    if i < n:
                        kind, pr = pairs[i // 2]
                        q, k, _, E, PT = attention_operands(kind)
                        if i >= 2:
                            pe.wait_ge(sem("at_read"), at(l, "at_read", i - 1))
                        for m in range(2):
                            last = mm(ps[SC[i % 2][m]][:, 0:S], q[64 * m:64 * m + 64, pr, (i % 2) * P:(i % 2 + 1) * P],
                                      k[64 * m:64 * m + 64, pr, :], start=True, stop=True)
                        last.then_inc(sem("at_s"), 1)
                    if 1 <= i <= n:
                        b = i - 1
                        kind, pr = pairs[b // 2]
                        E = attention_operands(kind)[3]
                        pe.wait_ge(sem("at_prob"), at(l, "at_prob", b + 1))
                        if b >= 2:
                            pe.wait_ge(sem("at_pt"), at(l, "at_pt", b - 1))
                        for m in range(1 if kind == "diff" else 2):
                            for kt in range(T):
                                last = tr(ps[TR[b % 2]][:, (2 * m + kt) * P:(2 * m + kt + 1) * P], E[:, b % 2, m, kt * P:(kt + 1) * P], ident)
                        last.then_inc(sem("at_tr"), 1)
                    if i >= 3 and i % 2 == 1:
                        b = i - 2
                        pi = b // 2
                        kind, pr = pairs[pi]
                        _, _, v, _, PT = attention_operands(kind)
                        pe.wait_ge(sem("at_pt"), at(l, "at_pt", b + 1))
                        if pi >= 2:
                            pe.wait_ge(sem("at_out"), at(l, "at_out", pi - 1))
                        bank = ps[PV[pi % 2]]
                        if kind == "diff":
                            for t in range(T):
                                for kt in range(T):
                                    last = mm(bank[:, t * P:(t + 1) * P], PT[:, pi % 2, kt, t * P:(t + 1) * P],
                                              v[:, kt, pr * P:(pr + 1) * P], start=(kt == 0), stop=(kt == T - 1))
                        else:
                            for m in range(2):
                                for kt in range(T):
                                    last = mm(bank[64 * m:64 * m + 64, 0:S], v[:, kt, (2 * pr + m) * DH:(2 * pr + m + 1) * DH],
                                              PT[:, pi % 2, 2 * m + kt, :], start=(kt == 0), stop=(kt == T - 1))
                        last.then_inc(sem("at_pv"), 1)

            pe.wait_ge(sem("bias_rep"), 1)
            for h in range(BIAS_HEADS):
                if h >= 4:
                    pe.wait_ge(sem("bias_sb"), h - 3)
                mm(ps[h % 4][:, :], brep[0:BUCKETS + 1, h, :], btab[0:BUCKETS + 1, :], start=True, stop=True).then_inc(sem("bias_mm"), 1)
            pe.wait_ge(sem("bias_sb"), BIAS_HEADS)
            pe.wait_ge(sem("const_in"), 16)

            with pe.Fori(0, DEPTH) as l:
                transpose_x(l, 0, x)
                pe.wait_ge(sem("xT_ready"), at(l, "xT_ready", 4))
                for i in range(6):
                    if i % 2 == 0:
                        unit_in(l, i // 2)
                    if i >= 4:
                        pe.wait_ge(sem("taps"), at(l, "taps", i - 3))
                    last = channels(l, i // 2, 2 * (i % 2), 4 + i % 4).then_inc(sem("proj"), 1)
                    if i == 1:
                        pe.wait_ge(sem("conv_rows"), at(l, "conv_rows", 64))
                        tr(ps[0][:, 48:136], convrow[0:88, 1, :], ident[0:88, 0:88])
                        tr(ps[0][:, 136:224], convrow[0:88, 2, :], ident[0:88, 0:88])
                        tr(ps[0][:, 0:48], convrow[0:48, 0, :], ident[0:48, 0:48]).then_inc(sem("cw_tr"), 1)
                unit_in(l, 3)
                pe.wait_ge(sem("cw_ready"), at(l, "cw_ready", 1))
                for t in range(T):
                    for k in range(KT):
                        last = mm(ps[0][:, 8 * t:8 * t + 8], xT[:, k, t * P:(t + 1) * P], slot(3, 512)[:, k, 0:8], start=(k == 0), stop=(k == KT - 1))
                last.then_inc(sem("ab_mm"), 1)
                for i in range(6, 10):
                    if i % 2 == 0:
                        unit_in(l, 4 + (i - 6) // 2)
                    pe.wait_ge(sem("taps"), at(l, "taps", i - 3))
                    last = channels(l, 4 + (i - 6) // 2, 2 * (i % 2), 4 + i % 4).then_inc(sem("proj"), 1)
                for i in range(4):
                    pe.wait_ge(sem("sq"), at(l, "sq", i + 1))
                    if i == 3:
                        pe.wait_ge(sem("ab_pre"), at(l, "ab_pre", 1))
                    mm(ps[(i + 1) % 4][:, :], ones, l2[:, i, :], start=True, stop=True).then_inc(sem("l2_mm"), 1)
                for i in range(10, 14):
                    if i % 2 == 0:
                        unit_in(l, 6 + (i - 10) // 2)
                    pe.wait_ge(sem("act_evac"), at(l, "act_evac", i - 9))
                    last = tokens(6 + (i - 10) // 2, i % 2, 4 + i % 4).then_inc(sem("proj"), 1)
                pe.wait_ge(sem("g_ready"), at(l, "g_ready", 1))
                pe.wait_ge(sem("l2_sum"), at(l, "l2_sum", 4))
                mm(ps[1][:, 0:8], C("cum"), g.rearrange("p x y -> p (x y)"), start=True, stop=True)
                for n in range(8):
                    last = mm(ps[2 + n // 4][:, (n % 4) * P:(n % 4 + 1) * P], gb[:, n, :], C("cum"), start=True, stop=True)
                last.then_inc(sem("cum_mm"), 1)
                pe.wait_ge(sem("act_evac"), at(l, "act_evac", 8))
                pe.wait_ge(sem("qk_norm"), at(l, "qk_norm", 4))
                for n in range(4):
                    t, base = n % 2, 4 + 4 * (n // 2)
                    for h in range(H):
                        last = tr(ps[4 + n][:, h * P:(h + 1) * P], qkv[:, base + h, t * P:(t + 1) * P], ident)
                    last.then_inc(sem("rows_tr"), 1)
                pe.wait_ge(sem("cum_read"), at(l, "cum_read", 1))
                for n in range(8):
                    t, h = n // 4, n % 4
                    kk = qkv[:, 4 + h, t * P:(t + 1) * P]
                    mm(ps[t][:, h * P:(h + 1) * P], kk, kk, start=True, stop=True)
                    last = mm(ps[2 + t][:, h * P:(h + 1) * P], kk, qkv[:, h, t * P:(t + 1) * P], start=True, stop=True)
                last.then_inc(sem("kk_mm"), 1)
                pe.wait_ge(sem("rows_a"), at(l, "rows_a", 1))
                pe.wait_ge(sem("rows_v"), at(l, "rows_v", 1))
                for lv in range(6):
                    for t in range(T):
                        n = 2 * lv + t
                        pe.wait_ge(sem("lvl"), at(l, "lvl", n + 1))
                        pe.wait_ge(sem("e_ready"), at(l, "e_ready", n - 1)) if lv else None
                        for h in range(H):
                            last = mm(ps[4 + t][:, h * P:(h + 1) * P], Lm[:, 4 * t + h, :], Em[:, 4 * t + h, :] if lv else ident, start=True, stop=True)
                        last.then_inc(sem("x_mm"), 1)
                    for t in range(T):
                        n = 2 * lv + t
                        pe.wait_ge(sem("x_evac"), at(l, "x_evac", n + 1))
                        for h in range(H):
                            last = mm(ps[6 + t][:, h * P:(h + 1) * P], Dm[:, 4 * t + h, :] if lv else ident, Xm[:, 4 * t + h, :], start=True, stop=True)
                        for h in range(H):
                            if lv < 5:
                                last = mm(ps[t][:, h * P:(h + 1) * P], Xm[:, 4 * t + h, :], Dm[:, 4 * t + h, :] if lv else ident, start=True, stop=True)
                        last.then_inc(sem("ed_mm"), 1)
                for t in range(T):
                    pe.wait_ge(sem("e_ready"), at(l, "e_ready", 11 + t))
                    for h in range(H):
                        n = 4 * t + h
                        mm(ps[2 + t][:, h * P:(h + 1) * P], Em[:, n, :], bv[:, n, :], start=True, stop=True)
                        last = mm(ps[4 + t][:, h * P:(h + 1) * P], bk[:, n, :], Em[:, n, :], start=True, stop=True)
                    last.then_inc(sem("sol_mm"), 1)
                pe.wait_ge(sem("qdec"), at(l, "qdec", 1))
                for c in range(S // CHUNK):
                    t, lo = c // 2, CHUNK * (c % 2)
                    rows_ = slice(lo, lo + CHUNK)
                    if c:
                        pe.wait_ge(sem("state"), at(l, "state", c))
                        pe.wait_ge(sem("w_ready2"), at(l, "w_ready2", 1))
                        for h in range(H):
                            last = mm(ps[6][rows_, h * P:(h + 1) * P], wT[:, 4 * t + h, rows_], state[:, h, :], start=True, stop=True)
                        last.then_inc(sem("pv_mm"), 1)
                    pe.wait_ge(sem("vnew"), at(l, "vnew", c + 1))
                    if c < 3:
                        for h in range(H):
                            last = mm(ps[1][:, h * P:(h + 1) * P], kdec[rows_, 4 * t + h, :], vnew[rows_, 4 * t + h, :], start=True, stop=True)
                        last.then_inc(sem("st_mm"), 1)
                    for h in range(H):
                        o_ = ps[7 * (1 - t)][rows_, h * P:(h + 1) * P]
                        if c:
                            mm(o_, qkv[:, h, c * CHUNK:(c + 1) * CHUNK], state[:, h, :], start=True, stop=False)
                        last = mm(o_, attT[rows_, 4 * t + h, rows_], vnew[rows_, 4 * t + h, :], start=(c == 0), stop=True)
                    last.then_inc(sem("o_step"), 1)
                for t in range(T):
                    pe.wait_ge(sem("o_rows"), at(l, "o_rows", t + 1))
                    for h in range(H):
                        last = tr(ps[2 + t][:, h * P:(h + 1) * P], uu[:, 4 * t + h, :], ident)
                    last.then_inc(sem("o_tr"), 1)
                pe.wait_ge(sem("mix_o"), at(l, "mix_o", 2))
                for i in range(4):
                    src = (qbT, qbT, kbT, kbT)[i][:, 2 * (i % 2):2 * (i % 2) + 2, :].rearrange("p x y -> p (x y)")
                    mm(ps[i][:, :], C("rot"), src, start=True, stop=True).then_inc(sem("rot_mm"), 1)
                pe.wait_ge(sem("rotated"), at(l, "rotated", 4))
                attention(l, LAYER_PAIRS)
                pe.wait_ge(sem("at_out"), at(l, "at_out", 4))
                rows_product(l, mixT, U_OUT, [4, 4])
                transpose_x(l, 1, x)
                pe.wait_ge(sem("xT_ready"), at(l, "xT_ready", 8))
                for j in range(FT):
                    u = U_UP + j // 2
                    if j % 2 == 0:
                        unit_in(l, u)
                    if j >= 4:
                        pe.wait_ge(sem("up_dve"), at(l, "up_dve", j - 3))
                    w = slot(u, 512)
                    for gv in range(2):
                        for k in range(KT):
                            c0 = gv * 256 + (j % 2) * P
                            last = mm(ps[4 + j % 4][:, gv * S:(gv + 1) * S], w[:, k, c0:c0 + P], xT[:, k, :], start=(k == 0), stop=(k == KT - 1))
                    last.then_inc(sem("up"), 1)
                pe.wait_ge(sem("hid"), at(l, "hid", FT))
                rows_product(l, hidT, U_DOWN, DOWN_TILES)
            if stop_a:
                return
            L = DEPTH
            transpose_x(L, 0, hrows, "h1_rows")
            pe.wait_ge(sem("xT_ready"), at(L, "xT_ready", 4))
            n = 0
            for u in range(6):
                unit_in(L, u)
                for i in range(2):
                    if n >= 4:
                        pe.wait_ge(sem("b_evac"), n - 3)
                    last = tokens(u, i, 4 + n % 4) if u in (2, 5) else channels(L, u, 2 * i, 4 + n % 4)
                    last.then_inc(sem("b_proj"), 1)
                    n += 1
            pe.wait_ge(sem("b_evac"), 12)
            attention(L, SECOND_PAIRS)
            pe.wait_ge(sem("oa_rows"), 4)
            for t in range(T):
                for h in range(H):
                    last = tr(ps[2 + t][:, h * P:(h + 1) * P], oa[:, t, h * P:(h + 1) * P], ident)
            last.then_inc(sem("oa_tr"), 1)
            pe.wait_ge(sem("oa_mix"), 2)
            pe.wait_ge(sem("at_out"), at(L, "at_out", 8))
            rows_product(L, mixT, 6, [4, 4], banks=(4, 5, 6, 7))
            for t in range(T):
                pe.wait_ge(sem("h2_rows"), t + 1)
                for kh in range(2):
                    for k in range(4):
                        last = tr(ps[2 * t + kh][:, k * P:(k + 1) * P], hrows[:, t, (4 * kh + k) * P:(4 * kh + k + 1) * P], ident)
                    last.then_inc(sem("h2_tr"), 1)
            pe.wait_ge(sem("h2T"), 4)
            for t in range(T):
                for k in range(KT):
                    last = mm(ps[4][:, NE * t:NE * (t + 1)], xT[:, k, t * P:(t + 1) * P], wr[:, k, :], start=(k == 0), stop=(k == KT - 1))
            last.then_inc(sem("logits"), 1)
            pe.wait_ge(sem("aff"), 1)
            for t in range(T):
                last = tr(ps[5][0:NE, t * P:(t + 1) * P], rl[:, t, :], ident)
            last.then_inc(sem("aff_tr"), 1)
            pe.wait_ge(sem("chosen"), 1)
            mm(ps[6][:, :], ones[0:NE, :], spread, start=True, stop=True)
            mm(ps[7][:, 0:NE], rep[:, 0:P], ident[0:NE, 0:NE], start=True, stop=True)
            mm(ps[7][:, NE:2 * NE], rep[:, P:2 * P], ident[0:NE, 0:NE], start=True, stop=True).then_inc(sem("spread_mm"), 1)
            pe.wait_ge(sem("onehot"), 1)
            for k in range(KT):
                if k >= 4:
                    pe.wait_ge(sem("xe_evac"), k - 3)
                for t in range(T):
                    last = mm(ps[k % 4][:, :], hrows[:, t, k * P:(k + 1) * P], oneT[:, t, :], start=(t == 0), stop=(t == T - 1))
                last.then_inc(sem("xe_mm"), 1)
            with pe.Fori(0, NE) as e:
                pe.wait_ge(sem("xe_ready"), e + 1)
                for k in range(KT):
                    s_ = k % GU_RING
                    pe.wait_ge(sem(f"gu_in{s_}"), e * (KT // GU_RING * 32) + 32 * (k // GU_RING + 1))
                    for b, (c0, n) in enumerate(PIECES):
                        for q in range(4):
                            c = (q % 2) * HALF + c0
                            last = mm(ps[b][32 * q:32 * q + 32, 0:n], xe[:, k, :], gu[:, s_, q // 2, c:c + n], start=(k == 0), stop=(k == KT - 1))
                    last.then_inc(sem("gu_free"), 1)
                for b, (c0, n) in enumerate(PIECES):
                    pe.wait_ge(sem("eh"), e * 3 + b + 1)
                    for m in (2 * b, 2 * b + 1):
                        last = tr(ps[HID_BANKS[b]][:, (m % 2) * P:(m % 2 + 1) * P], hh[:, m, :], ident)
                    last.then_inc(sem("eh_tr"), 1)
                for k in range(FT):
                    pe.wait_ge(sem("ehT"), e * 3 + (k // 4 + 1 if k < HT else 3))
                    pe.wait_ge(sem(f"d_in{k % D_RING}"), e * (FT // D_RING * 16) + 16 * (k // D_RING + 1))
                    for q in range(4):
                        last = mm(ps[5][32 * q:32 * q + 32, 0:256], hT[:, k % HT, 32 * (k // HT):32 * (k // HT) + 32], dring[:, k % D_RING, 256 * q:256 * q + 256],
                                  start=(k == 0), stop=(k == FT - 1))
                    last.then_inc(sem("d_free"), 1)
                pe.wait_ge(sem("ey"), e + 1)
                for t in range(T):
                    for q in range(4):
                        last = mm(ps[OUT_BANKS[q]][:, t * 256:(t + 1) * 256], pg[32 * q:32 * q + 32, t * P:(t + 1) * P],
                                  yq[32 * q:32 * q + 32, :], start=True, stop=True)
                last.then_inc(sem("eo_mm"), 1)

        @block.scalar
        def _(act):
            f = nc.scalar.activation

            def copy_xT(l, n):
                for t in range(T):
                    for kh in range(2):
                        act.wait_ge(sem("x_tr"), l * 8 + 4 * n + 2 * t + kh + 1)
                        f(xT[:, 4 * kh:4 * kh + 4, t * P:(t + 1) * P], ps[4 + 2 * t + kh][:, :].rearrange("p (x y) -> p x y", y=P), ACT.Copy).then_inc(sem("xT_ready"), 1)

            def attention(l, pairs):
                n = 2 * len(pairs)
                for i in range(n + 2):
                    if i < n:
                        E = attention_operands(pairs[i // 2][0])[3]
                        act.wait_ge(sem("at_read"), at(l, "at_read", i + 1))
                        for m in range(2):
                            last = f(E[:, i % 2, m, :], E[:, i % 2, m, :], ACT.Exp, bias=mx[:, i % 2, m:m + 1], accum_out=sm[:, i % 2, m:m + 1])
                        last.then_inc(sem("at_exp"), 1)
                    if 1 <= i <= n:
                        b = i - 1
                        kind, pr = pairs[b // 2]
                        PT = attention_operands(kind)[4]
                        act.wait_ge(sem("at_tr"), at(l, "at_tr", b + 1))
                        if b // 2 >= 2:
                            act.wait_ge(sem("at_pv"), at(l, "at_pv", b // 2 - 1))
                        w = 2 if kind == "diff" else 4
                        f(PT[:, b // 2 % 2, 0:w, (b % 2) * P:(b % 2 + 1) * P],
                          ps[TR[b % 2]][:, 0:w * P].rearrange("p (x y) -> p x y", y=P), ACT.Copy).then_inc(sem("at_pt"), 1)
                    if i >= 3 and i % 2 == 1:
                        pi = (i - 2) // 2
                        kind, pr = pairs[pi]
                        if kind != "diff":
                            act.wait_ge(sem("at_pv"), at(l, "at_pv", pi + 1))
                            f(mixT[:, 4 + pr, :], ps[PV[pi % 2]][:, 0:S], ACT.Copy).then_inc(sem("at_out"), 1)

            act.wait_ge(sem("const_in"), 16)
            with act.Fori(0, DEPTH) as l:
                copy_xT(l, 0)
                act.wait_ge(sem("cw_ready"), at(l, "cw_ready", 1))
                for i in range(7):
                    if i < 6:
                        act.wait_ge(sem("proj"), at(l, "proj", i + 1))
                        for j in range(2):
                            c = 2 * i + j
                            last = f(qkv[:, c, :], ps[4 + i % 4][:, j * S:(j + 1) * S], ACT.Copy, scale=cw[:, 36 + c:37 + c])
                        last.then_inc(sem("tap"), 1)
                    if i:
                        act.wait_ge(sem("taps"), at(l, "taps", i))
                        v = qkv[:, 2 * i - 2:2 * i, :]
                        f(v, v, ACT.Silu).then_inc(sem("silu"), 1)
                for i in range(4):
                    act.wait_ge(sem("silu"), at(l, "silu", i + 1))
                    f(l2[:, i, :], qkv[:, 2 * i:2 * i + 2, :].rearrange("p x y -> p (x y)"), ACT.Square).then_inc(sem("sq"), 1)
                for i in range(4):
                    act.wait_ge(sem("proj"), at(l, "proj", 7 + i))
                    dst = (qbT, kbT)[i // 2][:, 2 * (i % 2):2 * (i % 2) + 2, :].rearrange("p x y -> p (x y)")
                    f(dst, ps[4 + (6 + i) % 4][:, :], ACT.Copy).then_inc(sem("act_evac"), 1)
                for i in range(4):
                    act.wait_ge(sem("l2_sum"), at(l, "l2_sum", i + 1))
                    f(l2[:, i, :], l2[:, i, :], ACT.Sqrt).then_inc(sem("l2_rs"), 1)
                for i in range(4):
                    act.wait_ge(sem("proj"), at(l, "proj", 11 + i))
                    f((zg, vb)[i // 2][:, i % 2, :], ps[4 + (10 + i) % 4][:, :], ACT.Silu if i < 2 else ACT.Copy).then_inc(sem("act_evac"), 1)
                act.wait_ge(sem("ab_pre"), at(l, "ab_pre", 1))
                act.wait_ge(sem("small"), l * 48 + 48)
                f(eb, br, ACT.Exp, scale=-1.0)
                f(ea, nab, ACT.Exp)
                f(eal, alog, ACT.Exp)
                act.drain()
                f(el, ea, ACT.Ln, bias=1.0).then_inc(sem("ab_act"), 1)
                act.wait_ge(sem("arg_ready"), at(l, "arg_ready", 1))
                for n in range(8):
                    f(decS[:, n, :], decS[:, n, :], ACT.Exp, bias=gcol[:, n:n + 1])
                    f(decT[:, n, :], decT[:, n, :], ACT.Exp, bias=ngcol[:, n:n + 1])
                for t in range(T):
                    v = egb[:, 4 * t:4 * t + 4, :].rearrange("p x y -> p (x y)")
                    f(v, v, ACT.Exp)
                f(egc, gcol, ACT.Exp)
                f(ekd, gl, ACT.Exp).then_inc(sem("dec"), 1)
                act.wait_ge(sem("g_ready"), at(l, "g_ready", 1))
                for t in range(T):
                    act.wait_ge(sem("rows_tr"), at(l, "rows_tr", t + 3))
                    for h in range(H):
                        last = f(bv[:, 4 * t + h, :], ps[6 + t][:, h * P:(h + 1) * P], ACT.Copy, scale=beta[:, t, h:h + 1])
                last.then_inc(sem("rows_a"), 1)
                for lv in range(6):
                    for t in range(T):
                        n = 2 * lv + t
                        act.wait_ge(sem("x_mm"), at(l, "x_mm", n + 1))
                        f(Xm[:, 4 * t:4 * t + 4, :].rearrange("p x y -> p (x y)"), ps[4 + t][:, :], ACT.Copy).then_inc(sem("x_evac"), 1)
                for t in range(T):
                    act.wait_ge(sem("sol_mm"), at(l, "sol_mm", t + 1))
                    last = f(wT[:, 4 * t:4 * t + 4, :].rearrange("p x y -> p (x y)"), ps[4 + t][:, :], ACT.Copy)
                last.then_inc(sem("w_ready2"), 1)
                for t in range(T):
                    act.wait_ge(sem("o_step"), at(l, "o_step", 2 * t + 2))
                    for h in range(H):
                        n = 4 * t + h
                        last = f(Xm[:, n, :], ps[7 * (1 - t)][:, h * P:(h + 1) * P], ACT.Square, accum_out=o_ss[:, n:n + 1])
                    last.then_inc(sem("o_sq"), 1)
                    act.wait_ge(sem("o_sum"), at(l, "o_sum", t + 1))
                    f(o_rs[:, 4 * t:4 * t + 4], o_rs[:, 4 * t:4 * t + 4], ACT.Sqrt).then_inc(sem("o_rs"), 1)
                for t in range(T):
                    act.wait_ge(sem("o_tr"), at(l, "o_tr", t + 1))
                    f(mixT[:, 0:4, t * P:(t + 1) * P], ps[2 + t][:, :].rearrange("p (x y) -> p x y", y=P), ACT.Copy).then_inc(sem("mix_o"), 1)
                attention(l, LAYER_PAIRS)

                def layer_norm_root(n):
                    for t in range(T):
                        act.wait_ge(sem("y_stat"), at(l, "y_stat", 2 * n + t + 1))
                        f(rs[:, t, :], rs[:, t, :], ACT.Sqrt).then_inc(sem("y_rs"), 1)
                layer_norm_root(0)
                copy_xT(l, 1)
                for j in range(FT + 1):
                    if j < FT:
                        act.wait_ge(sem("up"), at(l, "up", j + 1))
                        if j >= 3:
                            act.wait_ge(sem("hid"), at(l, "hid", j - 2))
                        for gv in range(2):
                            c = gv * FT + j
                            last = f(facc[:, j % 3, gv, :], ps[4 + j % 4][:, gv * S:(gv + 1) * S], ACT.Identity,
                                     scale=cw[:, 136 + c:137 + c], bias=cw[:, 180 + c:181 + c])
                        last.then_inc(sem("up_act"), 1)
                    if j:
                        act.wait_ge(sem("up_dve"), at(l, "up_dve", j))
                        f(facc[:, (j - 1) % 3, 0, :], facc[:, (j - 1) % 3, 0, :], ACT.Silu).then_inc(sem("up_silu"), 1)
                layer_norm_root(1)
            if stop_a:
                return
            L = DEPTH
            def rms(n):
                for t in range(T):
                    act.wait_ge(sem("r_in"), 2 * n + t + 1)
                    f(sqbig, x[:, t, :], ACT.Square, accum_out=ssq[:, t:t + 1]).then_inc(sem("r_sq"), 1)
                    act.wait_ge(sem("r_sum"), 2 * n + t + 1)
                    f(rsb[:, t:t + 1], rsb[:, t:t + 1], ACT.Sqrt).then_inc(sem("r_rs"), 1)
            sqbig = xT.rearrange("p x y -> p (x y)")[:, 0:D]
            rms(0)
            copy_xT(L, 0)
            n = 0
            for u in range(6):
                dst = (qaT, kaT, va, qdT, kdT, vd)[u]
                for i in range(2):
                    act.wait_ge(sem("b_proj"), n + 1)
                    d_ = dst[:, i, :] if u in (2, 5) else dst[:, 2 * i:2 * i + 2, :].rearrange("p x y -> p (x y)")
                    f(d_, ps[4 + n % 4][:, :], ACT.Copy).then_inc(sem("b_evac"), 1)
                    n += 1
            act.wait_ge(sem("lam_dot"), 1)
            f(lame[:, 2:4], lame[:, 0:2], ACT.Exp).then_inc(sem("lam_exp"), 1)
            attention(L, SECOND_PAIRS)
            act.wait_ge(sem("oa_sum"), 1)
            f(lame, lame, ACT.Sqrt).then_inc(sem("oa_rs"), 1)
            for t in range(T):
                act.wait_ge(sem("oa_tr"), 1)
                f(mixT[:, 0:4, t * P:(t + 1) * P], ps[2 + t][:, :].rearrange("p (x y) -> p x y", y=P), ACT.Copy).then_inc(sem("oa_mix"), 1)
            rms(1)
            for t in range(T):
                for kh in range(2):
                    act.wait_ge(sem("h2_tr"), 2 * t + kh + 1)
                    f(xT[:, 4 * kh:4 * kh + 4, t * P:(t + 1) * P], ps[2 * t + kh][:, :].rearrange("p (x y) -> p x y", y=P), ACT.Copy).then_inc(sem("h2T"), 1)
            act.wait_ge(sem("rl_ready"), 1)
            for t in range(T):
                last = f(rl[:, t, :], rl[:, t, :], ACT.Exp, bias=rmax[:, t:t + 1], accum_out=rsum[:, t:t + 1])
            last.then_inc(sem("rl_exp"), 1)
            for k in range(KT):
                act.wait_ge(sem("xe_mm"), k + 1)
                f(xeT[:, k, :], ps[k % 4][:, :], ACT.Copy).then_inc(sem("xe_evac"), 1)
            with act.Fori(0, NE) as e:
                for b, (c0, n) in enumerate(PIECES):
                    act.wait_ge(sem("gu_free"), GU_RING + e * KT + KT)
                    f(sg[0:64, c0:c0 + n], ps[b][0:64, 0:n], ACT.Silu).then_inc(sem("esg"), 1)
                for b, (c0, n) in enumerate(PIECES):
                    act.wait_ge(sem("eh_tr"), e * 3 + b + 1)
                    last = f(hT[:, 4 * b:4 * b + 4, :], ps[HID_BANKS[b]][:, 0:S].rearrange("p (x y) -> p x y", y=64), ACT.Copy)
                    last.then_inc(sem("ehT"), 1)
                act.wait_ge(sem("d_free"), e * FT + FT + D_RING)
                f(yq, ps[5][:, 0:256], ACT.Copy).then_inc(sem("ey"), 1)
            rms(2)

        @block.vector
        def _(v):
            w = nc.vector

            def attention(l, pairs):
                n = 2 * len(pairs)
                for i in range(n + 3):
                    if i < n:
                        kind, pr = pairs[i // 2]
                        E, t = attention_operands(kind)[3], i % 2
                        v.wait_ge(sem("at_s"), at(l, "at_s", i + 1))
                        if i >= 2:
                            v.wait_ge(sem("at_tr"), at(l, "at_tr", i - 1))
                        for m in range(2):
                            if kind == "causal":
                                bias = C("causal")
                            else:
                                bias = bias12[:, pr if kind == "diff" else H + 2 * pr + m, :]
                            w.scalar_tensor_tensor(E[:, i % 2, m, :], ps[SC[i % 2][m]][:, 0:S], DH ** -0.5, bias[:, P - P * t:P - P * t + S], ALU.mult, ALU.add)
                        v.drain()
                        w.tensor_reduce(mx[:, i % 2, :], E[:, i % 2, :, :], AX.X, ALU.max, negate=True).then_inc(sem("at_read"), 1)
                    if 1 <= i <= n:
                        b = i - 1
                        kind, pr = pairs[b // 2]
                        E = attention_operands(kind)[3]
                        v.wait_ge(sem("at_exp"), at(l, "at_exp", b + 1))
                        w.reciprocal(rc[:, b % 2, :], sm[:, b % 2, :])
                        v.drain()
                        if kind == "diff":
                            w.tensor_scalar(rc[:, b % 2, 1:2], rc[:, b % 2, 1:2], neglam, None, ALU.mult)
                            v.drain()
                            w.tensor_scalar(E[:, b % 2, 1, :], E[:, b % 2, 1, :], rc[:, b % 2, 1:2], None, ALU.mult)
                            v.drain()
                            w.scalar_tensor_tensor(E[:, b % 2, 0, :], E[:, b % 2, 0, :], rc[:, b % 2, 0:1], E[:, b % 2, 1, :], ALU.mult, ALU.add).then_inc(sem("at_prob"), 1)
                        else:
                            for m in range(2):
                                last = w.tensor_scalar(E[:, b % 2, m, :], E[:, b % 2, m, :], rc[:, b % 2, m:m + 1], None, ALU.mult)
                            last.then_inc(sem("at_prob"), 1)
                    if i >= 3 and i % 2 == 1:
                        pi = (i - 3) // 2
                        kind, pr = pairs[pi]
                        if kind == "diff":
                            v.wait_ge(sem("at_pv"), at(l, "at_pv", pi + 1))
                            w.tensor_copy(oa[:, :, pr * P:(pr + 1) * P], ps[PV[pi % 2]][:, 0:S].rearrange("p (t n) -> p t n", n=P)).then_inc(sem("at_out"), 1)

            v.wait_ge(sem("bias_in"), 48)
            w.tensor_copy(brep[0:BUCKETS + 1, :, :], brel[0:BUCKETS + 1, :].unsqueeze(2).broadcast_to([BUCKETS + 1, BIAS_HEADS, P])).then_inc(sem("bias_rep"), 1)
            for h in range(BIAS_HEADS):
                v.wait_ge(sem("bias_mm"), h + 1)
                w.tensor_copy(tb_sb[:, h, :], ps[h % 4][:, :]).then_inc(sem("bias_sb"), 1)
            v.wait_ge(sem("layers_may"), 1)
            v.wait_ge(sem("const_in"), 16)
            v.wait_ge(sem("x_in"), 16)
            v.nop().then_inc(sem("x_rows"), 2)

            def layer_norm(l, n):
                v.wait_ge(sem("rows_used"), (l + 1) * ROW_UNITS + (ROW_UNITS if n else 2))
                v.wait_ge(sem(("ln1", "ln2")[n]), l * 32 + 32)
                for t in range(T):
                    for nh in range(2):
                        xs = x[:, t, nh * 512:(nh + 1) * 512]
                        w.scalar_tensor_tensor(xs, xs, ALPHA, ps[2 * t + nh][:, :], ALU.mult, ALU.add)
                    v.drain()
                    for nh in range(2):
                        w.bn_stats(st6[:, t, nh, :], x[:, t, nh * 512:(nh + 1) * 512])
                    v.drain()
                    w.bn_aggr(mv[:, t, :], st6[:, t, :, :])
                    v.drain()
                    w.tensor_scalar(rs[:, t, :], mv[:, t, 1:2], LN_EPS, None, ALU.add).then_inc(sem("y_stat"), 1)
                for t in range(T):
                    v.wait_ge(sem("y_rs"), at(l, "y_rs", 2 * n + t + 1))
                    w.reciprocal(rs[:, t, :], rs[:, t, :])
                    v.drain()
                    w.tensor_scalar(x[:, t, :], x[:, t, :], mv[:, t, 0:1], rs[:, t, :], ALU.subtract, ALU.mult)
                    v.drain()
                    w.tensor_mul(x[:, t, :], x[:, t, :], ln_g)
                    v.drain()
                    w.tensor_add(x[:, t, :], x[:, t, :], ln_b).then_inc(sem("x_rows"), 1)

            with v.Fori(0, DEPTH) as l:
                v.wait_ge(sem("cw_tr"), at(l, "cw_tr", 1))
                w.tensor_copy(cw, ps[0][:, 0:224]).then_inc(sem("cw_ready"), 1)
                v.drain()
                for i in range(6):
                    v.wait_ge(sem("tap"), at(l, "tap", i + 1))
                    for s in range(1, TAPS):
                        for j in range(2):
                            c = 2 * i + j
                            last = w.scalar_tensor_tensor(qkv[:, c, s:S], ps[4 + i % 4][:, j * S:(j + 1) * S - s], cw[:, 12 * (3 - s) + c:12 * (3 - s) + c + 1],
                                                          qkv[:, c, s:S], ALU.mult, ALU.add)
                        if s < TAPS - 1:
                            v.drain()
                    last.then_inc(sem("taps"), 1)
                v.wait_ge(sem("ab_mm"), at(l, "ab_mm", 1))
                v.wait_ge(sem("small"), l * 48 + 48)
                ab = ps[0][:, 0:16].rearrange("p (t n) -> p t n", n=8)
                w.tensor_add(ar, ab[:, :, 0:H], dtb.unsqueeze(1).broadcast_to([P, T, H]))
                w.tensor_copy(br, ab[:, :, H:2 * H])
                v.drain()
                w.tensor_scalar(nab, ar, -1.0, None, ALU.mult)
                v.drain()
                w.tensor_tensor(nab, nab, ar, ALU.min).then_inc(sem("ab_pre"), 1)
                for i in range(4):
                    v.wait_ge(sem("l2_mm"), at(l, "l2_mm", i + 1))
                    w.tensor_scalar(l2[:, i, :], ps[(i + 1) % 4][:, :], NORM_EPS, None, ALU.add).then_inc(sem("l2_sum"), 1)
                for i in range(4):
                    v.wait_ge(sem("l2_rs"), at(l, "l2_rs", i + 1))
                    w.reciprocal(l2[:, i, :], l2[:, i, :])
                    v.drain()
                    q2 = qkv[:, 2 * i:2 * i + 2, :].rearrange("p x y -> p (x y)")
                    w.scalar_tensor_tensor(q2, q2, DK ** -0.5 if i < 2 else 1.0, l2[:, i, :], ALU.mult, ALU.mult).then_inc(sem("qk_norm"), 1)
                v.wait_ge(sem("ab_act"), at(l, "ab_act", 1))
                w.scalar_tensor_tensor(g, ar, 0.0, el, ALU.max, ALU.add)
                w.tensor_scalar(beta, eb, 1.0, None, ALU.add)
                v.drain()
                w.scalar_tensor_tensor(g, g, -1.0, eal.unsqueeze(1).broadcast_to([P, T, H]), ALU.mult, ALU.mult)
                w.reciprocal(beta, beta)
                v.drain()
                w.tensor_copy(gb, g.rearrange("p x y -> p (x y)").unsqueeze(2).broadcast_to([P, 8, P])).then_inc(sem("g_ready"), 1)
                v.wait_ge(sem("act_evac"), at(l, "act_evac", 6))
                for t in range(T):
                    zz = zg[:, t, :].rearrange("p (h n) -> p h n", n=P)
                    w.tensor_mul(zz, zz, ng.unsqueeze(1).broadcast_to([P, H, P]))
                v.wait_ge(sem("cum_mm"), at(l, "cum_mm", 1))
                w.tensor_copy(gcol, ps[1][:, 0:8])
                for t in range(T):
                    cum = ps[2 + t][:, :].rearrange("p (h n) -> p h n", n=P)
                    w.scalar_tensor_tensor(decS[:, 4 * t:4 * t + 4, :], cum, -1.0, C("neg_strict").unsqueeze(1).broadcast_to([P, H, P]), ALU.mult, ALU.add)
                    w.tensor_add(decT[:, 4 * t:4 * t + 4, :], cum, C("neg_incl_t").unsqueeze(1).broadcast_to([P, H, P]))
                    w.tensor_copy(egb[:, 4 * t:4 * t + 4, :], cum)
                v.drain()
                w.tensor_scalar(ngcol, gcol, -1.0, None, ALU.mult)
                for lo in (0, CHUNK):
                    w.tensor_sub(gl[lo:lo + CHUNK, :], egb[lo:lo + CHUNK, :, lo + CHUNK - 1], gcol[lo:lo + CHUNK, :])
                v.drain().then_inc(sem("arg_ready"), 1)
                v.nop().then_inc(sem("cum_read"), 1)
                v.wait_ge(sem("dec"), at(l, "dec", 1))
                w.tensor_mul(beg, beta.rearrange("p x y -> p (x y)"), egc)
                v.drain()
                for n in range(8):
                    t, h = n // 4, n % 4
                    if h == 0:
                        v.wait_ge(sem("rows_tr"), at(l, "rows_tr", t + 1))
                    w.tensor_scalar(kdec[:, n, :], ps[4 + t][:, h * P:(h + 1) * P], ekd[:, n:n + 1], None, ALU.mult)
                    last = w.tensor_scalar(bk[:, n, :], ps[4 + t][:, h * P:(h + 1) * P], beg[:, n:n + 1], None, ALU.mult)
                last.then_inc(sem("rows_v"), 1)
                v.wait_ge(sem("kk_mm"), at(l, "kk_mm", 1))
                for n in range(8):
                    t, h = n // 4, n % 4
                    w.scalar_tensor_tensor(Am[:, n, :], ps[t][:, h * P:(h + 1) * P], beta[:, t, h:h + 1], decS[:, n, :], ALU.mult, ALU.mult)
                for t in range(T):
                    dt_ = decT[:, 4 * t:4 * t + 4, :].rearrange("p x y -> p (x y)")
                    w.tensor_mul(dt_, ps[2 + t][:, :], dt_)
                v.drain()

                def level(lv, t):
                    w.tensor_mul(Lm[:, 4 * t:4 * t + 4, :], Am[:, 4 * t:4 * t + 4, :], C(f"level{lv}").unsqueeze(1).broadcast_to([P, H, P])).then_inc(sem("lvl"), 1)
                for t in range(T):
                    level(0, t)
                for t in range(T):
                    qq = qkv[:, 0:4, t * P:(t + 1) * P]
                    w.tensor_mul(qq, qq, egb[:, 4 * t:4 * t + 4, :])
                v.drain().then_inc(sem("qdec"), 1)
                for lv in range(6):
                    for t in range(T):
                        n = 2 * lv + t
                        es, ds_ = Em[:, 4 * t:4 * t + 4, :], Dm[:, 4 * t:4 * t + 4, :]
                        idb = ident.unsqueeze(1).broadcast_to([P, H, P])
                        if lv < 5:
                            v.wait_ge(sem("x_mm"), at(l, "x_mm", n + 1))
                            level(lv + 1, t)
                        v.wait_ge(sem("ed_mm"), at(l, "ed_mm", n + 1))
                        last = w.tensor_sub(es, es if lv else idb, ps[6 + t][:, :].rearrange("p (h n) -> p h n", n=P))
                        if lv < 5:
                            last = w.tensor_sub(ds_, ds_ if lv else idb, ps[t][:, :].rearrange("p (h n) -> p h n", n=P))
                        last.then_inc(sem("e_ready"), 1)
                for t in range(T):
                    v.wait_ge(sem("sol_mm"), at(l, "sol_mm", t + 1))
                    last = w.tensor_copy(uu[:, 4 * t:4 * t + 4, :].rearrange("p x y -> p (x y)"), ps[2 + t][:, :])
                v.drain()
                for c in range(S // CHUNK):
                    t, lo = c // 2, CHUNK * (c % 2)
                    rows_ = slice(lo, lo + CHUNK)
                    if c == 0:
                        v.nop().then_inc(sem("vnew"), 1)
                    else:
                        v.wait_ge(sem("pv_mm"), at(l, "pv_mm", c))
                        vv = vnew[rows_, 4 * t:4 * t + 4, :].rearrange("p x y -> p (x y)")
                        w.tensor_sub(vv, vv, ps[6][rows_, :]).then_inc(sem("vnew"), 1)
                    if c < 3:
                        v.wait_ge(sem("st_mm"), at(l, "st_mm", c + 1))
                        if c:
                            v.wait_ge(sem("o_step"), at(l, "o_step", c + 1))
                            for h in range(H):
                                last = w.scalar_tensor_tensor(state[:, h, :], state[:, h, :], egb[:, 4 * t + h, lo + CHUNK - 1:lo + CHUNK],
                                                              ps[1][:, h * P:(h + 1) * P], ALU.mult, ALU.add)
                        else:
                            last = w.tensor_copy(state.rearrange("p x y -> p (x y)"), ps[1][:, :])
                        last.then_inc(sem("state"), 1)
                        v.drain()
                for t in range(T):
                    v.wait_ge(sem("o_sq"), at(l, "o_sq", t + 1))
                    w.tensor_scalar(o_rs[:, 4 * t:4 * t + 4], o_ss[:, 4 * t:4 * t + 4], 1.0 / DK, NORM_EPS, ALU.mult, ALU.add).then_inc(sem("o_sum"), 1)
                    v.wait_ge(sem("o_rs"), at(l, "o_rs", t + 1))
                    w.reciprocal(o_rs[:, 4 * t:4 * t + 4], o_rs[:, 4 * t:4 * t + 4])
                    v.drain()
                    for h in range(H):
                        last = w.scalar_tensor_tensor(uu[:, 4 * t + h, :], ps[7 * (1 - t)][:, h * P:(h + 1) * P], o_rs[:, 4 * t + h:4 * t + h + 1],
                                                      zg[:, t, h * P:(h + 1) * P], ALU.mult, ALU.mult)
                    last.then_inc(sem("o_rows"), 1)
                for i in range(4):
                    v.wait_ge(sem("rot_mm"), at(l, "rot_mm", i + 1))
                    src = (qbT, qbT, kbT, kbT)[i][:, 2 * (i % 2):2 * (i % 2) + 2, :]
                    r3 = rtmp.rearrange("p (x y) -> p x y", y=S)
                    w.tensor_mul(r3, ps[i][:, :].rearrange("p (x y) -> p x y", y=S), C("sin").unsqueeze(1).broadcast_to([P, 2, S]))
                    w.tensor_mul(src, src, C("cos").unsqueeze(1).broadcast_to([P, 2, S]))
                    v.drain()
                    w.tensor_add(src, src, r3)
                    v.drain().then_inc(sem("rotated"), 1)
                attention(l, LAYER_PAIRS)
                layer_norm(l, 0)
                for j in range(FT + 1):
                    if j < FT:
                        v.wait_ge(sem("up_act"), at(l, "up_act", j + 1))
                        for s in range(1, FTAPS):
                            for gv in range(2):
                                c = (2 - s) * 2 * FT + gv * FT + j
                                last = w.scalar_tensor_tensor(facc[:, j % 3, gv, s:S], ps[4 + j % 4][:, gv * S:(gv + 1) * S - s], cw[:, 48 + c:49 + c],
                                                              facc[:, j % 3, gv, s:S], ALU.mult, ALU.add)
                            if s < FTAPS - 1:
                                v.drain()
                        last.then_inc(sem("up_dve"), 1)
                        v.drain()
                    if j:
                        v.wait_ge(sem("up_silu"), at(l, "up_silu", j))
                        w.tensor_mul(hidT[:, j - 1, :], facc[:, (j - 1) % 3, 0, :], facc[:, (j - 1) % 3, 1, :]).then_inc(sem("hid"), 1)
                layer_norm(l, 1)
            if stop_a:
                return

            def rms(n, gsem, gval, dst, done):
                v.wait_ge(sem(gsem), gval)
                for t in range(T):
                    v.wait_ge(sem("r_sq"), 2 * n + t + 1)
                    w.tensor_scalar(rsb[:, t:t + 1], ssq[:, t:t + 1], 1.0 / D, NORM_EPS, ALU.mult, ALU.add).then_inc(sem("r_sum"), 1)
                    v.wait_ge(sem("r_rs"), 2 * n + t + 1)
                    w.reciprocal(rsb[:, t:t + 1], rsb[:, t:t + 1])
                    v.drain()
                    w.scalar_tensor_tensor(dst[:, t, :], x[:, t, :], rsb[:, t:t + 1], gbc, ALU.mult, ALU.mult).then_inc(sem(done), 1)

            L = DEPTH
            v.drain().then_inc(sem("r_in"), 2)
            rms(0, "g1", 16, hrows, "h1_rows")
            v.wait_ge(sem("b_small"), 96)
            for n in range(2):
                w.tensor_mul(lamv[:, 2 * n, :], lamv[:, 2 * n, :], lamv[:, 2 * n + 1, :])
            w.tensor_scalar(subg, subg, 1.0 - LAMBDA_INIT, None, ALU.mult)
            v.drain()
            for n in range(2):
                last = w.tensor_reduce(lame[:, n:n + 1], lamv[:, 2 * n, :], AX.X, ALU.add)
            last.then_inc(sem("lam_dot"), 1)
            v.wait_ge(sem("lam_exp"), 1)
            w.tensor_sub(neglam, lame[:, 3:4], lame[:, 2:3])
            v.drain()
            w.tensor_scalar(neglam, neglam, -LAMBDA_INIT, None, ALU.add)
            v.drain()
            v.wait_ge(sem("bias_back"), 16 * BIAS_HEADS)
            attention(L, SECOND_PAIRS)
            osq = bE.rearrange("p x y z -> p (x y z)")[:, 0:1024]
            oss = lame
            v.wait_ge(sem("at_tr"), at(L, "at_tr", 2 * len(SECOND_PAIRS)))
            v.drain()
            w.tensor_mul(osq, oa.rearrange("p x y -> p (x y)"), oa.rearrange("p x y -> p (x y)"))
            v.drain()
            w.tensor_reduce(oss, osq.rearrange("p (a n) -> p a n", n=P), AX.X, ALU.add)
            v.drain()
            w.tensor_scalar(oss, oss, 1.0 / P, SUBLN_EPS, ALU.mult, ALU.add).then_inc(sem("oa_sum"), 1)
            v.wait_ge(sem("oa_rs"), 1)
            w.reciprocal(oss, oss)
            v.drain()
            for t in range(T):
                for h in range(H):
                    o_ = oa[:, t, h * P:(h + 1) * P]
                    last = w.scalar_tensor_tensor(o_, o_, oss[:, 4 * t + h:4 * t + h + 1], subg, ALU.mult, ALU.mult)
            last.then_inc(sem("oa_rows"), 4)
            v.wait_ge(sem("rows_used"), (DEPTH + 1) * ROW_UNITS + 2)
            for t in range(T):
                for nh in range(2):
                    xs = x[:, t, nh * 512:(nh + 1) * 512]
                    last = w.tensor_add(xs, xs, ps[4 + 2 * t + nh][:, :])
            last.then_inc(sem("r_in"), 2)
            v.drain().then_inc(sem("att_over"), 1)
            rms(1, "g2", 16, hrows, "h2_rows")
            v.wait_ge(sem("logits"), 1)
            lg = ps[4][:, 0:2 * NE].rearrange("p (t n) -> p t n", n=NE)
            w.tensor_copy(rl, lg)
            w.tensor_reduce(rmax, lg, AX.X, ALU.max, negate=True)
            v.drain().then_inc(sem("rl_ready"), 1)
            v.wait_ge(sem("rl_exp"), 1)
            w.reciprocal(rsum, rsum)
            v.drain()
            w.tensor_mul(rl, rl, rsum.unsqueeze(2).broadcast_to([P, T, NE])).then_inc(sem("aff"), 1)
            v.wait_ge(sem("aff_tr"), 1)
            w.tensor_copy(affT, ps[5][0:NE, 0:S])
            v.drain()
            for r in range(CAP // 8):
                cur = affT if r % 2 == 0 else affW
                nxt = affW if r % 2 == 0 else affT
                w.max(topv[:, 8 * r:8 * r + 8], cur)
                v.drain()
                w.max_index(topidx[:, 8 * r:8 * r + 8], topv[:, 8 * r:8 * r + 8], cur)
                w.match_replace(nxt, topv[:, 8 * r:8 * r + 8], cur, -1.0)
                v.drain()
            w.tensor_copy(topf, topidx)
            v.drain()
            w.tensor_mul(spread.rearrange("p (e s) -> p e s", s=CAP), topf.unsqueeze(1).broadcast_to([NE, NE, CAP]), C("own")[0:NE, :].rearrange("p (e s) -> p e s", s=CAP))
            w.tensor_copy(rep[:, 0:P].rearrange("p (q s) -> p q s", s=CAP), topf.unsqueeze(1).broadcast_to([NE, 4, CAP]))
            w.tensor_copy(rep[:, P:2 * P].rearrange("p (q s) -> p q s", s=CAP), topv.unsqueeze(1).broadcast_to([NE, 4, CAP]))
            v.drain().then_inc(sem("chosen"), 1)
            v.wait_ge(sem("spread_mm"), 1)
            for t in range(T):
                last = w.tensor_scalar(oneT[:, t, :], ps[6][:, :], C("tok_col")[:, t:t + 1], None, ALU.is_equal)
            last.then_inc(sem("onehot"), 1)
            w.tensor_copy(idx4, ps[7][:, 0:NE])
            w.tensor_copy(g4, ps[7][:, NE:2 * NE])
            v.drain()
            v.wait_ge(sem("xe_evac"), KT)
            w.memset(hh[64:P, 5, :], 0.0)
            with v.Fori(0, NE) as e:
                w.tensor_copy(xe, xeT[:, :, bass.ds(e * CAP, CAP)])
                w.tensor_scalar(pg, C("tok_row"), idx4[:, bass.ds(e, 1)], g4[:, bass.ds(e, 1)], ALU.is_equal, ALU.mult)
                v.drain().then_inc(sem("xe_ready"), 1)
                for b, (c0, n) in enumerate(PIECES):
                    v.wait_ge(sem("esg"), e * 3 + b + 1)
                    for odd in range(2):
                        m = 2 if odd == 0 or b < 2 else 1
                        blocks = lambda y: y.rearrange("p (m n) -> p m n", n=P)[:, odd::2, :][:, 0:m, :]
                        last = w.tensor_mul(hh[64 * odd:64 * odd + 64, 2 * b:2 * b + m, :], blocks(sg[0:64, c0:c0 + n]), blocks(ps[b][64:P, 0:n]))
                    last.then_inc(sem("eh"), 1)
                v.wait_ge(sem("eo_mm"), e + 1)
                for q in range(4):
                    xs = x[:, :, q * 256:(q + 1) * 256]
                    w.tensor_add(xs, xs, ps[OUT_BANKS[q]][:, :].rearrange("p (t n) -> p t n", n=256))
                v.drain()
            v.nop().then_inc(sem("r_in"), 2)
            rms(2, "g3", 16, x, "final_rows")


_INS = ["x", "w_in", "gdn_conv_w", "gdn_a_log", "gdn_dt_bias", "gdn_norm_g", "w_out", "ln1_g", "ln1_b", "w_up",
        "ffn_conv_w", "ffn_conv_b", "w_down", "ln2_g", "ln2_b", "norm1_g_2", "w_in_2", "lam_q1_2", "lam_k1_2",
        "lam_q2_2", "lam_k2_2", "subln_g_2", "w_out_2", "rel_bias_2", "norm2_g_2", "w_router_2", "w_gate_2",
        "w_up_2", "w_down_2", "norm_f_g_2"]


def kernel(**inputs):
    import concourse.bacc as bacc
    from concourse.bass_utils import run_bass_kernel_spmd

    nc = bacc.Bacc("TRN2", target_bir_lowering=False, num_devices=1)
    consts, cat = constants()
    table, takes = bias_tables()
    arrays = {"consts": consts, "bias_table": table, "takes": takes}
    for name in _INS:
        v = np.ascontiguousarray(inputs[name])
        arrays[name] = v.reshape(1, -1) if v.ndim == 1 else v
    a = {name: nc.dram_tensor("in_" + name, v.shape, mybir.dt.from_np(v.dtype), kind="ExternalInput").ap() for name, v in arrays.items()}
    out = nc.dram_tensor("out", (1, S, D), F32, kind="ExternalOutput").ap()
    scratch = nc.dram_tensor("bias_rows", (BIAS_HEADS, P * 2 * S), F32, kind="Internal").ap()
    build(nc, a, out, scratch, cat)
    r = run_bass_kernel_spmd(nc, [{"in_" + name: v for name, v in arrays.items()}], core_ids=[0])
    return r.results[0]["out"]
```

```python
import numpy as np
from contextlib import ExitStack

import concourse.bass as bass
from concourse import mybir

F32 = mybir.dt.float32
U32 = mybir.dt.uint32
ACT = mybir.ActivationFunctionType
ALU = mybir.AluOpType
AX = mybir.AxisListType

P = 128
S = 256
T = S // P
D = 1024
KT = D // P
DEPTH = 2
H = 4
DK = 128
QKV = 3 * H * DK
CHUNK = 64
FF = 2816
FT = FF // P
TAPS, FTAPS = 4, 3
ROPE_HALF, ROPE_THETA, DH = 8, 500000.0, 64
NE, CAP = 16, 32
BUCKETS, BIAS_HEADS = 32, 12
ALPHA = (2 * DEPTH) ** 0.25
LN_EPS, NORM_EPS, SUBLN_EPS = 1e-5, 1e-6, 1e-5
LAMBDA_INIT = 0.2
NEG = -1e30

RING = 4
SBUF_FLOATS = 53200
SLOT = 4096
OFF = {"q": 0, "k": 512, "v": 1024, "ab": 1536, "z": 1544, "qb": 2056, "kb": 2568, "vb": 3080}
UNITS_IN = ["q", "k", "v", "ab", "z", "qb", "kb", "vb"]
U_OUT, U_UP, U_DOWN = 8, 10, 21
DOWN_TILES = [4, 3, 3, 3, 3, 3, 3]
UNITS = 28
ROW_UNITS = 2 + len(DOWN_TILES)
UNITS_IN_2 = [0, 512, 1024, 1536, 2048, 2560]
GU_RING, D_RING = 4, 11
HALF = FF // 2
HT = HALF // P
PIECES = [(0, 512), (512, 512), (1024, 384)]
IN_BANKS = (0, 1, 4, 5, 0, 1, 6, 7, 4, 5)
UP_BANKS = (0, 1, 4, 5)
AHEAD = 3
ROT_BANKS = (6, 1, 4, 5)
XE_BANKS, FIRST = (3, 4, 6, 7), 4 * CAP
ROWS_BANKS = (2, 3, 6, 7)
H2_BANKS = (0, 1, 4, 5)
HID_BANKS, OUT_BANKS = (3, 4, 6), (6, 7, 3, 4)


def constants():
    i = np.arange(P)[:, None]
    j = np.arange(P)[None, :]
    same = (i // CHUNK) == (j // CHUNK)
    neg = lambda ok: np.where(ok, 0.0, NEG)
    parts = {
        "ident": (i == j) * 1.0,
        "ones": np.ones((P, P)),
        "eps": np.broadcast_to(np.array([[LN_EPS, NORM_EPS, SUBLN_EPS, 0.0]]), (P, 4)),
        "cum": (same & (i <= j)) * 1.0,
        "neg_strict": neg(same & (i > j)),
        "neg_incl_t": neg(same & (i <= j)),
    }
    for n in range(6):
        s = 1 << n
        parts[f"level{n}"] = ((i // (2 * s) == j // (2 * s)) & (i % (2 * s) >= s) & (j % (2 * s) < s)) * 1.0
    rot = np.zeros((P, P))
    cos, sin = np.ones((P, S)), np.zeros((P, S))
    inv = np.float32(ROPE_THETA) ** (-np.arange(ROPE_HALF, dtype=np.float32) / np.float32(ROPE_HALF))
    ang = np.arange(S, dtype=np.float32)[:, None] * inv[None, :].astype(np.float32)
    for h in range(P // DH):
        for c in range(ROPE_HALF):
            a, b = h * DH + c, h * DH + ROPE_HALF + c
            rot[b, a], rot[a, b] = -1.0, 1.0
            cos[[a, b]] = np.cos(ang[:, c])
            sin[[a, b]] = np.sin(ang[:, c])
    parts["rot"], parts["cos"], parts["sin"] = rot, cos, sin
    jj = np.arange(3 * P)[None, :]
    parts["causal"] = neg(jj <= i + P)
    parts["tok_row"] = np.broadcast_to(np.arange(S)[None, :], (P, S))
    parts["tok_col"] = np.concatenate([i, i + P], 1)
    own = (np.arange(NE)[:, None] == (np.arange(NE * CAP) // CAP)[None, :]) * 1.0
    parts["own"] = np.concatenate([own, np.zeros((P - NE, NE * CAP))])
    at, cols = {}, 0
    for name, a in parts.items():
        at[name] = (cols, a.shape[1])
        cols += a.shape[1]
    return np.ascontiguousarray(np.concatenate([np.asarray(a, np.float32) for a in parts.values()], 1)), at


def bias_tables():
    rel = np.arange(-(S - 1), S + 1)
    n = np.abs(rel)
    half, exact = BUCKETS // 2, BUCKETS // 4
    nf = np.maximum(n, 1).astype(np.float32)
    large = exact + (np.log(nf / np.float32(exact)) / np.float32(np.log(1024 / exact)) * np.float32(half - exact)).astype(np.int32)
    bucket = np.where(rel > 0, half, 0) + np.where(n < exact, n, np.minimum(large, half - 1))
    count = (n <= 64) * 1 + (rel % 4 == 0) * 1 + (rel % 16 == 0) * 1
    table = np.zeros((BUCKETS + 1, 2 * S), np.float32)
    table[bucket, np.arange(2 * S)] = 1.0
    table[BUCKETS] = np.where(count > 0, np.log(np.maximum(count, 1)), NEG)
    takes = np.zeros((1, BIAS_HEADS), np.float32)
    takes[0, H:] = 1.0
    return table, takes


PER = dict(
    x_rows=4, rows_t0=2, x0_tr=2, x0T=2, x1_tr=4, x1T=4, x_tr=8, conv_rows=64, small=48, ln1=32, ln2=32, cw_tr=1, cw_ready=1,
    proj=14, tap=6, taps=6, silu=6, act_evac=8, ab_mm=1, ab_pre=1, ab_act=1, g_ready=1,
    sq=4, ss_mm=1, ss_sum=1, ss_ln=1, cum_mm=1, cum_read=1, egb_read=1, zg=1, arg_ready=1, dec=1, rows_tr=4, rows_a=1, rows_v=1,
    kk_mm=1, a_ready=1, x_mm=12, x_evac=12, ed_mm=12, dec_cols=1, e_ready=12, lvl=12, sol_mm=2, u_ready=1, w_ready2=1,
    qdec=1, pv_mm=3, vnew=4, st_mm=3, state=3, o_step=4, o_sq=2, o_sum=2, o_rs=2, o_rows=2, o_tr=2, mix_o=2,
    rot_mm=4, rotated=4, at_s=8, at_read=8, at_exp=8, at_prob=8, at_tr=8, at_pt=8, at_pv=4, at_out=4,
    mo_mm=1, y_stat=4, y_rs=4, up=22, up_act=22, up_dve=22, up_silu=22, hid=22, dn_mm=1,
)


def build(nc, a, out, scratch, CAT, STOP=None):
    ctx = ExitStack()
    with ctx:
        free = SBUF_FLOATS
        arena = ctx.enter_context(nc.sbuf_tensor("arena", [P, free], F32))
        ps = [ctx.enter_context(nc.psum_tensor(f"bank{i}", [P, 512], F32)) for i in range(8)]
        sems = {}

        def sem(name):
            if name not in sems:
                sems[name] = ctx.enter_context(nc.semaphore(name))
            return sems[name]

        def at(l, name, k):
            return l * PER[name] + k

        class Region:
            def __init__(self, lo, hi):
                self.at, self.hi = lo, hi

            def take(self, *dims):
                n = int(np.prod(dims))
                assert self.at + n <= self.hi, (dims, self.at, n, self.hi)
                v = arena[:, self.at:self.at + n]
                self.at += n
                if len(dims) == 2:
                    v = v.rearrange("p (x y) -> p x y", y=dims[1])
                if len(dims) == 3:
                    v = v.rearrange("p (x y z) -> p x y z", y=dims[1], z=dims[2])
                if len(dims) == 4:
                    v = v.rearrange("p (x y z w) -> p x y z w", y=dims[1], z=dims[2], w=dims[3])
                return v

        NC = sum(n for _, n in CAT.values())
        keep = Region(0, free)
        const = keep.take(NC)
        C = lambda name: const[:, CAT[name][0]:CAT[name][0] + CAT[name][1]]
        ident, ones = C("ident"), C("ones")
        ln_eps, norm_eps, subln_eps = (C("eps")[:, i:i + 1] for i in range(3))
        x = keep.take(T, D)
        xT = keep.take(KT, S)
        mixT = keep.take(KT, S)
        st6 = keep.take(T, 2, 6)
        mv = keep.take(T, 2)
        rs = keep.take(T, 1)
        mx, sm, rc = keep.take(4, 2), keep.take(4, 2), keep.take(4, 2)
        lo_ring = keep.at
        ring = keep.take(RING, SLOT)
        lo_free = keep.at
        gu = Region(lo_ring, free).take(GU_RING, 2, FF)
        dreg = Region(lo_ring + GU_RING * 2 * FF, free)
        dring = dreg.take(D_RING, D)
        c_lo = dreg.at

        def slot(u, n=None):
            v = ring[:, u % RING, :]
            return v if n is None else v.rearrange("p (k n) -> p k n", n=n)

        A = Region(lo_free, free)
        ln_g, ln_b = A.take(D), A.take(D)
        convrow = A.take(3, P)
        cw = A.take(48 + 88 + 88)
        dtb, alog, ng = A.take(H), A.take(H), A.take(P)
        mark = A.at
        qkv = A.take(12, S)
        qbT, kbT = A.take(4, S), A.take(4, S)
        vb, zg = A.take(T, 512), A.take(T, 512)
        small = A.take(240)
        so = [0]

        def tiny(*dims):
            n = int(np.prod(dims))
            v = small[:, so[0]:so[0] + n]
            so[0] += n
            assert so[0] <= 240
            return v if len(dims) == 1 else v.rearrange("p (x y) -> p x y", y=dims[1])
        ar, br, nab, eb, ea, el, g, beta = (tiny(T, H) for _ in range(8))
        eal = tiny(H)
        ss, lnh, tot, etot = (tiny(2 * T * H) for _ in range(4))
        gm = tiny(2, T * H)
        gcol, ngcol, egc, beg, gl, ekd, o_ss, o_rs = (tiny(T * H) for _ in range(8))
        gdn = A.at
        l2 = A.take(4, 512)
        gb = A.take(8, P)
        decS = A.take(8, P)
        decT = A.take(8, P)
        egb = A.take(8, P)
        bk, kdec, bv = A.take(8, P), A.take(8, P), A.take(8, P)
        Am, Dm, Em = A.take(8, P), A.take(8, P), A.take(8, P)
        Lm, Xm = l2.rearrange("p x y -> p (x y)")[:, 0:1024].rearrange("p (x y) -> p x y", y=P), l2.rearrange("p x y -> p (x y)")[:, 1024:2048].rearrange("p (x y) -> p x y", y=P)
        attT = decT
        uu, vnew, wT = gb, gb, decS
        state = A.take(H, P)
        lnb = l2.rearrange("p x y -> p (x y)").rearrange("p (x y) -> p x y", y=P)
        G = Region(gdn, free)
        att_e = G.take(4, 2, S)
        att_pt = G.take(2, 4, S)
        rtmp = G.take(512)
        Fr = Region(mark, free)
        hidT = Fr.take(FT, S)
        facc = Fr.take(3, 2, S)
        a_end = A.at

        bg = Region(c_lo, free)
        hrows = bg.take(T, D)
        gbc = bg.take(D)
        xeT = bg.take(KT, NE * CAP)
        oneT = bg.take(T, NE * CAP)
        c_tiny = bg.take(320)
        c_end = bg.at
        B = Region(lo_free, c_lo)
        qaT, kaT, qdT, kdT = (B.take(4, S) for _ in range(4))
        va, vd = B.take(T, 512), B.take(T, 512)
        bE = B.take(4, 2, S)
        bPT = B.take(2, 4, S)
        bias12 = Region(c_lo + T * D + D, free).take(BIAS_HEADS, 3 * P)
        oa = B.take(T, 512)
        pro = Region(max(c_end, a_end), free)
        tb_sb, btab, brel = pro.take(2 * S), pro.take(2 * S), pro.take(BIAS_HEADS)
        E2 = mixT.rearrange("p x y -> p (x y)")
        sg = E2[:, 0:HALF]
        xe = xT.rearrange("p x y -> p (x y)")[:, 0:KT * CAP].rearrange("p (k s) -> p k s", s=CAP)
        pg = xT.rearrange("p x y -> p (x y)")[:, 256:512]
        hT = xT.rearrange("p x y -> p (x y)")[:, 512:512 + (HT + 1) * 64].rearrange("p (k s) -> p k s", s=64)
        yq = xT.rearrange("p x y -> p (x y)")[:, 1280:1536]
        hh = hrows.rearrange("p x y -> p (x y)")[:, 0:6 * P].rearrange("p (m n) -> p m n", n=P)
        to = [0]

        def ct(*dims):
            n = int(np.prod(dims))
            v = c_tiny[:, to[0]:to[0] + n]
            to[0] += n
            assert to[0] <= 320
            return v if len(dims) == 1 else v.rearrange("p (x y) -> p x y", y=dims[1])
        wr = ct(KT, NE)
        topidx = ct(CAP)[0:NE, :].bitcast(U32)
        ssq, rsb = ct(T), ct(T)
        neglam = ct(1)
        subg = Region(B.at, c_lo).take(P)
        lamv = Region(B.at + P, c_lo).take(4, DH)
        lame = Region(B.at + P + 256, c_lo).take(8)
        rl, rmax, rsum = ct(T, NE), ct(T), ct(T)
        affT = oneT.rearrange("p x y -> p (x y)")[0:NE, 0:S]
        affW = oneT.rearrange("p x y -> p (x y)")[0:NE, S:2 * S]
        topv = xeT.rearrange("p x y -> p (x y)")[0:NE, 0:CAP]
        topf = xeT.rearrange("p x y -> p (x y)")[0:NE, 64:64 + CAP]
        spread = xeT.rearrange("p x y -> p (x y)")[0:NE, 512:1024]
        rep = xeT.rearrange("p x y -> p (x y)")[0:NE, 1024:1280]
        idx4, g4 = ct(NE), ct(NE)

        block = ctx.enter_context(nc.Block())
        stop_a = STOP == "a"

        @block.sync
        def _(sp):
            sp.dma_start(x, a["x"][0].rearrange("(t p) n -> p t n", p=P)).then_inc(sem("x_in"), 16)
            sp.dma_start(const[:, 0:2 * P + 4], a["consts"][:, 0:2 * P + 4]).then_inc(sem("ident_in"), 16)
            sp.sem_inc(sem("rows_used"), ROW_UNITS)

            def used(l, u):
                if u in (0, 1, 2):
                    return "proj", at(l, "proj", 2 * (u + 1))
                if u == 3:
                    return "ab_mm", at(l, "ab_mm", 1)
                if u < U_OUT:
                    return "proj", at(l, "proj", 2 * u)
                if U_UP <= u < U_DOWN:
                    return "up", at(l, "up", 2 * (u - U_UP + 1))
                return "rows_used", (l + 1) * ROW_UNITS + (u - U_OUT + 1 if u < U_UP else u - U_DOWN + 3)

            def stream(l, u, halves, before=None):
                name, value = before or (used(l, u - RING) if u >= RING else used(l - 1, UNITS + u - RING))
                sp.wait_ge(sem(name), value)
                for to_, from_ in halves:
                    sp.dma_start(to_, from_).then_inc(sem(f"slot_in{u % RING}"), 16)

            def columns(w, l, c, n, u):
                v = w[bass.ds(l, 1), :, c:c + n].rearrange("o (k p) n -> p (o k) n", p=P)
                s = slot(u, 512)[:, :, 0:n]
                return [(s[:, 0:4], v[:, 0:4]), (s[:, 4:8], v[:, 4:8])]

            def rows(w, l, k0, n, u):
                v = w[bass.ds(l, 1), k0 * P:(k0 + n) * P, :].rearrange("o (k p) n -> p (o k) n", p=P)
                s = slot(u, 1024)
                h = n // 2
                return [(s[:, 0:h], v[:, 0:h]), (s[:, h:n], v[:, h:n])]

            def bcast(w, l, n):
                return w[bass.ds(l, 1), :].broadcast_to([P, n])

            with sp.Fori(0, DEPTH) as l:
                for u, name in enumerate(UNITS_IN):
                    stream(l, u, columns(a["w_in"], l, OFF[name], 8 if name == "ab" else 512, u))
                    if u == RING - 1:
                        sp.wait_ge(sem("x_rows"), at(l, "x_rows", 2))
                        c = a["gdn_conv_w"][bass.ds(l, 1)].rearrange("o j (t p) -> (o j t) p", p=P)
                        sp.dma_start(convrow[0:48, 0, :], c).then_inc(sem("conv_rows"), 16)
                        f = a["ffn_conv_w"][bass.ds(l, 1)].rearrange("o j (t p) -> (o j t) p", p=P)
                        sp.dma_start(convrow[0:88, 1, :], f[0:88, :]).then_inc(sem("conv_rows"), 16)
                        sp.dma_start(convrow[0:44, 2, :], f[88:132, :]).then_inc(sem("conv_rows"), 8 * 2)
                        sp.dma_start(convrow[44:88, 2, :], a["ffn_conv_b"][bass.ds(l, 1)].rearrange("o (t p) -> (o t) p", p=P)).then_inc(sem("conv_rows"), 16)
                        sp.dma_start(dtb, bcast(a["gdn_dt_bias"], l, H)).then_inc(sem("small"), 16)
                        sp.dma_start(alog, bcast(a["gdn_a_log"], l, H)).then_inc(sem("small"), 16)
                        sp.dma_start(ng, bcast(a["gdn_norm_g"], l, P)).then_inc(sem("small"), 16)
                        sp.dma_start(ln_g, bcast(a["ln1_g"], l, D)).then_inc(sem("ln1"), 16)
                        sp.dma_start(ln_b, bcast(a["ln1_b"], l, D)).then_inc(sem("ln1"), 16)
                for i in range(2):
                    stream(l, U_OUT + i, rows(a["w_out"], l, 4 * i, 4, U_OUT + i))
                for i in range(11):
                    u = U_UP + i
                    s = slot(u, 512)
                    g_ = a["w_up"][bass.ds(l, 1), :, 256 * i:256 * i + 256].rearrange("o (k p) n -> p (o k) n", p=P)
                    v_ = a["w_up"][bass.ds(l, 1), :, FF + 256 * i:FF + 256 * i + 256].rearrange("o (k p) n -> p (o k) n", p=P)
                    stream(l, u, [(s[:, :, 0:256], g_), (s[:, :, 256:512], v_)])
                    if i == RING - 1:
                        sp.wait_ge(sem("x_rows"), at(l, "x_rows", 4))
                        sp.dma_start(ln_g, bcast(a["ln2_g"], l, D)).then_inc(sem("ln2"), 16)
                        sp.dma_start(ln_b, bcast(a["ln2_b"], l, D)).then_inc(sem("ln2"), 16)
                k0 = 0
                for i, n in enumerate(DOWN_TILES):
                    stream(l, U_DOWN + i, rows(a["w_down"], l, k0, n, U_DOWN + i))
                    k0 += n
            if stop_a:
                sp.wait_ge(sem("x_rows"), 2 + 2 * PER["x_rows"])
                sp.dma_start(out[0].rearrange("(t p) n -> p t n", p=P), x).then_inc(sem("stored"), 16)
                sp.wait_ge(sem("stored"), 16)
                return
            for u, c in enumerate(UNITS_IN_2):
                stream(DEPTH, u, columns(a["w_in_2"], 0, c, 512, u), ("b_proj", 2 * (u - RING + 1)) if u >= RING else None)
            for i in range(2):
                stream(DEPTH, 6 + i, rows(a["w_out_2"], 0, 4 * i, 4, 6 + i), ("b_proj", 2 * (3 + i)))
            sp.sem_inc(sem("gu_free"), GU_RING)
            sp.sem_inc(sem("d_free"), D_RING)

            def gate_up(e, k):
                for n, w in enumerate(("w_gate_2", "w_up_2")):
                    sp.dma_start(gu[:, k % GU_RING, n, :], a[w][0, bass.ds(e, 1), k * P:(k + 1) * P, :].rearrange("o p n -> (o p) n")
                                 ).then_inc(sem(f"gu_in{k % GU_RING}"), 16)

            def down(e, k):
                sp.dma_start(dring[:, k % D_RING, :], a["w_down_2"][0, bass.ds(e, 1), k * P:(k + 1) * P, :].rearrange("o p n -> (o p) n")
                             ).then_inc(sem(f"d_in{k % D_RING}"), 16)

            sp.wait_ge(sem("b_proj"), 12)
            gate_up(0, 0)
            sp.wait_ge(sem("oa_tr"), 1)
            gate_up(0, 3)
            for k in range(D_RING):
                down(0, k)
            sp.wait_ge(sem("rows_used"), (DEPTH + 1) * ROW_UNITS + 2)
            gate_up(0, 1)
            gate_up(0, 2)

            def rest_of_expert(e, gu_done, d_done):
                for k in range(gu_done, KT):
                    sp.wait_ge(sem("gu_free"), e * KT + k + 1)
                    gate_up(e, k)
                for k in range(d_done, FT):
                    sp.wait_ge(sem("d_free"), e * FT + k + 1)
                    down(e, k)
            rest_of_expert(0, GU_RING, D_RING)
            with sp.Fori(1, NE) as e:
                rest_of_expert(e, 0, 0)
            for t in range(T):
                sp.wait_ge(sem("final_rows"), t + 1)
                sp.dma_start(out[0, t * P:(t + 1) * P, :], x[:, t, :]).then_inc(sem("stored"), 16)
            sp.wait_ge(sem("stored"), 16 * T)

        @block.gpsimd
        def _(pool):
            pool.wait_ge(sem("slot_in1"), 32)
            pool.dma_start(const[:, 2 * P + 4:NC], a["consts"][:, 2 * P + 4:NC]).then_inc(sem("const_in"), 16)
            pool.dma_start(btab[0:BUCKETS + 1, :], a["bias_table"]).then_inc(sem("bias_in"), 16)
            pool.dma_start(brel[0:BUCKETS, :], a["rel_bias_2"]).then_inc(sem("bias_in"), 16)
            pool.dma_start(brel[BUCKETS:BUCKETS + 1, :], a["takes"]).then_inc(sem("bias_in"), 16)

            if stop_a:
                return
            with pool.Fori(0, DEPTH) as l:
                pool.wait_ge(sem("act_evac"), at(l, "act_evac", 2))
                pool.wait_ge(sem("small"), l * 48 + 48)
                for t in range(T):
                    zz = zg[:, t, :].rearrange("p (h n) -> p h n", n=P)
                    last = nc.gpsimd.tensor_tensor(zz, zz, ng.unsqueeze(1).broadcast_to([P, H, P]), ALU.mult)
                last.then_inc(sem("zg"), 1)
                pool.wait_ge(sem("kk_mm"), at(l, "kk_mm", 1))
                pool.wait_ge(sem("egb_read"), at(l, "egb_read", 1))
                for t in range(T):
                    qq = qkv[:, 0:4, t * P:(t + 1) * P]
                    last = nc.gpsimd.tensor_tensor(qq, qq, egb[:, 4 * t:4 * t + 4, :], ALU.mult)
                last.then_inc(sem("qdec"), 1)
            pool.wait_ge(sem("x_rows"), at(DEPTH, "x_rows", 2))
            pool.dma_start(gbc, a["norm1_g_2"].broadcast_to([P, D])).then_inc(sem("g1"), 16)
            pool.wait_ge(sem("bias_sb"), 1)
            pool.dma_start(scratch.rearrange("h (p n) -> h p n", p=P), tb_sb[0:BIAS_HEADS, :].unsqueeze(1).broadcast_to([BIAS_HEADS, P, 2 * S])).then_inc(sem("bias_out"), 16)
            pool.wait_ge(sem("bias_out"), 16)
            for h in range(BIAS_HEADS):
                v = scratch[h:h + 1, P - 1:P - 1 + P * (2 * S - 1)].rearrange("o (p n) -> (o p) n", p=P)[:, 0:3 * P]
                pool.dma_start(bias12[:, h, :], v).then_inc(sem("bias_back"), 16)
            pool.dma_start(subg, a["subln_g_2"].broadcast_to([P, P])).then_inc(sem("b_small"), 16)
            for n, name in enumerate(("lam_q1_2", "lam_k1_2", "lam_q2_2", "lam_k2_2")):
                pool.dma_start(lamv[:, n, :], a[name].broadcast_to([P, DH])).then_inc(sem("b_small"), 16)
            pool.dma_start(wr, a["w_router_2"][0].rearrange("(k p) e -> p k e", p=P)).then_inc(sem("b_small"), 16)
            pool.wait_ge(sem("h1_rows"), T)
            pool.dma_start(gbc, a["norm2_g_2"].broadcast_to([P, D])).then_inc(sem("g2"), 16)
            pool.wait_ge(sem("h2_rows"), T)
            pool.dma_start(gbc, a["norm_f_g_2"].broadcast_to([P, D])).then_inc(sem("g3"), 16)

        LAYER_PAIRS = [("causal", n) for n in range(4)]
        SECOND_PAIRS = [("diff", n) for n in range(4)] + [("dil", n) for n in range(4)]
        SC, TR, PV = ((2, 3), (4, 5)), (6, 7), (0, 1)

        def attention_operands(kind):
            if kind == "causal":
                return qbT, kbT, vb, att_e, att_pt
            return (qaT, kaT, va, bE, bPT) if kind == "diff" else (qdT, kdT, vd, bE, bPT)

        def out_read(l, pairs, pi):
            kind = pairs[pi][0]
            done = sum(1 for k_, _ in pairs[:pi + 1] if k_ == kind)
            return (sem("oa_read"), done) if kind == "diff" else (sem("at_out"), at(l, "at_out", done))

        @block.tensor
        def _(pe):
            mm, tr = nc.tensor.matmul, nc.tensor.transpose

            def unit_in(l, u):
                pe.wait_ge(sem(f"slot_in{u % RING}"), l * (UNITS // RING * 32) + 32 * (u // RING + 1))

            def transpose_x(src, t, done):
                for kh in range(2):
                    for k in range(4):
                        last = tr(ps[4 + 2 * t + kh][:, k * P:(k + 1) * P], src[:, t, (4 * kh + k) * P:(4 * kh + k + 1) * P], ident)
                    if t or kh:
                        last.then_inc(sem(done), 1)

            def second_tile(l, n):
                pe.wait_ge(sem("x_rows"), at(l, "x_rows", 2 * n + 2))
                transpose_x(x, 1, "x1_tr")
                pe.wait_ge(sem("x1T"), at(l, "x1T", 2 * n + 2))

            def channels(u, j0, bank, t=None, step=1):
                w = slot(u, 512)
                lo, n = (0, S) if t is None else (t * P, P)
                for j in range(2):
                    c = (j0 + j * step) * P
                    for k in range(KT):
                        last = mm(ps[bank][:, j * S + lo:j * S + lo + n], w[:, k, c:c + P], xT[:, k, lo:lo + n], start=(k == 0), stop=(k == KT - 1))
                return last

            def tokens(u, t, bank):
                w = slot(u, 512)
                for k in range(KT):
                    last = mm(ps[bank][:, :], xT[:, k, t * P:(t + 1) * P], w[:, k, :], start=(k == 0), stop=(k == KT - 1))
                return last

            def rows_product(l, lhsT, u0, tiles, ready, between=None):
                split = len(tiles) - 2
                done, K = 0, sum(tiles)

                def products(u, k0, t):
                    w = slot(u0 + u, 1024)
                    for kk in range(tiles[u]):
                        if t == 0:
                            ready(k0 + kk)
                        for nh in range(2):
                            last = mm(ps[ROWS_BANKS[2 * t + nh]][:, :], lhsT[:, k0 + kk, t * P:(t + 1) * P], w[:, kk, nh * 512:(nh + 1) * 512],
                                      start=(k0 + kk == 0), stop=(k0 + kk == K - 1))
                    return last

                for u in range(split):
                    unit_in(l, u0 + u)
                    products(u, done, 0)
                    products(u, done, 1).then_inc(sem("rows_used"), 1)
                    done += tiles[u]
                for t in range(T):
                    k0 = done
                    for u in (split, split + 1):
                        if t == 0:
                            unit_in(l, u0 + u)
                        elif u == split + 1 and between:
                            between()
                        last = products(u, k0, t)
                        k0 += tiles[u]
                        if t:
                            last.then_inc(sem("rows_used"), 1)
                    if t == 0:
                        last.then_inc(sem("rows_t0"), 1)

            def attention(l, pairs, before_transposes=None):
                n = 2 * len(pairs)
                for i in range(n + 4):
                    if i < n:
                        kind, pr = pairs[i // 2]
                        q, k, _, E, PT = attention_operands(kind)
                        if i >= 2:
                            pe.wait_ge(sem("at_read"), at(l, "at_read", i - 1))
                        for m in range(2):
                            last = mm(ps[SC[i % 2][m]][:, 0:S], q[64 * m:64 * m + 64, pr, (i % 2) * P:(i % 2 + 1) * P],
                                      k[64 * m:64 * m + 64, pr, :], start=True, stop=True)
                        last.then_inc(sem("at_s"), 1)
                    if i == 2 and before_transposes:
                        before_transposes()
                    if 2 <= i < n + 2:
                        b = i - 2
                        kind, pr = pairs[b // 2]
                        E = attention_operands(kind)[3]
                        pe.wait_ge(sem("at_prob"), at(l, "at_prob", b + 1))
                        if b >= 2:
                            pe.wait_ge(sem("at_pt"), at(l, "at_pt", b - 1))
                        for m in range(1 if kind == "diff" else 2):
                            for kt in range(T):
                                last = tr(ps[TR[b % 2]][:, (2 * m + kt) * P:(2 * m + kt + 1) * P], E[:, b % 4, m, kt * P:(kt + 1) * P], ident)
                        last.then_inc(sem("at_tr"), 1)
                    if i >= 5 and i % 2 == 1:
                        pi = (i - 5) // 2
                        kind, pr = pairs[pi]
                        _, _, v, _, PT = attention_operands(kind)
                        pe.wait_ge(sem("at_pt"), at(l, "at_pt", 2 * pi + 2))
                        if pi >= 2:
                            pe.wait_ge(*out_read(l, pairs, pi - 2))
                        bank = ps[PV[pi % 2]]
                        if kind == "diff":
                            for t in range(T):
                                for kt in range(T):
                                    last = mm(bank[:, t * P:(t + 1) * P], PT[:, pi % 2, kt, t * P:(t + 1) * P],
                                              v[:, kt, pr * P:(pr + 1) * P], start=(kt == 0), stop=(kt == T - 1))
                        else:
                            for m in range(2):
                                for kt in range(T):
                                    last = mm(bank[64 * m:64 * m + 64, 0:S], v[:, kt, (2 * pr + m) * DH:(2 * pr + m + 1) * DH],
                                              PT[:, pi % 2, 2 * m + kt, :], start=(kt == 0), stop=(kt == T - 1))
                        last.then_inc(sem("at_pv"), 1)

            pe.wait_ge(sem("ident_in"), 16)

            def first_tile(rows):
                pe.wait_ge(sem("x_rows"), rows)
                transpose_x(x, 0, "x0_tr")

            first_tile(1)
            with pe.Fori(0, DEPTH) as l:
                pe.wait_ge(sem("x0T"), at(l, "x0T", 1))
                for i in range(AHEAD):
                    if i % 2 == 0:
                        unit_in(l, i // 2)
                    channels(i // 2, 2 * (i % 2), IN_BANKS[i], t=0)
                second_tile(l, 0)
                for i in range(6):
                    if i < AHEAD:
                        channels(i // 2, 2 * (i % 2), IN_BANKS[i], t=1).then_inc(sem("proj"), 1)
                    else:
                        if i % 2 == 0:
                            unit_in(l, i // 2)
                        if i >= 4:
                            pe.wait_ge(sem("taps"), at(l, "taps", i - 3))
                        channels(i // 2, 2 * (i % 2), IN_BANKS[i]).then_inc(sem("proj"), 1)
                    if i == 1:
                        pe.wait_ge(sem("conv_rows"), at(l, "conv_rows", 64))
                        tr(ps[2][:, 48:136], convrow[0:88, 1, :], ident[0:88, 0:88])
                        tr(ps[2][:, 136:224], convrow[0:88, 2, :], ident[0:88, 0:88])
                        tr(ps[2][:, 0:48], convrow[0:48, 0, :], ident[0:48, 0:48]).then_inc(sem("cw_tr"), 1)
                unit_in(l, 3)
                pe.wait_ge(sem("cw_ready"), at(l, "cw_ready", 1))
                for t in range(T):
                    for k in range(KT):
                        last = mm(ps[2][:, 8 * t:8 * t + 8], xT[:, k, t * P:(t + 1) * P], slot(3, 512)[:, k, 0:8], start=(k == 0), stop=(k == KT - 1))
                last.then_inc(sem("ab_mm"), 1)
                unit_in(l, 4)
                for i in (6, 7):
                    tokens(4, i % 2, IN_BANKS[i]).then_inc(sem("proj"), 1)
                pe.wait_ge(sem("sq"), at(l, "sq", 4))
                for qk in range(2):
                    for n in range(8):
                        t, h = n // 4, n % 4
                        c = 4 * (1 - qk) + h
                        last = mm(ps[3][:, 8 * qk + n:8 * qk + n + 1], l2[:, c // 2, (c % 2) * S + t * P:(c % 2) * S + (t + 1) * P], ones[:, 0:1], start=True, stop=True)
                last.then_inc(sem("ss_mm"), 1)
                unit_in(l, 5)
                for i in (8, 9):
                    pe.wait_ge(sem("taps"), at(l, "taps", i - 5))
                    channels(5, 2 * (i % 2), IN_BANKS[i]).then_inc(sem("proj"), 1)
                pe.wait_ge(sem("act_evac"), at(l, "act_evac", 2))
                for t in range(T):
                    for h in range(H):
                        last = tr(ps[6 + t][:, h * P:(h + 1) * P], qkv[:, 4 + h, t * P:(t + 1) * P], ident)
                    last.then_inc(sem("rows_tr"), 1)
                pe.wait_ge(sem("const_in"), 16)
                pe.wait_ge(sem("g_ready"), at(l, "g_ready", 1))
                pe.wait_ge(sem("act_evac"), at(l, "act_evac", 4))
                mm(ps[5][:, 0:8], C("cum"), g.rearrange("p x y -> p (x y)"), start=True, stop=True)
                mm(ps[5][:, 8:24], ones, gm.rearrange("p x y -> p (x y)"), start=True, stop=True)
                for t in range(T):
                    for qk in range(2):
                        for h in range(H):
                            o_ = ps[t + 2 * (1 - qk)][:, h * P:(h + 1) * P]
                            mm(o_, gb[:, 4 * t + h, :], C("cum"), start=True, stop=False)
                            last = mm(o_, lnb[:, 8 * qk + 4 * t + h, :], ident, start=False, stop=True)
                last.then_inc(sem("cum_mm"), 1)
                pe.wait_ge(sem("cum_read"), at(l, "cum_read", 1))
                for t in range(T):
                    for h in range(H):
                        last = tr(ps[4 + t][:, h * P:(h + 1) * P], qkv[:, 8 + h, t * P:(t + 1) * P], ident)
                    last.then_inc(sem("rows_tr"), 1)
                pe.wait_ge(sem("egb_read"), at(l, "egb_read", 1))
                for n in range(8):
                    t, h = n // 4, n % 4
                    kk = qkv[:, 4 + h, t * P:(t + 1) * P]
                    mm(ps[t][:, h * P:(h + 1) * P], kk, kk, start=True, stop=True)
                    last = mm(ps[2 + t][:, h * P:(h + 1) * P], kk, qkv[:, h, t * P:(t + 1) * P], start=True, stop=True)
                last.then_inc(sem("kk_mm"), 1)
                pe.wait_ge(sem("rows_a"), at(l, "rows_a", 1))
                pe.wait_ge(sem("rows_v"), at(l, "rows_v", 1))
                for lv in range(6):
                    for t in range(T):
                        n = 2 * lv + t
                        pe.wait_ge(sem("lvl"), at(l, "lvl", n + 1))
                        pe.wait_ge(sem("e_ready"), at(l, "e_ready", n - 1)) if lv else None
                        for h in range(H):
                            last = mm(ps[4 + t][:, h * P:(h + 1) * P], Lm[:, 4 * t + h, :], Em[:, 4 * t + h, :] if lv else ident, start=True, stop=True)
                        last.then_inc(sem("x_mm"), 1)
                    for t in range(T):
                        n = 2 * lv + t
                        pe.wait_ge(sem("x_evac"), at(l, "x_evac", n + 1))
                        for h in range(H):
                            last = mm(ps[6 + t][:, h * P:(h + 1) * P], Dm[:, 4 * t + h, :] if lv else ident, Xm[:, 4 * t + h, :], start=True, stop=True)
                        for h in range(H):
                            if lv < 5:
                                last = mm(ps[t][:, h * P:(h + 1) * P], Xm[:, 4 * t + h, :], Dm[:, 4 * t + h, :] if lv else ident, start=True, stop=True)
                        last.then_inc(sem("ed_mm"), 1)
                for t in range(T):
                    pe.wait_ge(sem("e_ready"), at(l, "e_ready", 11 + t))
                    for h in range(H):
                        n = 4 * t + h
                        mm(ps[2 + t][:, h * P:(h + 1) * P], Em[:, n, :], bv[:, n, :], start=True, stop=True)
                        last = mm(ps[4 + t][:, h * P:(h + 1) * P], bk[:, n, :], Em[:, n, :], start=True, stop=True)
                    last.then_inc(sem("sol_mm"), 1)
                def fill(i):
                    if i == 0:
                        pe.wait_ge(sem("w_ready2"), at(l, "w_ready2", 1))
                    if i == 2:
                        pe.wait_ge(sem("vnew"), at(l, "vnew", 1))
                    if i % 2 == 0:
                        unit_in(l, 6 + i // 2)
                    last = channels(6, 2 * i, 4 + i) if i < 2 else tokens(7, i - 2, i)
                    last.then_inc(sem("proj"), 1)

                fill(0)
                pe.wait_ge(sem("qdec"), at(l, "qdec", 1))
                for c in range(S // CHUNK):
                    t, lo = c // 2, CHUNK * (c % 2)
                    rows_ = slice(lo, lo + CHUNK)
                    if c:
                        pe.wait_ge(sem("state"), at(l, "state", c))
                        for h in range(H):
                            last = mm(ps[6][rows_, h * P:(h + 1) * P], wT[:, 4 * t + h, rows_], state[:, h, :], start=True, stop=True)
                        last.then_inc(sem("pv_mm"), 1)
                        fill(c)
                    pe.wait_ge(sem("vnew"), at(l, "vnew", c + 1))
                    if c < 3:
                        for h in range(H):
                            last = mm(ps[1][:, h * P:(h + 1) * P], kdec[rows_, 4 * t + h, :], vnew[rows_, 4 * t + h, :], start=True, stop=True)
                        last.then_inc(sem("st_mm"), 1)
                    for h in range(H):
                        o_ = ps[7 * (1 - t)][rows_, h * P:(h + 1) * P]
                        if c:
                            mm(o_, qkv[:, h, c * CHUNK:(c + 1) * CHUNK], state[:, h, :], start=True, stop=False)
                        last = mm(o_, attT[rows_, 4 * t + h, rows_], vnew[rows_, 4 * t + h, :], start=(c == 0), stop=True)
                    last.then_inc(sem("o_step"), 1)
                pe.wait_ge(sem("act_evac"), at(l, "act_evac", 6))
                for i in range(4):
                    src = (qbT, qbT, kbT, kbT)[i][:, 2 * (i % 2):2 * (i % 2) + 2, :].rearrange("p x y -> p (x y)")
                    mm(ps[ROT_BANKS[i]][:, :], C("rot"), src, start=True, stop=True).then_inc(sem("rot_mm"), 1)
                pe.wait_ge(sem("act_evac"), at(l, "act_evac", 8))
                pe.wait_ge(sem("rotated"), at(l, "rotated", 4))

                def outputs_transposed():
                    for t in range(T):
                        pe.wait_ge(sem("o_rows"), at(l, "o_rows", t + 1))
                        for h in range(H):
                            last = tr(ps[ROT_BANKS[t]][:, h * P:(h + 1) * P], uu[:, 4 * t + h, :], ident)
                        last.then_inc(sem("o_tr"), 1)
                    pe.wait_ge(sem("mix_o"), at(l, "mix_o", 2))

                attention(l, LAYER_PAIRS, outputs_transposed)
                rows_product(l, mixT, U_OUT, [4, 4], lambda k: k >= 4 and pe.wait_ge(sem("at_out"), at(l, "at_out", k - 3)),
                             lambda: first_tile(at(l, "x_rows", 3)))
                def up(j, t=None):
                    return channels(U_UP + j // 2, j % 2, UP_BANKS[j % 4], t=t, step=2)

                pe.wait_ge(sem("x0T"), at(l, "x0T", 2))
                for j in range(AHEAD):
                    if j % 2 == 0:
                        unit_in(l, U_UP + j // 2)
                    up(j, 0)
                second_tile(l, 1)
                for j in range(AHEAD):
                    up(j, 1).then_inc(sem("up"), 1)
                for j in range(AHEAD, FT):
                    if j % 2 == 0:
                        unit_in(l, U_UP + j // 2)
                    if j >= 4:
                        pe.wait_ge(sem("up_dve"), at(l, "up_dve", j - 3))
                    up(j).then_inc(sem("up"), 1)
                rows_product(l, hidT, U_DOWN, DOWN_TILES, lambda k: pe.wait_ge(sem("hid"), at(l, "hid", k + 1)),
                             lambda: first_tile(at(l, "x_rows", 5)))
            if stop_a:
                return
            L = DEPTH
            pe.wait_ge(sem("h1_rows"), 1)
            transpose_x(hrows, 0, "x0_tr")
            pe.wait_ge(sem("x0T"), at(L, "x0T", 2))
            for n in range(AHEAD):
                if n % 2 == 0:
                    unit_in(L, n // 2)
                channels(n // 2, 2 * (n % 2), UP_BANKS[n % 4], t=0)
            pe.wait_ge(sem("h1_rows"), 2)
            transpose_x(hrows, 1, "x1_tr")
            pe.wait_ge(sem("x1T"), at(L, "x1T", 2))
            pe.wait_ge(sem("bias_in"), 48)
            mm(ps[3][0:BIAS_HEADS, :], brel[0:BUCKETS + 1, :], btab[0:BUCKETS + 1, :], start=True, stop=True).then_inc(sem("bias_mm"), 1)
            for n in range(12):
                u, i = n // 2, n % 2
                if n < AHEAD:
                    last = channels(u, 2 * i, UP_BANKS[n % 4], t=1)
                else:
                    if i == 0:
                        unit_in(L, u)
                    if n >= 4:
                        pe.wait_ge(sem("b_evac"), n - 3)
                    last = tokens(u, i, UP_BANKS[n % 4]) if u in (2, 5) else channels(u, 2 * i, UP_BANKS[n % 4])
                last.then_inc(sem("b_proj"), 1)
            pe.wait_ge(sem("b_evac"), 12)
            pe.wait_ge(sem("bias_sb"), 1)
            attention(L, SECOND_PAIRS)
            pe.wait_ge(sem("oa_rows"), 4)
            for t in range(T):
                for h in range(H):
                    last = tr(ps[2 + t][:, h * P:(h + 1) * P], oa[:, t, h * P:(h + 1) * P], ident)
            last.then_inc(sem("oa_tr"), 1)
            pe.wait_ge(sem("oa_mix"), 2)
            rows_product(L, mixT, 6, [4, 4], lambda k: k >= 4 and pe.wait_ge(sem("at_out"), at(L, "at_out", k - 3)))
            for t in range(T):
                pe.wait_ge(sem("h2_rows"), t + 1)
                for kh in range(2):
                    for k in range(4):
                        last = tr(ps[H2_BANKS[2 * t + kh]][:, k * P:(k + 1) * P], hrows[:, t, (4 * kh + k) * P:(4 * kh + k + 1) * P], ident)
                    last.then_inc(sem("h2_tr"), 1)
            pe.wait_ge(sem("h2T"), 4)
            for t in range(T):
                for k in range(KT):
                    last = mm(ps[2][:, NE * t:NE * (t + 1)], xT[:, k, t * P:(t + 1) * P], wr[:, k, :], start=(k == 0), stop=(k == KT - 1))
            last.then_inc(sem("logits"), 1)
            pe.wait_ge(sem("aff"), 1)
            for t in range(T):
                last = tr(ps[3][0:NE, t * P:(t + 1) * P], rl[:, t, :], ident)
            last.then_inc(sem("aff_tr"), 1)
            pe.wait_ge(sem("chosen"), 1)
            mm(ps[6][:, :], ones[0:NE, :], spread, start=True, stop=True)
            mm(ps[7][:, 0:NE], rep[:, 0:P], ident[0:NE, 0:NE], start=True, stop=True)
            mm(ps[7][:, NE:2 * NE], rep[:, P:2 * P], ident[0:NE, 0:NE], start=True, stop=True).then_inc(sem("spread_mm"), 1)
            pe.wait_ge(sem("onehot"), 1)
            for k in range(KT):
                for t in range(T):
                    last = mm(ps[4 + k // 4][:, (k % 4) * P:(k % 4 + 1) * P], hrows[:, t, k * P:(k + 1) * P], oneT[:, t, 0:FIRST], start=(t == 0), stop=(t == T - 1))
                if k % 4 == 3:
                    last.then_inc(sem("xe_mm"), 1)

            def other_experts_tokens():
                pe.wait_ge(sem("xe_evac"), 2)
                for k in range(KT):
                    if k >= 4:
                        pe.wait_ge(sem("xe_evac"), 2 + k - 3)
                    for t in range(T):
                        last = mm(ps[XE_BANKS[k % 4]][:, 0:NE * CAP - FIRST], hrows[:, t, k * P:(k + 1) * P], oneT[:, t, FIRST:NE * CAP], start=(t == 0), stop=(t == T - 1))
                    last.then_inc(sem("xe_mm"), 1)

            def expert(e, between=None):
                pe.wait_ge(sem("xe_ready"), e + 1)
                for k in range(KT):
                    if k == GU_RING and between:
                        between()
                    s_ = k % GU_RING
                    pe.wait_ge(sem(f"gu_in{s_}"), e * (KT // GU_RING * 32) + 32 * (k // GU_RING + 1))
                    for b, (c0, n) in enumerate(PIECES):
                        for q in range(4):
                            c = (q % 2) * HALF + c0
                            last = mm(ps[b][32 * q:32 * q + 32, 0:n], xe[:, k, :], gu[:, s_, q // 2, c:c + n], start=(k == 0), stop=(k == KT - 1))
                    last.then_inc(sem("gu_free"), 1)
                if between:
                    pe.wait_ge(sem("xe_evac"), 2 + KT)
                for b, (c0, n) in enumerate(PIECES):
                    pe.wait_ge(sem("eh"), e * 3 + b + 1)
                    for m in (2 * b, 2 * b + 1):
                        last = tr(ps[HID_BANKS[b]][:, (m % 2) * P:(m % 2 + 1) * P], hh[:, m, :], ident)
                    last.then_inc(sem("eh_tr"), 1)
                for k in range(FT):
                    pe.wait_ge(sem("ehT"), e * 3 + (k // 4 + 1 if k < HT else 3))
                    pe.wait_ge(sem(f"d_in{k % D_RING}"), e * (FT // D_RING * 16) + 16 * (k // D_RING + 1))
                    for q in range(4):
                        last = mm(ps[5][32 * q:32 * q + 32, 0:256], hT[:, k % HT, 32 * (k // HT):32 * (k // HT) + 32], dring[:, k % D_RING, 256 * q:256 * q + 256],
                                  start=(k == 0), stop=(k == FT - 1))
                    last.then_inc(sem("d_free"), 1)
                pe.wait_ge(sem("ey"), e + 1)
                for t in range(T):
                    for q in range(4):
                        last = mm(ps[OUT_BANKS[q]][:, t * 256:(t + 1) * 256], pg[32 * q:32 * q + 32, t * P:(t + 1) * P],
                                  yq[32 * q:32 * q + 32, :], start=True, stop=True)
                last.then_inc(sem("eo_mm"), 1)

            expert(0, other_experts_tokens)
            with pe.Fori(1, NE) as e:
                expert(e)

        @block.scalar
        def _(act):
            f = nc.scalar.activation

            def copy_x1T(l, n):
                act.wait_ge(sem("x1_tr"), at(l, "x1_tr", 2 * n + 2))
                f(xT[:, 4:8, P:2 * P], ps[7][:, :].rearrange("p (x y) -> p x y", y=P), ACT.Copy).then_inc(sem("x1T"), 1)

            def attention(l, pairs, before_transposes=None):
                n = 2 * len(pairs)
                for i in range(n + 5):
                    if i < n:
                        E = attention_operands(pairs[i // 2][0])[3]
                        act.wait_ge(sem("at_read"), at(l, "at_read", i + 1))
                        for m in range(2):
                            last = f(E[:, i % 4, m, :], E[:, i % 4, m, :], ACT.Exp, bias=mx[:, i % 4, m:m + 1], accum_out=sm[:, i % 4, m:m + 1])
                        last.then_inc(sem("at_exp"), 1)
                    if i == 2 and before_transposes:
                        before_transposes()
                    if 2 <= i < n + 2:
                        b = i - 2
                        kind, pr = pairs[b // 2]
                        PT = attention_operands(kind)[4]
                        act.wait_ge(sem("at_tr"), at(l, "at_tr", b + 1))
                        if b // 2 >= 2:
                            act.wait_ge(sem("at_pv"), at(l, "at_pv", b // 2 - 1))
                        w = 2 if kind == "diff" else 4
                        f(PT[:, b // 2 % 2, 0:w, (b % 2) * P:(b % 2 + 1) * P],
                          ps[TR[b % 2]][:, 0:w * P].rearrange("p (x y) -> p x y", y=P), ACT.Copy).then_inc(sem("at_pt"), 1)
                    if i >= 6 and i % 2 == 0:
                        pi = (i - 6) // 2
                        kind, pr = pairs[pi]
                        if kind != "diff":
                            act.wait_ge(sem("at_pv"), at(l, "at_pv", pi + 1))
                            f(mixT[:, 4 + pr, :], ps[PV[pi % 2]][:, 0:S], ACT.Copy).then_inc(sem("at_out"), 1)

            with act.Fori(0, DEPTH) as l:
                copy_x1T(l, 0)
                act.wait_ge(sem("cw_ready"), at(l, "cw_ready", 1))
                for i in range(7):
                    if i < 6:
                        act.wait_ge(sem("proj"), at(l, "proj", i + 1))
                        for j in range(2):
                            c = 2 * i + j
                            last = f(qkv[:, c, :], ps[IN_BANKS[i]][:, j * S:(j + 1) * S], ACT.Copy, scale=cw[:, 36 + c:37 + c])
                        last.then_inc(sem("tap"), 1)
                    if i:
                        act.wait_ge(sem("taps"), at(l, "taps", i))
                        v = qkv[:, 2 * i - 2:2 * i, :]
                        f(v, v, ACT.Silu).then_inc(sem("silu"), 1)
                for i in range(4):
                    act.wait_ge(sem("silu"), at(l, "silu", i + 1))
                    f(l2[:, i, :], qkv[:, 2 * i:2 * i + 2, :].rearrange("p x y -> p (x y)"), ACT.Square).then_inc(sem("sq"), 1)
                for i in (6, 7):
                    act.wait_ge(sem("proj"), at(l, "proj", i + 1))
                    f(zg[:, i % 2, :], ps[IN_BANKS[i]][:, :], ACT.Silu).then_inc(sem("act_evac"), 1)
                act.wait_ge(sem("ab_pre"), at(l, "ab_pre", 1))
                act.wait_ge(sem("small"), l * 48 + 48)
                f(eb, br, ACT.Exp, scale=-1.0)
                f(ea, nab, ACT.Exp)
                f(eal, alog, ACT.Exp)
                act.drain()
                f(el, ea, ACT.Ln, bias=1.0).then_inc(sem("ab_act"), 1)
                act.wait_ge(sem("ss_sum"), at(l, "ss_sum", 1))
                f(lnh, ss, ACT.Ln).then_inc(sem("ss_ln"), 1)
                for i in (8, 9):
                    act.wait_ge(sem("proj"), at(l, "proj", i + 1))
                    f(qbT[:, 2 * (i % 2):2 * (i % 2) + 2, :].rearrange("p x y -> p (x y)"), ps[IN_BANKS[i]][:, :], ACT.Copy).then_inc(sem("act_evac"), 1)
                act.wait_ge(sem("arg_ready"), at(l, "arg_ready", 1))
                for t in range(T):
                    last = f(egb[:, 4 * t:4 * t + 4, :].rearrange("p x y -> p (x y)"), ps[t][:, :], ACT.Exp)
                last.then_inc(sem("egb_read"), 1)
                f(egc, gcol, ACT.Exp)
                f(etot, tot, ACT.Exp)
                f(ekd, gl, ACT.Exp).then_inc(sem("dec_cols"), 1)
                for n in range(8):
                    f(decS[:, n, :], decS[:, n, :], ACT.Exp, bias=gcol[:, n:n + 1])
                for n in range(8):
                    last = f(decT[:, n, :], decT[:, n, :], ACT.Exp, bias=ngcol[:, n:n + 1])
                last.then_inc(sem("dec"), 1)
                act.wait_ge(sem("g_ready"), at(l, "g_ready", 1))
                for t in range(T):
                    act.wait_ge(sem("rows_tr"), at(l, "rows_tr", t + 3))
                    for h in range(H):
                        last = f(bv[:, 4 * t + h, :], ps[4 + t][:, h * P:(h + 1) * P], ACT.Copy, scale=beta[:, t, h:h + 1])
                last.then_inc(sem("rows_a"), 1)
                for lv in range(6):
                    for t in range(T):
                        n = 2 * lv + t
                        act.wait_ge(sem("x_mm"), at(l, "x_mm", n + 1))
                        f(Xm[:, 4 * t:4 * t + 4, :].rearrange("p x y -> p (x y)"), ps[4 + t][:, :], ACT.Copy).then_inc(sem("x_evac"), 1)
                for t in range(T):
                    act.wait_ge(sem("sol_mm"), at(l, "sol_mm", t + 1))
                    last = f(wT[:, 4 * t:4 * t + 4, :].rearrange("p x y -> p (x y)"), ps[4 + t][:, :], ACT.Copy)
                last.then_inc(sem("w_ready2"), 1)
                for i in (10, 11):
                    act.wait_ge(sem("proj"), at(l, "proj", i + 1))
                    f(kbT[:, 2 * (i % 2):2 * (i % 2) + 2, :].rearrange("p x y -> p (x y)"), ps[4 + i % 2][:, :], ACT.Copy).then_inc(sem("act_evac"), 1)
                for t in range(T):
                    act.wait_ge(sem("o_step"), at(l, "o_step", 2 * t + 2))
                    for h in range(H):
                        n = 4 * t + h
                        f(Xm[:, n, :], ps[7 * (1 - t)][:, h * P:(h + 1) * P], ACT.Square, accum_out=o_ss[:, n:n + 1])
                    act.drain()
                    f(o_rs[:, 4 * t:4 * t + 4], o_ss[:, 4 * t:4 * t + 4], ACT.Sqrt, scale=1.0 / DK, bias=norm_eps).then_inc(sem("o_rs"), 1)
                    if t == 0:
                        for i in (12, 13):
                            act.wait_ge(sem("proj"), at(l, "proj", i + 1))
                            f(vb[:, i % 2, :], ps[2 + i % 2][:, :], ACT.Copy).then_inc(sem("act_evac"), 1)

                def outputs_copied():
                    for t in range(T):
                        act.wait_ge(sem("o_tr"), at(l, "o_tr", t + 1))
                        f(mixT[:, 0:4, t * P:(t + 1) * P], ps[ROT_BANKS[t]][:, :].rearrange("p (x y) -> p x y", y=P), ACT.Copy).then_inc(sem("mix_o"), 1)
                attention(l, LAYER_PAIRS, outputs_copied)

                def layer_norm_root(n, t):
                    act.wait_ge(sem("y_stat"), at(l, "y_stat", 2 * n + t + 1))
                    f(rs[:, t, :], mv[:, t, 1:2], ACT.Sqrt, bias=ln_eps).then_inc(sem("y_rs"), 1)
                for t in range(T):
                    layer_norm_root(0, t)
                copy_x1T(l, 1)
                for j in range(FT + 1):
                    if j < FT:
                        act.wait_ge(sem("up"), at(l, "up", j + 1))
                        if j >= 3:
                            act.wait_ge(sem("hid"), at(l, "hid", j - 2))
                        for gv in range(2):
                            c = gv * FT + j
                            last = f(facc[:, j % 3, gv, :], ps[UP_BANKS[j % 4]][:, gv * S:(gv + 1) * S], ACT.Identity,
                                     scale=cw[:, 136 + c:137 + c], bias=cw[:, 180 + c:181 + c])
                        last.then_inc(sem("up_act"), 1)
                    if j:
                        act.wait_ge(sem("up_dve"), at(l, "up_dve", j))
                        f(facc[:, (j - 1) % 3, 0, :], facc[:, (j - 1) % 3, 0, :], ACT.Silu).then_inc(sem("up_silu"), 1)
                for t in range(T):
                    layer_norm_root(1, t)
            if stop_a:
                return
            L = DEPTH
            def rms(n, t):
                if n == 0:
                    act.wait_ge(sem("x_rows"), at(L, "x_rows", t + 1))
                else:
                    act.wait_ge(sem("r_in"), 2 * (n - 1) + t + 1)
                squares = (xT if (n, t) == (1, 0) else mixT).rearrange("p x y -> p (x y)")[:, 0:D]
                f(squares, x[:, t, :], ACT.Square, accum_out=ssq[:, t:t + 1])
                act.drain()
                f(rsb[:, t:t + 1], ssq[:, t:t + 1], ACT.Sqrt, scale=1.0 / D, bias=norm_eps).then_inc(sem("r_rs"), 1)
            for t in range(T):
                rms(0, t)
            copy_x1T(L, 0)
            n = 0
            for u in range(6):
                dst = (qaT, kaT, va, qdT, kdT, vd)[u]
                for i in range(2):
                    act.wait_ge(sem("b_proj"), n + 1)
                    d_ = dst[:, i, :] if u in (2, 5) else dst[:, 2 * i:2 * i + 2, :].rearrange("p x y -> p (x y)")
                    f(d_, ps[UP_BANKS[n % 4]][:, :], ACT.Copy).then_inc(sem("b_evac"), 1)
                    n += 1
            act.wait_ge(sem("lam_dot"), 1)
            f(lame[:, 2:4], lame[:, 0:2], ACT.Exp).then_inc(sem("lam_exp"), 1)
            attention(L, SECOND_PAIRS)
            act.wait_ge(sem("oa_sum"), 1)
            f(lame, lame, ACT.Sqrt, scale=1.0 / P, bias=subln_eps).then_inc(sem("oa_rs"), 1)
            for t in range(T):
                act.wait_ge(sem("oa_tr"), 1)
                f(mixT[:, 0:4, t * P:(t + 1) * P], ps[2 + t][:, :].rearrange("p (x y) -> p x y", y=P), ACT.Copy).then_inc(sem("oa_mix"), 1)
            for t in range(T):
                rms(1, t)
            for t in range(T):
                for kh in range(2):
                    act.wait_ge(sem("h2_tr"), 2 * t + kh + 1)
                    f(xT[:, 4 * kh:4 * kh + 4, t * P:(t + 1) * P], ps[H2_BANKS[2 * t + kh]][:, :].rearrange("p (x y) -> p x y", y=P), ACT.Copy).then_inc(sem("h2T"), 1)
            act.wait_ge(sem("rl_ready"), 1)
            for t in range(T):
                last = f(rl[:, t, :], rl[:, t, :], ACT.Exp, bias=rmax[:, t:t + 1], accum_out=rsum[:, t:t + 1])
            last.then_inc(sem("rl_exp"), 1)
            for i in range(2):
                act.wait_ge(sem("xe_mm"), i + 1)
                f(xeT[:, 4 * i:4 * i + 4, 0:FIRST], ps[4 + i][:, :].rearrange("p (x y) -> p x y", y=P), ACT.Copy).then_inc(sem("xe_evac"), 1)
            for k in range(KT):
                act.wait_ge(sem("xe_mm"), 2 + k + 1)
                f(xeT[:, k, FIRST:NE * CAP], ps[XE_BANKS[k % 4]][:, 0:NE * CAP - FIRST], ACT.Copy).then_inc(sem("xe_evac"), 1)
            with act.Fori(0, NE) as e:
                for b, (c0, n) in enumerate(PIECES):
                    act.wait_ge(sem("gu_free"), GU_RING + e * KT + KT)
                    f(sg[0:64, c0:c0 + n], ps[b][0:64, 0:n], ACT.Silu).then_inc(sem("esg"), 1)
                for b, (c0, n) in enumerate(PIECES):
                    act.wait_ge(sem("eh_tr"), e * 3 + b + 1)
                    last = f(hT[:, 4 * b:4 * b + 4, :], ps[HID_BANKS[b]][:, 0:S].rearrange("p (x y) -> p x y", y=64), ACT.Copy)
                    last.then_inc(sem("ehT"), 1)
                act.wait_ge(sem("d_free"), e * FT + FT + D_RING)
                f(yq, ps[5][:, 0:256], ACT.Copy).then_inc(sem("ey"), 1)
            for t in range(T):
                rms(2, t)

        @block.vector
        def _(v):
            w = nc.vector

            def attention(l, pairs):
                n = 2 * len(pairs)
                for i in range(n + 5):
                    if i < n:
                        kind, pr = pairs[i // 2]
                        E, t = attention_operands(kind)[3], i % 2
                        v.wait_ge(sem("at_s"), at(l, "at_s", i + 1))
                        if i >= 4:
                            v.wait_ge(sem("at_tr"), at(l, "at_tr", i - 3))
                        for m in range(2):
                            if kind == "causal":
                                bias = C("causal")
                            else:
                                bias = bias12[:, pr if kind == "diff" else H + 2 * pr + m, :]
                            w.scalar_tensor_tensor(E[:, i % 4, m, :], ps[SC[i % 2][m]][:, 0:S], DH ** -0.5, bias[:, P - P * t:P - P * t + S], ALU.mult, ALU.add)
                        v.drain()
                        w.tensor_reduce(mx[:, i % 4, :], E[:, i % 4, :, :], AX.X, ALU.max, negate=True).then_inc(sem("at_read"), 1)
                    if 1 <= i <= n:
                        b = i - 1
                        kind, pr = pairs[b // 2]
                        E = attention_operands(kind)[3]
                        v.wait_ge(sem("at_exp"), at(l, "at_exp", b + 1))
                        w.reciprocal(rc[:, b % 4, :], sm[:, b % 4, :])
                        v.drain()
                        if kind == "diff":
                            w.tensor_scalar(rc[:, b % 4, 1:2], rc[:, b % 4, 1:2], neglam, None, ALU.mult)
                            v.drain()
                            w.tensor_scalar(E[:, b % 4, 1, :], E[:, b % 4, 1, :], rc[:, b % 4, 1:2], None, ALU.mult)
                            v.drain()
                            w.scalar_tensor_tensor(E[:, b % 4, 0, :], E[:, b % 4, 0, :], rc[:, b % 4, 0:1], E[:, b % 4, 1, :], ALU.mult, ALU.add).then_inc(sem("at_prob"), 1)
                        else:
                            for m in range(2):
                                last = w.tensor_scalar(E[:, b % 4, m, :], E[:, b % 4, m, :], rc[:, b % 4, m:m + 1], None, ALU.mult)
                            last.then_inc(sem("at_prob"), 1)
                    if i >= 6 and i % 2 == 0:
                        pi = (i - 6) // 2
                        kind, pr = pairs[pi]
                        if kind == "diff":
                            v.wait_ge(sem("at_pv"), at(l, "at_pv", pi + 1))
                            w.tensor_copy(oa[:, :, pr * P:(pr + 1) * P], ps[PV[pi % 2]][:, 0:S].rearrange("p (t n) -> p t n", n=P)).then_inc(sem("oa_read"), 1)

            v.wait_ge(sem("x_in"), 16)
            v.nop().then_inc(sem("x_rows"), 2)

            def copy_x0T(value):
                v.wait_ge(sem("x0_tr"), value)
                for kh in range(2):
                    last = w.tensor_copy(xT[:, 4 * kh:4 * kh + 4, 0:P], ps[4 + kh][:, :].rearrange("p (x y) -> p x y", y=P))
                last.then_inc(sem("x0T"), 1)

            def copy_x1T(l, n):
                v.wait_ge(sem("x1_tr"), at(l, "x1_tr", 2 * n + 1))
                w.tensor_copy(xT[:, 0:4, P:2 * P], ps[6][:, :].rearrange("p (x y) -> p x y", y=P)).then_inc(sem("x1T"), 1)

            def layer_norm(l, n):
                v.wait_ge(sem(("ln1", "ln2")[n]), l * 32 + 32)
                for t in range(T):
                    if t == 0:
                        v.wait_ge(sem("rows_t0"), at(l, "rows_t0", n + 1))
                    else:
                        v.wait_ge(sem("rows_used"), (l + 1) * ROW_UNITS + (ROW_UNITS if n else 2))
                    for nh in range(2):
                        xs = x[:, t, nh * 512:(nh + 1) * 512]
                        w.scalar_tensor_tensor(xs, xs, ALPHA, ps[ROWS_BANKS[2 * t + nh]][:, :], ALU.mult, ALU.add)
                    v.drain()
                    for nh in range(2):
                        w.bn_stats(st6[:, t, nh, :], x[:, t, nh * 512:(nh + 1) * 512])
                    v.drain()
                    w.bn_aggr(mv[:, t, :], st6[:, t, :, :]).then_inc(sem("y_stat"), 1)
                    v.drain()
                    w.scalar_tensor_tensor(x[:, t, :], x[:, t, :], mv[:, t, 0:1], ln_g, ALU.subtract, ALU.mult)
                    v.wait_ge(sem("y_rs"), at(l, "y_rs", 2 * n + t + 1))
                    w.reciprocal(rs[:, t, :], rs[:, t, :])
                    v.drain()
                    w.scalar_tensor_tensor(x[:, t, :], x[:, t, :], rs[:, t, :], ln_b, ALU.mult, ALU.add).then_inc(sem("x_rows"), 1)
                    if t == 0:
                        copy_x0T(at(l, "x0_tr", n + 2))

            copy_x0T(1)
            with v.Fori(0, DEPTH) as l:
                copy_x1T(l, 0)
                v.wait_ge(sem("cw_tr"), at(l, "cw_tr", 1))
                w.tensor_copy(cw, ps[2][:, 0:224]).then_inc(sem("cw_ready"), 1)
                v.drain()
                for i in range(6):
                    v.wait_ge(sem("tap"), at(l, "tap", i + 1))
                    for s in range(1, TAPS):
                        for j in range(2):
                            c = 2 * i + j
                            last = w.scalar_tensor_tensor(qkv[:, c, s:S], ps[IN_BANKS[i]][:, j * S:(j + 1) * S - s], cw[:, 12 * (3 - s) + c:12 * (3 - s) + c + 1],
                                                          qkv[:, c, s:S], ALU.mult, ALU.add)
                        if s < TAPS - 1:
                            v.drain()
                    last.then_inc(sem("taps"), 1)
                v.wait_ge(sem("const_in"), 16)
                v.wait_ge(sem("ab_mm"), at(l, "ab_mm", 1))
                v.wait_ge(sem("small"), l * 48 + 48)
                ab = ps[2][:, 0:16].rearrange("p (t n) -> p t n", n=8)
                w.tensor_add(ar, ab[:, :, 0:H], dtb.unsqueeze(1).broadcast_to([P, T, H]))
                w.tensor_copy(br, ab[:, :, H:2 * H])
                v.drain()
                w.tensor_scalar(nab, ar, -1.0, None, ALU.mult)
                v.drain()
                w.tensor_tensor(nab, nab, ar, ALU.min).then_inc(sem("ab_pre"), 1)
                v.wait_ge(sem("ss_mm"), at(l, "ss_mm", 1))
                w.tensor_scalar(ss[:, 0:8], ps[3][:, 0:8], NORM_EPS, None, ALU.add)
                w.tensor_scalar(ss[:, 8:16], ps[3][:, 8:16], NORM_EPS, DK, ALU.add, ALU.mult).then_inc(sem("ss_sum"), 1)
                v.wait_ge(sem("ab_act"), at(l, "ab_act", 1))
                w.scalar_tensor_tensor(g, ar, 0.0, el, ALU.max, ALU.add)
                w.tensor_scalar(beta, eb, 1.0, None, ALU.add)
                v.drain()
                w.scalar_tensor_tensor(g, g, -1.0, eal.unsqueeze(1).broadcast_to([P, T, H]), ALU.mult, ALU.mult)
                w.reciprocal(beta, beta)
                v.drain()
                w.tensor_copy(gb, g.rearrange("p x y -> p (x y)").unsqueeze(2).broadcast_to([P, 8, P]))
                for c in range(2):
                    w.tensor_scalar(gm[:, c, :], g.rearrange("p x y -> p (x y)"), C("cum")[:, CHUNK * c + CHUNK - 1:CHUNK * c + CHUNK], None, ALU.mult)
                v.wait_ge(sem("ss_ln"), at(l, "ss_ln", 1))
                w.tensor_scalar(lnh[:, 0:8], lnh[:, 0:8], 0.5, None, ALU.mult)
                w.tensor_scalar(lnh[:, 8:16], lnh[:, 8:16], -0.5, None, ALU.mult)
                v.drain()
                w.tensor_copy(lnb, lnh.unsqueeze(2).broadcast_to([P, 16, P])).then_inc(sem("g_ready"), 1)
                v.wait_ge(sem("cum_mm"), at(l, "cum_mm", 1))
                w.tensor_sub(gcol, ps[5][:, 0:8], lnh[:, 0:8])
                w.scalar_tensor_tensor(ngcol, ps[5][:, 0:8], -1.0, lnh[:, 0:8], ALU.mult, ALU.subtract)
                w.tensor_copy(tot, ps[5][:, 8:24])
                v.drain()
                for c in range(2):
                    lo = CHUNK * c
                    w.tensor_add(gl[lo:lo + CHUNK, :], tot[lo:lo + CHUNK, 8 * c:8 * c + 8], ngcol[lo:lo + CHUNK, :])
                for t in range(T):
                    bias = lambda name: C(name).unsqueeze(1).broadcast_to([P, H, P])
                    w.scalar_tensor_tensor(decS[:, 4 * t:4 * t + 4, :], ps[2 + t][:, :].rearrange("p (h n) -> p h n", n=P), -1.0, bias("neg_strict"), ALU.mult, ALU.add)
                    w.tensor_add(decT[:, 4 * t:4 * t + 4, :], ps[t][:, :].rearrange("p (h n) -> p h n", n=P), bias("neg_incl_t"))
                v.drain().then_inc(sem("arg_ready"), 1)
                v.nop().then_inc(sem("cum_read"), 1)
                v.wait_ge(sem("dec_cols"), at(l, "dec_cols", 1))
                w.tensor_mul(beg, beta.rearrange("p x y -> p (x y)"), egc)
                v.drain()
                for n in range(8):
                    t, h = n // 4, n % 4
                    if h == 0:
                        v.wait_ge(sem("rows_tr"), at(l, "rows_tr", t + 1))
                    w.tensor_scalar(kdec[:, n, :], ps[6 + t][:, h * P:(h + 1) * P], ekd[:, n:n + 1], None, ALU.mult)
                    last = w.tensor_scalar(bk[:, n, :], ps[6 + t][:, h * P:(h + 1) * P], beg[:, n:n + 1], None, ALU.mult)
                last.then_inc(sem("rows_v"), 1)
                v.wait_ge(sem("dec"), at(l, "dec", 1))
                v.wait_ge(sem("kk_mm"), at(l, "kk_mm", 1))
                for n in range(8):
                    t, h = n // 4, n % 4
                    w.scalar_tensor_tensor(Am[:, n, :], ps[t][:, h * P:(h + 1) * P], beta[:, t, h:h + 1], decS[:, n, :], ALU.mult, ALU.mult)
                for t in range(T):
                    dt_ = decT[:, 4 * t:4 * t + 4, :].rearrange("p x y -> p (x y)")
                    w.tensor_mul(dt_, ps[2 + t][:, :], dt_)
                v.drain()

                def level(lv, t):
                    w.tensor_mul(Lm[:, 4 * t:4 * t + 4, :], Am[:, 4 * t:4 * t + 4, :], C(f"level{lv}").unsqueeze(1).broadcast_to([P, H, P])).then_inc(sem("lvl"), 1)
                for t in range(T):
                    level(0, t)
                for lv in range(6):
                    for t in range(T):
                        n = 2 * lv + t
                        es, ds_ = Em[:, 4 * t:4 * t + 4, :], Dm[:, 4 * t:4 * t + 4, :]
                        idb = ident.unsqueeze(1).broadcast_to([P, H, P])
                        if lv < 5:
                            v.wait_ge(sem("x_mm"), at(l, "x_mm", n + 1))
                            level(lv + 1, t)
                        v.wait_ge(sem("ed_mm"), at(l, "ed_mm", n + 1))
                        last = w.tensor_sub(es, es if lv else idb, ps[6 + t][:, :].rearrange("p (h n) -> p h n", n=P))
                        if lv < 5:
                            last = w.tensor_sub(ds_, ds_ if lv else idb, ps[t][:, :].rearrange("p (h n) -> p h n", n=P))
                        last.then_inc(sem("e_ready"), 1)
                for t in range(T):
                    v.wait_ge(sem("sol_mm"), at(l, "sol_mm", t + 1))
                    last = w.tensor_copy(uu[:, 4 * t:4 * t + 4, :].rearrange("p x y -> p (x y)"), ps[2 + t][:, :])
                v.drain()
                for c in range(S // CHUNK):
                    t, lo = c // 2, CHUNK * (c % 2)
                    rows_ = slice(lo, lo + CHUNK)
                    if c == 0:
                        v.nop().then_inc(sem("vnew"), 1)
                    else:
                        v.wait_ge(sem("pv_mm"), at(l, "pv_mm", c))
                        vv = vnew[rows_, 4 * t:4 * t + 4, :].rearrange("p x y -> p (x y)")
                        w.tensor_sub(vv, vv, ps[6][rows_, :]).then_inc(sem("vnew"), 1)
                    if c < 3:
                        v.wait_ge(sem("st_mm"), at(l, "st_mm", c + 1))
                        if c:
                            v.wait_ge(sem("o_step"), at(l, "o_step", c + 1))
                            for h in range(H):
                                last = w.scalar_tensor_tensor(state[:, h, :], state[:, h, :], etot[:, 8 * (c % 2) + 4 * t + h:8 * (c % 2) + 4 * t + h + 1],
                                                              ps[1][:, h * P:(h + 1) * P], ALU.mult, ALU.add)
                        else:
                            last = w.tensor_copy(state.rearrange("p x y -> p (x y)"), ps[1][:, :])
                        last.then_inc(sem("state"), 1)
                        v.drain()
                def outputs(t):
                    v.wait_ge(sem("o_rs"), at(l, "o_rs", t + 1))
                    w.reciprocal(o_rs[:, 4 * t:4 * t + 4], o_rs[:, 4 * t:4 * t + 4])
                    v.drain()
                    for h in range(H):
                        last = w.scalar_tensor_tensor(uu[:, 4 * t + h, :], ps[7 * (1 - t)][:, h * P:(h + 1) * P], o_rs[:, 4 * t + h:4 * t + h + 1],
                                                      zg[:, t, h * P:(h + 1) * P], ALU.mult, ALU.mult)
                    last.then_inc(sem("o_rows"), 1)

                v.wait_ge(sem("zg"), at(l, "zg", 1))
                outputs(0)
                for i in range(4):
                    v.wait_ge(sem("rot_mm"), at(l, "rot_mm", i + 1))
                    src = (qbT, qbT, kbT, kbT)[i][:, 2 * (i % 2):2 * (i % 2) + 2, :]
                    r3 = rtmp.rearrange("p (x y) -> p x y", y=S)
                    w.tensor_mul(r3, ps[ROT_BANKS[i]][:, :].rearrange("p (x y) -> p x y", y=S), C("sin").unsqueeze(1).broadcast_to([P, 2, S]))
                    w.tensor_mul(src, src, C("cos").unsqueeze(1).broadcast_to([P, 2, S]))
                    v.drain()
                    w.tensor_add(src, src, r3)
                    v.drain().then_inc(sem("rotated"), 1)
                outputs(1)
                attention(l, LAYER_PAIRS)
                layer_norm(l, 0)
                copy_x1T(l, 1)
                for j in range(FT + 1):
                    if j < FT:
                        v.wait_ge(sem("up_act"), at(l, "up_act", j + 1))
                        for s in range(1, FTAPS):
                            for gv in range(2):
                                c = (2 - s) * 2 * FT + gv * FT + j
                                last = w.scalar_tensor_tensor(facc[:, j % 3, gv, s:S], ps[UP_BANKS[j % 4]][:, gv * S:(gv + 1) * S - s], cw[:, 48 + c:49 + c],
                                                              facc[:, j % 3, gv, s:S], ALU.mult, ALU.add)
                            if s < FTAPS - 1:
                                v.drain()
                        last.then_inc(sem("up_dve"), 1)
                        v.drain()
                    if j:
                        v.wait_ge(sem("up_silu"), at(l, "up_silu", j))
                        w.tensor_mul(hidT[:, j - 1, :], facc[:, (j - 1) % 3, 0, :], facc[:, (j - 1) % 3, 1, :]).then_inc(sem("hid"), 1)
                layer_norm(l, 1)
            if stop_a:
                return

            def rms(n, t, dst, done):
                if t == 0:
                    v.wait_ge(sem(f"g{n + 1}"), 16)
                v.wait_ge(sem("r_rs"), 2 * n + t + 1)
                w.reciprocal(rsb[:, t:t + 1], rsb[:, t:t + 1])
                v.drain()
                w.scalar_tensor_tensor(dst[:, t, :], x[:, t, :], rsb[:, t:t + 1], gbc, ALU.mult, ALU.mult).then_inc(sem(done), 1)

            L = DEPTH
            rms(0, 0, hrows, "h1_rows")
            rms(0, 1, hrows, "h1_rows")
            copy_x0T(at(L, "x0_tr", 2))
            copy_x1T(L, 0)
            v.wait_ge(sem("bias_mm"), 1)
            w.tensor_copy(tb_sb[0:BIAS_HEADS, :], ps[3][0:BIAS_HEADS, :]).then_inc(sem("bias_sb"), 1)
            v.wait_ge(sem("b_small"), 96)
            for n in range(2):
                w.tensor_mul(lamv[:, 2 * n, :], lamv[:, 2 * n, :], lamv[:, 2 * n + 1, :])
            w.tensor_scalar(subg, subg, 1.0 - LAMBDA_INIT, None, ALU.mult)
            v.drain()
            for n in range(2):
                last = w.tensor_reduce(lame[:, n:n + 1], lamv[:, 2 * n, :], AX.X, ALU.add)
            last.then_inc(sem("lam_dot"), 1)
            v.wait_ge(sem("lam_exp"), 1)
            w.tensor_sub(neglam, lame[:, 3:4], lame[:, 2:3])
            v.drain()
            w.tensor_scalar(neglam, neglam, -LAMBDA_INIT, None, ALU.add)
            v.drain()
            v.wait_ge(sem("bias_back"), 16 * BIAS_HEADS)
            attention(L, SECOND_PAIRS)
            osq = bE.rearrange("p x y z -> p (x y z)")[:, 0:1024]
            oss = lame
            v.wait_ge(sem("at_tr"), at(L, "at_tr", 2 * len(SECOND_PAIRS)))
            v.drain()
            w.tensor_mul(osq, oa.rearrange("p x y -> p (x y)"), oa.rearrange("p x y -> p (x y)"))
            v.drain()
            w.tensor_reduce(oss, osq.rearrange("p (a n) -> p a n", n=P), AX.X, ALU.add).then_inc(sem("oa_sum"), 1)
            v.wait_ge(sem("oa_rs"), 1)
            w.reciprocal(oss, oss)
            v.drain()
            for t in range(T):
                for h in range(H):
                    o_ = oa[:, t, h * P:(h + 1) * P]
                    last = w.scalar_tensor_tensor(o_, o_, oss[:, 4 * t + h:4 * t + h + 1], subg, ALU.mult, ALU.mult)
            last.then_inc(sem("oa_rows"), 4)
            for t in range(T):
                if t == 0:
                    v.wait_ge(sem("rows_t0"), at(L, "rows_t0", 1))
                else:
                    v.wait_ge(sem("rows_used"), (DEPTH + 1) * ROW_UNITS + 2)
                for nh in range(2):
                    xs = x[:, t, nh * 512:(nh + 1) * 512]
                    last = w.tensor_add(xs, xs, ps[ROWS_BANKS[2 * t + nh]][:, :])
                last.then_inc(sem("r_in"), 1)
                v.drain()
                rms(1, t, hrows, "h2_rows")
            v.wait_ge(sem("logits"), 1)
            lg = ps[2][:, 0:2 * NE].rearrange("p (t n) -> p t n", n=NE)
            w.tensor_copy(rl, lg)
            w.tensor_reduce(rmax, lg, AX.X, ALU.max, negate=True)
            v.drain().then_inc(sem("rl_ready"), 1)
            v.wait_ge(sem("rl_exp"), 1)
            w.reciprocal(rsum, rsum)
            v.drain()
            w.tensor_mul(rl, rl, rsum.unsqueeze(2).broadcast_to([P, T, NE])).then_inc(sem("aff"), 1)
            v.wait_ge(sem("aff_tr"), 1)
            w.tensor_copy(affT, ps[3][0:NE, 0:S])
            v.drain()
            for r in range(CAP // 8):
                cur = affT if r % 2 == 0 else affW
                nxt = affW if r % 2 == 0 else affT
                w.max(topv[:, 8 * r:8 * r + 8], cur)
                v.drain()
                w.max_index(topidx[:, 8 * r:8 * r + 8], topv[:, 8 * r:8 * r + 8], cur)
                w.match_replace(nxt, topv[:, 8 * r:8 * r + 8], cur, -1.0)
                v.drain()
            w.tensor_copy(topf, topidx)
            v.drain()
            w.tensor_mul(spread.rearrange("p (e s) -> p e s", s=CAP), topf.unsqueeze(1).broadcast_to([NE, NE, CAP]), C("own")[0:NE, :].rearrange("p (e s) -> p e s", s=CAP))
            w.tensor_copy(rep[:, 0:P].rearrange("p (q s) -> p q s", s=CAP), topf.unsqueeze(1).broadcast_to([NE, 4, CAP]))
            w.tensor_copy(rep[:, P:2 * P].rearrange("p (q s) -> p q s", s=CAP), topv.unsqueeze(1).broadcast_to([NE, 4, CAP]))
            v.drain().then_inc(sem("chosen"), 1)
            v.wait_ge(sem("spread_mm"), 1)
            for t in range(T):
                last = w.tensor_scalar(oneT[:, t, :], ps[6][:, :], C("tok_col")[:, t:t + 1], None, ALU.is_equal)
            last.then_inc(sem("onehot"), 1)
            w.tensor_copy(idx4, ps[7][:, 0:NE])
            w.tensor_copy(g4, ps[7][:, NE:2 * NE])
            v.drain()
            def expert(e, first=False):
                v.wait_ge(sem("xe_evac"), 2 if first else 2 + KT)
                w.tensor_copy(xe, xeT[:, :, bass.ds(e * CAP, CAP)])
                w.tensor_scalar(pg, C("tok_row"), idx4[:, bass.ds(e, 1)], g4[:, bass.ds(e, 1)], ALU.is_equal, ALU.mult)
                v.drain().then_inc(sem("xe_ready"), 1)
                if first:
                    v.wait_ge(sem("xe_mm"), 2 + KT)
                    w.memset(hh[64:P, 5, :], 0.0)
                for b, (c0, n) in enumerate(PIECES):
                    v.wait_ge(sem("esg"), e * 3 + b + 1)
                    for odd in range(2):
                        m = 2 if odd == 0 or b < 2 else 1
                        blocks = lambda y: y.rearrange("p (m n) -> p m n", n=P)[:, odd::2, :][:, 0:m, :]
                        last = w.tensor_mul(hh[64 * odd:64 * odd + 64, 2 * b:2 * b + m, :], blocks(sg[0:64, c0:c0 + n]), blocks(ps[b][64:P, 0:n]))
                    last.then_inc(sem("eh"), 1)
                v.wait_ge(sem("eo_mm"), e + 1)
                for q in range(4):
                    xs = x[:, :, q * 256:(q + 1) * 256]
                    w.tensor_add(xs, xs, ps[OUT_BANKS[q]][:, :].rearrange("p (t n) -> p t n", n=256))
                v.drain()
            expert(0, True)
            with v.Fori(1, NE) as e:
                expert(e)
            v.drain().then_inc(sem("r_in"), 2)
            for t in range(T):
                rms(2, t, x, "final_rows")


_INS = ["x", "w_in", "gdn_conv_w", "gdn_a_log", "gdn_dt_bias", "gdn_norm_g", "w_out", "ln1_g", "ln1_b", "w_up",
        "ffn_conv_w", "ffn_conv_b", "w_down", "ln2_g", "ln2_b", "norm1_g_2", "w_in_2", "lam_q1_2", "lam_k1_2",
        "lam_q2_2", "lam_k2_2", "subln_g_2", "w_out_2", "rel_bias_2", "norm2_g_2", "w_router_2", "w_gate_2",
        "w_up_2", "w_down_2", "norm_f_g_2"]


def kernel(**inputs):
    import concourse.bacc as bacc
    from concourse.bass_utils import run_bass_kernel_spmd

    nc = bacc.Bacc("TRN2", target_bir_lowering=False, num_devices=1)
    consts, cat = constants()
    table, takes = bias_tables()
    arrays = {"consts": consts, "bias_table": table, "takes": takes}
    for name in _INS:
        v = np.ascontiguousarray(inputs[name])
        arrays[name] = v.reshape(1, -1) if v.ndim == 1 else v
    a = {name: nc.dram_tensor("in_" + name, v.shape, mybir.dt.from_np(v.dtype), kind="ExternalInput").ap() for name, v in arrays.items()}
    out = nc.dram_tensor("out", (1, S, D), F32, kind="ExternalOutput").ap()
    scratch = nc.dram_tensor("bias_rows", (BIAS_HEADS, P * 2 * S), F32, kind="Internal").ap()
    build(nc, a, out, scratch, cat)
    r = run_bass_kernel_spmd(nc, [{"in_" + name: v for name, v in arrays.items()}], core_ids=[0])
    return r.results[0]["out"]
```

```python
import numpy as np
from contextlib import ExitStack

import concourse.bass as bass
from concourse import mybir

F32 = mybir.dt.float32
U32 = mybir.dt.uint32
ACT = mybir.ActivationFunctionType
ALU = mybir.AluOpType
AX = mybir.AxisListType

P = 128
S = 256
T = S // P
D = 1024
KT = D // P
DEPTH = 2
H = 4
DK = 128
CHUNK = 64
FF = 2816
FT = FF // P
TAPS, FTAPS = 4, 3
ROPE_HALF, ROPE_THETA, DH = 8, 500000.0, 64
NE, CAP = 16, 32
BUCKETS, BIAS_HEADS = 32, 12
ALPHA = (2 * DEPTH) ** 0.25
LN_EPS, NORM_EPS, SUBLN_EPS = 1e-5, 1e-6, 1e-5
LAMBDA_INIT = 0.2
NEG = -1e30

RING = 4
SBUF_FLOATS = 53200
SLOT = 4096
OFF = {"q": 0, "k": 512, "v": 1024, "ab": 1536, "z": 1544, "qb": 2056, "kb": 2568, "vb": 3080}
UNITS_IN = ["q", "k", "v", "ab", "z", "qb", "kb", "vb"]
U_OUT, U_UP, U_DOWN = 8, 10, 21
DOWN_TILES = [4, 3, 3, 3, 3, 3, 3]
UNITS = 28
ROW_UNITS = 2 + len(DOWN_TILES)
UNITS_IN_2 = [0, 512, 1024, 1536, 2048, 2560]
GU_RING, D_RING = 4, 11
HALF = FF // 2
HT = HALF // P
PIECES = [(0, 512), (512, 512), (1024, 384)]
IN_BANKS = (0, 1, 4, 5, 0, 1, 6, 7, 4, 5)
UP_BANKS = (0, 1, 4, 5)
SECOND_BANKS = (0, 1, 4, 5, 0, 1, 4, 5, 4, 5, 4, 5)
SECOND_BANKS_AFTER = {4: 1, 5: 2, 6: 3, 7: 4, 8: 7, 9: 8, 10: 9, 11: 10}
AHEAD = 3
O_BANKS = (6, 1)
XE_BANKS, FIRST = (3, 4, 6, 7), 4 * CAP
ROWS_BANKS = (2, 3, 6, 7)
H2_BANKS = (0, 1, 4, 5)
HID_BANKS, OUT_BANKS = (3, 4, 6), (6, 7, 3, 4)


def constants():
    i = np.arange(P)[:, None]
    j = np.arange(P)[None, :]
    same = (i // CHUNK) == (j // CHUNK)
    neg = lambda ok: np.where(ok, 0.0, NEG)
    parts = {
        "ident": (i == j) * 1.0,
        "ones": np.ones((P, P)),
        "eps": np.broadcast_to(np.array([[LN_EPS, NORM_EPS, SUBLN_EPS, 0.0]]), (P, 4)),
        "cum": (same & (i <= j)) * 1.0,
        "neg_strict": neg(same & (i > j)),
        "neg_incl_t": neg(same & (i <= j)),
    }
    for n in range(6):
        s = 1 << n
        parts[f"level{n}"] = ((i // (2 * s) == j // (2 * s)) & (i % (2 * s) >= s) & (j % (2 * s) < s)) * 1.0
    rot = np.zeros((P, P))
    cos, sin = np.ones((P, S)), np.zeros((P, S))
    inv = np.float32(ROPE_THETA) ** (-np.arange(ROPE_HALF, dtype=np.float32) / np.float32(ROPE_HALF))
    ang = np.arange(S, dtype=np.float32)[:, None] * inv[None, :].astype(np.float32)
    for h in range(P // DH):
        for c in range(ROPE_HALF):
            a, b = h * DH + c, h * DH + ROPE_HALF + c
            rot[b, a], rot[a, b] = -1.0, 1.0
            cos[[a, b]] = np.cos(ang[:, c])
            sin[[a, b]] = np.sin(ang[:, c])
    parts["rot"], parts["cos"], parts["sin"] = rot, cos, sin
    jj = np.arange(3 * P)[None, :]
    parts["causal"] = neg(jj <= i + P)
    parts["tok_row"] = np.broadcast_to(np.arange(S)[None, :], (P, S))
    parts["tok_col"] = np.concatenate([i, i + P], 1)
    own = (np.arange(NE)[:, None] == (np.arange(NE * CAP) // CAP)[None, :]) * 1.0
    parts["own"] = np.concatenate([own, np.zeros((P - NE, NE * CAP))])
    at, cols = {}, 0
    for name, a in parts.items():
        at[name] = (cols, a.shape[1])
        cols += a.shape[1]
    return np.ascontiguousarray(np.concatenate([np.asarray(a, np.float32) for a in parts.values()], 1)), at


def bias_tables():
    rel = np.arange(-(S - 1), S + 1)
    n = np.abs(rel)
    half, exact = BUCKETS // 2, BUCKETS // 4
    nf = np.maximum(n, 1).astype(np.float32)
    large = exact + (np.log(nf / np.float32(exact)) / np.float32(np.log(1024 / exact)) * np.float32(half - exact)).astype(np.int32)
    bucket = np.where(rel > 0, half, 0) + np.where(n < exact, n, np.minimum(large, half - 1))
    count = (n <= 64) * 1 + (rel % 4 == 0) * 1 + (rel % 16 == 0) * 1
    table = np.zeros((BUCKETS + 1, 2 * S), np.float32)
    table[bucket, np.arange(2 * S)] = 1.0
    table[BUCKETS] = np.where(count > 0, np.log(np.maximum(count, 1)), NEG)
    takes = np.zeros((1, BIAS_HEADS), np.float32)
    takes[0, H:] = 1.0
    return table, takes


PER = dict(
    x_rows=4, rows_t0=2, x0_transposed=2, x0_copied=2, x1_transposed=4, x1_copied=4, conv_in=64, small_in=48,
    ln1_in=32, ln2_in=32, conv_transposed=1, conv_weights=1, projected=14, last_tap=6, convolved=6, channels_silu=6,
    projection_read=8, gate_logits=1, gate_inputs=1, gate_exps=1, decay_logs=1, squares=4, norm_sums=1,
    norm_sums_read=1, norm_logs=1, cumulated=1, query_decays=1, z_gated=1, decay_arguments=1, pair_decays=2,
    kv_rows=4, values_scaled=1, keys_scaled=1, key_products=3, x_product=12, x_copied=10, update_product=10,
    intra_scores=1, q_swapped=1, q_swapped_read=1, q_rotated=1, token_decays=1, inverse_updated=12, level_masked=12,
    solved=2, w_copied=1, queries_decayed=1, predicted=3, new_values=4, state_product=3, state_updated=3,
    output_step=4, output_root=2, output_rows=2, output_transposed=2, output_mixed=2, k_swapped=2, k_rotated=2,
    scores=8, scores_biased=8, exps=8, probs=8, probs_transposed=8, probs_copied=8, attended=4, attended_read=4,
    norm_stats=4, norm_root=4, up_product=22, up_last_tap=22, up_convolved=22, gate_silu=22, hidden_ready=22,
)


def build(nc, a, out, scratch, CAT):
    ctx = ExitStack()
    with ctx:
        free = SBUF_FLOATS
        arena = ctx.enter_context(nc.sbuf_tensor("arena", [P, free], F32))
        ps = [ctx.enter_context(nc.psum_tensor(f"bank{i}", [P, 512], F32)) for i in range(8)]
        sems = {}

        def sem(name):
            if name not in sems:
                sems[name] = ctx.enter_context(nc.semaphore(name))
            return sems[name]

        def at(l, name, k):
            return l * PER[name] + k

        class Region:
            def __init__(self, lo, hi):
                self.at, self.hi = lo, hi

            def take(self, *dims):
                n = int(np.prod(dims))
                assert self.at + n <= self.hi, (dims, self.at, n, self.hi)
                v = arena[:, self.at:self.at + n]
                self.at += n
                if len(dims) == 2:
                    v = v.rearrange("p (x y) -> p x y", y=dims[1])
                if len(dims) == 3:
                    v = v.rearrange("p (x y z) -> p x y z", y=dims[1], z=dims[2])
                if len(dims) == 4:
                    v = v.rearrange("p (x y z w) -> p x y z w", y=dims[1], z=dims[2], w=dims[3])
                return v

        NC = sum(n for _, n in CAT.values())
        keep = Region(0, free)
        const = keep.take(NC)
        table = lambda name: const[:, CAT[name][0]:CAT[name][0] + CAT[name][1]]
        ident, ones = table("ident"), table("ones")
        ln_eps, norm_eps, subln_eps = (table("eps")[:, i:i + 1] for i in range(3))
        x = keep.take(T, D)
        xT = keep.take(KT, S)
        mixT = keep.take(KT, S)
        stats = keep.take(T, 2, 6)
        mean_var = keep.take(T, 2)
        inv_std = keep.take(T, 1)
        neg_max, exp_sum, inv_sum = keep.take(4, 2), keep.take(4, 2), keep.take(4, 2)
        ring_at = keep.at
        ring = keep.take(RING, SLOT)
        after_ring = keep.at
        gate_up_ring = Region(ring_at, free).take(GU_RING, 2, FF)
        down_region = Region(ring_at + GU_RING * 2 * FF, free)
        down_ring = down_region.take(D_RING, D)
        after_experts_ring = down_region.at

        def slot(u, n=None):
            v = ring[:, u % RING, :]
            return v if n is None else v.rearrange("p (k n) -> p k n", n=n)

        layer_scratch = Region(after_ring, free)
        ln_g, ln_b = layer_scratch.take(D), layer_scratch.take(D)
        conv_rows = layer_scratch.take(3, P)
        conv_w = layer_scratch.take(48 + 88 + 88)
        dt_bias, a_log, norm_gain = layer_scratch.take(H), layer_scratch.take(H), layer_scratch.take(P)
        kept_end = layer_scratch.at
        qkv = layer_scratch.take(12, S)
        att_q, att_k = layer_scratch.take(4, S), layer_scratch.take(4, S)
        att_v, z_gate = layer_scratch.take(T, 512), layer_scratch.take(T, 512)
        small = layer_scratch.take(240)
        tiny_at = [0]

        def tiny(*dims):
            n = int(np.prod(dims))
            v = small[:, tiny_at[0]:tiny_at[0] + n]
            tiny_at[0] += n
            assert tiny_at[0] <= 240
            return v if len(dims) == 1 else v.rearrange("p (x y) -> p x y", y=dims[1])
        a_logit, b_logit, neg_abs_a, exp_neg_b, exp_neg_abs_a, log1p_a, g, beta = (tiny(T, H) for _ in range(8))
        exp_a_log = tiny(H)
        norm_sq, norm_log, chunk_sum, chunk_decay = (tiny(2 * T * H) for _ in range(4))
        g_by_chunk = tiny(2, T * H)
        decay_arg, decay_t_arg, key_decay, beta_decay, end_arg, end_decay, out_sq, out_root = (tiny(T * H) for _ in range(8))
        delta_at = layer_scratch.at
        qk_squares = layer_scratch.take(4, 512)
        g_spread = layer_scratch.take(8, P)
        decay = layer_scratch.take(8, P)
        decay_t = layer_scratch.take(8, P)
        query_decay = layer_scratch.take(8, P)
        keys_beta, keys_end, values_beta = layer_scratch.take(8, P), layer_scratch.take(8, P), layer_scratch.take(8, P)
        A_all, inverse, inverse_t = layer_scratch.take(8, P), layer_scratch.take(8, P), layer_scratch.take(8, P)
        level_part, half_product = (qk_squares[:, 2 * i:2 * i + 2, :].rearrange("p x y -> p (x y)").rearrange("p (x y) -> p x y", y=P) for i in range(2))
        q_swapped = qkv[:, 4:8, :].rearrange("p x y -> p (x y)").rearrange("p (x y) -> p x y", y=512)
        intra = decay_t
        u_rows, v_new, w_t = g_spread, g_spread, decay
        state = layer_scratch.take(H, P)
        norm_log_spread = qk_squares.rearrange("p x y -> p (x y)").rearrange("p (x y) -> p x y", y=P)
        attention_scratch = Region(delta_at, free)
        att_scores = attention_scratch.take(4, 2, S)
        att_probs_t = attention_scratch.take(2, 4, S)
        rot_tmp = attention_scratch.take(512)
        feed_forward = Region(kept_end, free)
        hidT = feed_forward.take(FT, S)
        ff_conv = feed_forward.take(3, 2, S)
        a_end = layer_scratch.at

        second_scratch = Region(after_experts_ring, free)
        normed_rows = second_scratch.take(T, D)
        gain = second_scratch.take(D)
        chosen_x_t = second_scratch.take(KT, NE * CAP)
        one_hot = second_scratch.take(T, NE * CAP)
        c_tiny = second_scratch.take(320)
        c_end = second_scratch.at
        second_attention = Region(after_ring, after_experts_ring)
        qaT, kaT, qdT, kdT = (second_attention.take(4, S) for _ in range(4))
        va, vd = second_attention.take(T, 512), second_attention.take(T, 512)
        scores_2 = second_attention.take(4, 2, S)
        probs_t_2 = second_attention.take(2, 4, S)
        bias12 = Region(after_experts_ring + T * D + D, free).take(BIAS_HEADS, 3 * P)
        diff_out = second_attention.take(T, 512)
        bias_scratch = Region(max(c_end, a_end), free)
        distance_bias, bucket_table, bucket_bias = bias_scratch.take(2 * S), bias_scratch.take(2 * S), bias_scratch.take(BIAS_HEADS)
        mix_flat = mixT.rearrange("p x y -> p (x y)")
        expert_gate = mix_flat[:, 0:HALF]
        expert_x = xT.rearrange("p x y -> p (x y)")[:, 0:KT * CAP].rearrange("p (k s) -> p k s", s=CAP)
        placing = xT.rearrange("p x y -> p (x y)")[:, 256:512]
        hidden_t = xT.rearrange("p x y -> p (x y)")[:, 512:512 + (HT + 1) * 64].rearrange("p (k s) -> p k s", s=64)
        out_quarters = normed_rows.rearrange("p x y -> p (x y)")[:, D:2 * D]
        hidden = normed_rows.rearrange("p x y -> p (x y)")[:, 0:6 * P].rearrange("p (m n) -> p m n", n=P)
        second_tiny_at = [0]

        def second_tiny(*dims):
            n = int(np.prod(dims))
            v = c_tiny[:, second_tiny_at[0]:second_tiny_at[0] + n]
            second_tiny_at[0] += n
            assert second_tiny_at[0] <= 320
            return v if len(dims) == 1 else v.rearrange("p (x y) -> p x y", y=dims[1])
        router_w = second_tiny(KT, NE)
        topidx = second_tiny(CAP)[0:NE, :].bitcast(U32)
        sum_sq, inv_rms = second_tiny(T), second_tiny(T)
        neg_lambda = second_tiny(1)
        subln_gain = Region(second_attention.at, after_experts_ring).take(P)
        lambda_vectors = Region(second_attention.at + P, after_experts_ring).take(4, DH)
        lambda_parts = Region(second_attention.at + P + 256, after_experts_ring).take(8)
        router, rmax, rsum = second_tiny(T, NE), second_tiny(T), second_tiny(T)
        affT = one_hot.rearrange("p x y -> p (x y)")[0:NE, 0:S]
        affW = one_hot.rearrange("p x y -> p (x y)")[0:NE, S:2 * S]
        topv = chosen_x_t.rearrange("p x y -> p (x y)")[0:NE, 0:CAP]
        topf = chosen_x_t.rearrange("p x y -> p (x y)")[0:NE, 64:64 + CAP]
        spread = chosen_x_t.rearrange("p x y -> p (x y)")[0:NE, 512:1024]
        rep = chosen_x_t.rearrange("p x y -> p (x y)")[0:NE, 1024:1280]
        places, affinity = second_tiny(NE), second_tiny(NE)

        block = ctx.enter_context(nc.Block())

        @block.sync
        def _(sp):
            sp.dma_start(bucket_table[0:BUCKETS + 1, :], a["bias_table"]).then_inc(sem("bias_in"), 16)
            sp.dma_start(bucket_bias[0:BUCKETS, :], a["rel_bias_2"]).then_inc(sem("bias_in"), 16)
            sp.dma_start(bucket_bias[BUCKETS:BUCKETS + 1, :], a["takes"]).then_inc(sem("bias_in"), 16)
            sp.dma_start(x, a["x"][0].rearrange("(t p) n -> p t n", p=P)).then_inc(sem("x_in"), 16)
            sp.dma_start(const[:, 0:2 * P + 4], a["consts"][:, 0:2 * P + 4]).then_inc(sem("ident_in"), 16)
            sp.sem_inc(sem("rows_used"), ROW_UNITS)

            def used(l, u):
                if u in (0, 1, 2):
                    return "projected", at(l, "projected", 2 * (u + 1))
                if u == 3:
                    return "gate_logits", at(l, "gate_logits", 1)
                if u < U_OUT:
                    return "projected", at(l, "projected", 2 * u)
                if U_UP <= u < U_DOWN:
                    return "up_product", at(l, "up_product", 2 * (u - U_UP + 1))
                return "rows_used", (l + 1) * ROW_UNITS + (u - U_OUT + 1 if u < U_UP else u - U_DOWN + 3)

            def stream(l, u, halves, before=None):
                name, value = before or (used(l, u - RING) if u >= RING else used(l - 1, UNITS + u - RING))
                sp.wait_ge(sem(name), value)
                for to_, from_ in halves:
                    sp.dma_start(to_, from_).then_inc(sem(f"slot_in{u % RING}"), 16)

            def columns(w, l, c, n, u):
                v = w[bass.ds(l, 1), :, c:c + n].rearrange("o (k p) n -> p (o k) n", p=P)
                s = slot(u, 512)[:, :, 0:n]
                return [(s[:, 0:4], v[:, 0:4]), (s[:, 4:8], v[:, 4:8])]

            def rows(w, l, k0, n, u):
                v = w[bass.ds(l, 1), k0 * P:(k0 + n) * P, :].rearrange("o (k p) n -> p (o k) n", p=P)
                s = slot(u, 1024)
                h = n // 2
                return [(s[:, 0:h], v[:, 0:h]), (s[:, h:n], v[:, h:n])]

            def bcast(w, l, n):
                return w[bass.ds(l, 1), :].broadcast_to([P, n])

            with sp.Fori(0, DEPTH) as l:
                for u, name in enumerate(UNITS_IN):
                    stream(l, u, columns(a["w_in"], l, OFF[name], 8 if name == "ab" else 512, u))
                    if u == RING - 1:
                        sp.wait_ge(sem("x_rows"), at(l, "x_rows", 2))
                        c = a["gdn_conv_w"][bass.ds(l, 1)].rearrange("o j (t p) -> (o j t) p", p=P)
                        sp.dma_start(conv_rows[0:48, 0, :], c).then_inc(sem("conv_in"), 16)
                        f = a["ffn_conv_w"][bass.ds(l, 1)].rearrange("o j (t p) -> (o j t) p", p=P)
                        sp.dma_start(conv_rows[0:88, 1, :], f[0:88, :]).then_inc(sem("conv_in"), 16)
                        sp.dma_start(conv_rows[0:44, 2, :], f[88:132, :]).then_inc(sem("conv_in"), 8 * 2)
                        sp.dma_start(conv_rows[44:88, 2, :], a["ffn_conv_b"][bass.ds(l, 1)].rearrange("o (t p) -> (o t) p", p=P)).then_inc(sem("conv_in"), 16)
                        sp.dma_start(dt_bias, bcast(a["gdn_dt_bias"], l, H)).then_inc(sem("small_in"), 16)
                        sp.dma_start(a_log, bcast(a["gdn_a_log"], l, H)).then_inc(sem("small_in"), 16)
                        sp.dma_start(norm_gain, bcast(a["gdn_norm_g"], l, P)).then_inc(sem("small_in"), 16)
                        sp.dma_start(ln_g, bcast(a["ln1_g"], l, D)).then_inc(sem("ln1_in"), 16)
                        sp.dma_start(ln_b, bcast(a["ln1_b"], l, D)).then_inc(sem("ln1_in"), 16)
                for i in range(2):
                    stream(l, U_OUT + i, rows(a["w_out"], l, 4 * i, 4, U_OUT + i))
                for i in range(11):
                    u = U_UP + i
                    s = slot(u, 512)
                    g_ = a["w_up"][bass.ds(l, 1), :, 256 * i:256 * i + 256].rearrange("o (k p) n -> p (o k) n", p=P)
                    v_ = a["w_up"][bass.ds(l, 1), :, FF + 256 * i:FF + 256 * i + 256].rearrange("o (k p) n -> p (o k) n", p=P)
                    stream(l, u, [(s[:, :, 0:256], g_), (s[:, :, 256:512], v_)])
                    if i == RING - 1:
                        sp.wait_ge(sem("x_rows"), at(l, "x_rows", 4))
                        sp.dma_start(ln_g, bcast(a["ln2_g"], l, D)).then_inc(sem("ln2_in"), 16)
                        sp.dma_start(ln_b, bcast(a["ln2_b"], l, D)).then_inc(sem("ln2_in"), 16)
                k0 = 0
                for i, n in enumerate(DOWN_TILES):
                    stream(l, U_DOWN + i, rows(a["w_down"], l, k0, n, U_DOWN + i))
                    k0 += n
            for u, c in enumerate(UNITS_IN_2):
                stream(DEPTH, u, columns(a["w_in_2"], 0, c, 512, u), ("projected_2", 2 * (u - RING + 1)) if u >= RING else None)
            for i in range(2):
                stream(DEPTH, 6 + i, rows(a["w_out_2"], 0, 4 * (1 - i), 4, 6 + i), ("projected_2", 2 * (3 + i)))
            sp.sem_inc(sem("gate_up_free"), GU_RING)
            sp.sem_inc(sem("down_free"), D_RING)

            def gate_up(e, k):
                for n, w in enumerate(("w_gate_2", "w_up_2")):
                    sp.dma_start(gate_up_ring[:, k % GU_RING, n, :], a[w][0, bass.ds(e, 1), k * P:(k + 1) * P, :].rearrange("o p n -> (o p) n")
                                 ).then_inc(sem(f"gu_in{k % GU_RING}"), 16)

            def down(e, k):
                sp.dma_start(down_ring[:, k % D_RING, :], a["w_down_2"][0, bass.ds(e, 1), k * P:(k + 1) * P, :].rearrange("o p n -> (o p) n")
                             ).then_inc(sem(f"d_in{k % D_RING}"), 16)

            sp.wait_ge(sem("projected_2"), 12)
            gate_up(0, 0)
            sp.wait_ge(sem("diff_transposed"), 1)
            gate_up(0, 3)
            for k in range(D_RING):
                down(0, k)
            sp.wait_ge(sem("rows_used"), (DEPTH + 1) * ROW_UNITS + 2)
            gate_up(0, 1)
            gate_up(0, 2)

            def stream_gate_up(e, ks):
                for k in ks:
                    sp.wait_ge(sem("gate_up_free"), e * KT + k + 1)
                    gate_up(e, k)

            def stream_down(e, ks):
                for k in ks:
                    sp.wait_ge(sem("down_free"), e * FT + k + 1)
                    down(e, k)

            stream_gate_up(0, range(GU_RING, KT))
            stream_gate_up(1, range(0, 2))
            stream_down(0, range(D_RING, FT))
            stream_gate_up(1, range(2, KT))
            stream_down(1, range(FT))
            with sp.Fori(2, NE) as e:
                stream_gate_up(e, range(KT))
                stream_down(e, range(FT))
            for t in range(T):
                sp.wait_ge(sem("final_rows"), t + 1)
                sp.dma_start(out[0, t * P:(t + 1) * P, :], x[:, t, :]).then_inc(sem("stored"), 16)
            sp.wait_ge(sem("stored"), 16 * T)

        @block.gpsimd
        def _(pool):
            pool.wait_ge(sem("slot_in1"), 32)
            pool.dma_start(const[:, 2 * P + 4:NC], a["consts"][:, 2 * P + 4:NC]).then_inc(sem("const_in"), 16)
            pool.wait_ge(sem("bias_copied"), 1)
            pool.wait_ge(sem("key_products"), 1)
            pool.dma_start(scratch.rearrange("h (p n) -> h p n", p=P), distance_bias[0:BIAS_HEADS, :].unsqueeze(1).broadcast_to([BIAS_HEADS, P, 2 * S])).then_inc(sem("bias_out"), 16)
            with pool.Fori(0, DEPTH) as l:
                pool.wait_ge(sem("projection_read"), at(l, "projection_read", 2))
                pool.wait_ge(sem("small_in"), l * 48 + 48)
                for t in range(T):
                    zz = z_gate[:, t, :].rearrange("p (h n) -> p h n", n=P)
                    last = nc.gpsimd.tensor_tensor(zz, zz, norm_gain.unsqueeze(1).broadcast_to([P, H, P]), ALU.mult)
                last.then_inc(sem("z_gated"), 1)
                pool.wait_ge(sem("key_products"), at(l, "key_products", 3))
                pool.wait_ge(sem("query_decays"), at(l, "query_decays", 1))
                for t in range(T):
                    qq = qkv[:, 0:4, t * P:(t + 1) * P]
                    last = nc.gpsimd.tensor_tensor(qq, qq, query_decay[:, 4 * t:4 * t + 4, :], ALU.mult)
                last.then_inc(sem("queries_decayed"), 1)
                pool.wait_ge(sem("q_swapped_read"), at(l, "q_swapped_read", 1))
                qo = qkv[:, 4:8, :]
                nc.gpsimd.tensor_tensor(qo, qo, table("sin").unsqueeze(1).broadcast_to([P, 4, S]), ALU.mult)
                nc.gpsimd.tensor_tensor(att_q, att_q, table("cos").unsqueeze(1).broadcast_to([P, 4, S]), ALU.mult)
                pool.drain()
                nc.gpsimd.tensor_tensor(att_q, att_q, qo, ALU.add).then_inc(sem("q_rotated"), 1)
            pool.wait_ge(sem("rows_used"), DEPTH * ROW_UNITS + 2)
            pool.dma_start(gain, a["norm1_g_2"].broadcast_to([P, D])).then_inc(sem("gain_in1"), 16)
            pool.wait_ge(sem("bias_out"), 16)
            for h in range(BIAS_HEADS):
                v = scratch[h:h + 1, P - 1:P - 1 + P * (2 * S - 1)].rearrange("o (p n) -> (o p) n", p=P)[:, 0:3 * P]
                pool.dma_start(bias12[:, h, :], v).then_inc(sem("bias_back"), 16)
            pool.dma_start(subln_gain, a["subln_g_2"].broadcast_to([P, P])).then_inc(sem("second_small_in"), 16)
            for n, name in enumerate(("lam_q1_2", "lam_k1_2", "lam_q2_2", "lam_k2_2")):
                pool.dma_start(lambda_vectors[:, n, :], a[name].broadcast_to([P, DH])).then_inc(sem("second_small_in"), 16)
            pool.dma_start(router_w, a["w_router_2"][0].rearrange("(k p) e -> p k e", p=P)).then_inc(sem("second_small_in"), 16)
            pool.wait_ge(sem("h1_rows"), T)
            pool.dma_start(gain, a["norm2_g_2"].broadcast_to([P, D])).then_inc(sem("gain_in2"), 16)
            pool.wait_ge(sem("h2_rows"), T)
            pool.dma_start(gain, a["norm_f_g_2"].broadcast_to([P, D])).then_inc(sem("gain_in3"), 16)

        LAYER_PAIRS = [("causal", n) for n in range(4)]
        SECOND_PAIRS = [("diff", n) for n in range(4)] + [("dil", n) for n in range(4)]
        SC, TR, PV = ((2, 3), (4, 5)), (6, 7), (0, 1)

        def attention_operands(kind):
            if kind == "causal":
                return att_q, att_k, att_v, att_scores, att_probs_t
            return (qaT, kaT, va, scores_2, probs_t_2) if kind == "diff" else (qdT, kdT, vd, scores_2, probs_t_2)

        def keys(kind, t):
            return P if kind == "causal" and t == 0 else S

        def score_banks(kind, i):
            return SC[0] if kind == "diff" else SC[i % 2]

        def out_read(l, pairs, pi):
            kind = pairs[pi][0]
            done = sum(1 for k_, _ in pairs[:pi + 1] if k_ == kind)
            return (sem("diff_read"), done) if kind == "diff" else (sem("attended_read"), at(l, "attended_read", done))

        @block.tensor
        def _(pe):
            mm, tr = nc.tensor.matmul, nc.tensor.transpose

            def unit_in(l, u):
                pe.wait_ge(sem(f"slot_in{u % RING}"), l * (UNITS // RING * 32) + 32 * (u // RING + 1))

            def transpose_x(src, t, done):
                for kh in range(2):
                    for k in range(4):
                        last = tr(ps[4 + 2 * t + kh][:, k * P:(k + 1) * P], src[:, t, (4 * kh + k) * P:(4 * kh + k + 1) * P], ident)
                    if t or kh:
                        last.then_inc(sem(done), 1)

            def second_tile(l, n):
                pe.wait_ge(sem("x_rows"), at(l, "x_rows", 2 * n + 2))
                transpose_x(x, 1, "x1_transposed")
                pe.wait_ge(sem("x1_copied"), at(l, "x1_copied", 2 * n + 2))

            def channels(u, j0, bank, t=None, step=1, half=None):
                w = slot(u, 512)
                lo, n = (0, S) if t is None else (t * P, P)
                for j in range(2) if half is None else (half,):
                    c = (j0 + j * step) * P
                    for k in range(KT):
                        last = mm(ps[bank][:, j * S + lo:j * S + lo + n], w[:, k, c:c + P], xT[:, k, lo:lo + n], start=(k == 0), stop=(k == KT - 1))
                return last

            def tokens(u, t, bank, half=None):
                w = slot(u, 512)
                for k in range(KT) if half is None else range(KT // 2 * half, KT // 2 * (half + 1)):
                    last = mm(ps[bank][:, :], xT[:, k, t * P:(t + 1) * P], w[:, k, :], start=(k == 0), stop=(k == KT - 1))
                return last

            def rows_product(l, lhsT, u0, tiles, ready, between=None, k_first=0):
                split = len(tiles) - 2
                done, K = 0, sum(tiles)

                def products(u, k0, t):
                    w = slot(u0 + u, 1024)
                    for kk in range(tiles[u]):
                        if t == 0:
                            ready(k0 + kk)
                        for nh in range(2):
                            last = mm(ps[ROWS_BANKS[2 * t + nh]][:, :], lhsT[:, (k0 + kk + k_first) % K, t * P:(t + 1) * P], w[:, kk, nh * 512:(nh + 1) * 512],
                                      start=(k0 + kk == 0), stop=(k0 + kk == K - 1))
                    return last

                for u in range(split):
                    unit_in(l, u0 + u)
                    products(u, done, 0)
                    products(u, done, 1).then_inc(sem("rows_used"), 1)
                    done += tiles[u]
                for t in range(T):
                    k0 = done
                    for u in (split, split + 1):
                        if t == 0:
                            unit_in(l, u0 + u)
                        elif u == split + 1 and between:
                            between()
                        last = products(u, k0, t)
                        k0 += tiles[u]
                        if t:
                            last.then_inc(sem("rows_used"), 1)
                    if t == 0:
                        last.then_inc(sem("rows_t0"), 1)

            def attention(l, pairs, at_step={}):
                n = 2 * len(pairs)
                switch = 2 * sum(1 for kind, _ in pairs if kind == "diff")
                for i in range(n + 4):
                    if i < n:
                        kind, pr = pairs[i // 2]
                        q, k, _, E, PT = attention_operands(kind)
                        banks, before = score_banks(kind, i), i - (1 if kind == "diff" or i == switch else 2)
                        if before >= 0:
                            pe.wait_ge(sem("scores_biased"), at(l, "scores_biased", before + 1))
                        n_ = keys(kind, i % 2)
                        for m in range(2):
                            last = mm(ps[banks[m]][:, 0:n_], q[64 * m:64 * m + 64, pr, (i % 2) * P:(i % 2 + 1) * P],
                                      k[64 * m:64 * m + 64, pr, 0:n_], start=True, stop=True)
                        last.then_inc(sem("scores"), 1)
                    if i in at_step:
                        at_step[i]()
                    if 2 <= i < n + 2:
                        b = i - 2
                        kind, pr = pairs[b // 2]
                        E = attention_operands(kind)[3]
                        pe.wait_ge(sem("probs"), at(l, "probs", b + 1))
                        if b >= 2:
                            pe.wait_ge(sem("probs_copied"), at(l, "probs_copied", b - 1))
                        for m in range(1 if kind == "diff" else 2):
                            for kt in range(keys(kind, b % 2) // P):
                                last = tr(ps[TR[b % 2]][:, (2 * m + kt) * P:(2 * m + kt + 1) * P], E[:, b % 4, m, kt * P:(kt + 1) * P], ident)
                        last.then_inc(sem("probs_transposed"), 1)
                    if i >= 5 and i % 2 == 1:
                        pi = (i - 5) // 2
                        kind, pr = pairs[pi]
                        _, _, v, _, PT = attention_operands(kind)
                        pe.wait_ge(sem("probs_copied"), at(l, "probs_copied", 2 * pi + 2))
                        if pi >= 2:
                            pe.wait_ge(*out_read(l, pairs, pi - 2))
                        bank = ps[PV[pi % 2]]
                        if kind == "diff":
                            for t in range(T):
                                for kt in range(T):
                                    last = mm(bank[:, t * P:(t + 1) * P], PT[:, pi % 2, kt, t * P:(t + 1) * P],
                                              v[:, kt, pr * P:(pr + 1) * P], start=(kt == 0), stop=(kt == T - 1))
                        else:
                            for m in range(2):
                                for kt in range(T):
                                    q0 = kt * P if kind == "causal" else 0
                                    last = mm(bank[64 * m:64 * m + 64, q0:S], v[:, kt, (2 * pr + m) * DH:(2 * pr + m + 1) * DH],
                                              PT[:, pi % 2, 2 * m + kt, q0:S], start=(kt == 0), stop=(kt == T - 1))
                        last.then_inc(sem("attended"), 1)

            pe.wait_ge(sem("ident_in"), 16)

            def first_tile(rows):
                pe.wait_ge(sem("x_rows"), rows)
                transpose_x(x, 0, "x0_transposed")

            pe.wait_ge(sem("bias_in"), 48)
            mm(ps[3][0:BIAS_HEADS, :], bucket_bias[0:BUCKETS + 1, :], bucket_table[0:BUCKETS + 1, :], start=True, stop=True).then_inc(sem("bias_product"), 1)
            first_tile(1)
            with pe.Fori(0, DEPTH) as l:
                pe.wait_ge(sem("x0_copied"), at(l, "x0_copied", 1))
                for i in range(AHEAD):
                    if i % 2 == 0:
                        unit_in(l, i // 2)
                    channels(i // 2, 2 * (i % 2), IN_BANKS[i], t=0)
                second_tile(l, 0)
                for i in range(6):
                    if i < AHEAD:
                        channels(i // 2, 2 * (i % 2), IN_BANKS[i], t=1).then_inc(sem("projected"), 1)
                    else:
                        if i % 2 == 0:
                            unit_in(l, i // 2)
                        if i >= 4:
                            pe.wait_ge(sem("convolved"), at(l, "convolved", i - 3))
                        channels(i // 2, 2 * (i % 2), IN_BANKS[i]).then_inc(sem("projected"), 1)
                    if i == 1:
                        pe.wait_ge(sem("conv_in"), at(l, "conv_in", 64))
                        tr(ps[2][:, 48:136], conv_rows[0:88, 1, :], ident[0:88, 0:88])
                        tr(ps[2][:, 136:224], conv_rows[0:88, 2, :], ident[0:88, 0:88])
                        tr(ps[2][:, 0:48], conv_rows[0:48, 0, :], ident[0:48, 0:48]).then_inc(sem("conv_transposed"), 1)
                unit_in(l, 3)
                unit_in(l, 4)
                pe.wait_ge(sem("conv_weights"), at(l, "conv_weights", 1))
                for t in range(T):
                    for k in range(KT):
                        tokens_of = xT[:, k, t * P:(t + 1) * P]
                        logits = mm(ps[2][:, 8 * t:8 * t + 8], tokens_of, slot(3, 512)[:, k, 0:8], start=(k == 0), stop=(k == KT - 1))
                        if (t, k) == (T - 1, KT - 1):
                            logits.then_inc(sem("gate_logits"), 1)
                        last = mm(ps[IN_BANKS[6 + t]][:, :], tokens_of, slot(4, 512)[:, k, :], start=(k == 0), stop=(k == KT - 1))
                    last.then_inc(sem("projected"), 1)
                pe.wait_ge(sem("squares"), at(l, "squares", 4))
                unit_in(l, 5)
                pe.wait_ge(sem("convolved"), at(l, "convolved", 3))
                for j in range(2):
                    for k in range(KT):
                        last = mm(ps[IN_BANKS[8]][:, j * S:(j + 1) * S], slot(5, 512)[:, k, j * P:(j + 1) * P], xT[:, k, :], start=(k == 0), stop=(k == KT - 1))
                        if j == 0:
                            for n in (2 * k, 2 * k + 1):
                                t, h = n // 4 % 2, n % 4
                                c = h if n >= 8 else 4 + h
                                of_norms = mm(ps[3][:, n:n + 1], qk_squares[:, c // 2, (c % 2) * S + t * P:(c % 2) * S + (t + 1) * P], ones[:, 0:1], start=True, stop=True)
                    if j == 0:
                        of_norms.then_inc(sem("norm_sums"), 1)
                last.then_inc(sem("projected"), 1)
                pe.wait_ge(sem("const_in"), 16)
                pe.wait_ge(sem("decay_logs"), at(l, "decay_logs", 1))
                pe.wait_ge(sem("projection_read"), at(l, "projection_read", 3))
                mm(ps[4][:, 0:8], table("cum"), g.rearrange("p x y -> p (x y)"), start=True, stop=True)
                mm(ps[4][:, 8:24], ones, g_by_chunk.rearrange("p x y -> p (x y)"), start=True, stop=True)
                for t in range(T):
                    for qk in range(2):
                        for h in range(H):
                            o_ = ps[t + 2 * (1 - qk)][:, h * P:(h + 1) * P]
                            mm(o_, g_spread[:, 4 * t + h, :], table("cum"), start=True, stop=False)
                            last = mm(o_, norm_log_spread[:, 8 * qk + 4 * t + h, :], ident, start=False, stop=True)
                last.then_inc(sem("cumulated"), 1)
                pe.wait_ge(sem("projection_read"), at(l, "projection_read", 2))
                for t in range(T):
                    for h in range(H):
                        last = tr(ps[6 + t][:, h * P:(h + 1) * P], qkv[:, 4 + h, t * P:(t + 1) * P], ident)
                    last.then_inc(sem("kv_rows"), 1)
                pe.wait_ge(sem("convolved"), at(l, "convolved", 4))
                channels(5, 2, IN_BANKS[9]).then_inc(sem("projected"), 1)
                pe.wait_ge(sem("decay_arguments"), at(l, "decay_arguments", 1))
                for t in range(T):
                    if t:
                        pe.wait_ge(sem("projection_read"), at(l, "projection_read", 4))
                    for h in range(H):
                        last = tr(ps[4 + t][:, h * P:(h + 1) * P], qkv[:, 8 + h, t * P:(t + 1) * P], ident)
                    last.then_inc(sem("kv_rows"), 1)
                pe.wait_ge(sem("query_decays"), at(l, "query_decays", 1))
                keys_of = lambda t, h: qkv[:, 4 + h, t * P:(t + 1) * P]
                for t in range(T):
                    for h in range(H):
                        last = mm(ps[t][:, h * P:(h + 1) * P], keys_of(t, h), keys_of(t, h), start=True, stop=True)
                    last.then_inc(sem("key_products"), 1)
                for t in range(T):
                    for h in range(H):
                        last = mm(ps[2 + t][:, h * P:(h + 1) * P], keys_of(t, h), qkv[:, h, t * P:(t + 1) * P], start=True, stop=True)
                last.then_inc(sem("key_products"), 1)
                pe.wait_ge(sem("values_scaled"), at(l, "values_scaled", 1))
                pe.wait_ge(sem("keys_scaled"), at(l, "keys_scaled", 1))
                for lv in range(6):
                    for t in range(T):
                        n = 2 * lv + t
                        pe.wait_ge(sem("level_masked"), at(l, "level_masked", n + 1))
                        if lv:
                            pe.wait_ge(sem("inverse_updated"), at(l, "inverse_updated", n - 1))
                        for h in range(H):
                            last = mm(ps[4 + t][:, h * P:(h + 1) * P], level_part[:, 4 * t + h, :], inverse_t[:, 4 * t + h, :] if lv else ident, start=True, stop=True)
                        last.then_inc(sem("x_product"), 1)
                    if lv == 2:
                        pe.wait_ge(sem("intra_scores"), at(l, "intra_scores", 1))
                        for i in range(2):
                            last = mm(ps[2 + i][:, :], table("rot"), att_q[:, 2 * i:2 * i + 2, :].rearrange("p x y -> p (x y)"), start=True, stop=True)
                        last.then_inc(sem("q_swapped"), 1)
                    for t in range(T):
                        n = 2 * lv + t
                        if lv == 0:
                            continue
                        pe.wait_ge(sem("x_copied"), at(l, "x_copied", n - 1))
                        for h in range(H):
                            last = mm(ps[6 + t][:, h * P:(h + 1) * P], inverse[:, 4 * t + h, :], half_product[:, 4 * t + h, :], start=True, stop=True)
                        for h in range(H):
                            if lv < 5:
                                last = mm(ps[t][:, h * P:(h + 1) * P], half_product[:, 4 * t + h, :], inverse[:, 4 * t + h, :], start=True, stop=True)
                        last.then_inc(sem("update_product"), 1)
                pe.wait_ge(sem("q_swapped_read"), at(l, "q_swapped_read", 1))
                for t in range(T):
                    pe.wait_ge(sem("inverse_updated"), at(l, "inverse_updated", 11 + t))
                    for h in range(H):
                        n = 4 * t + h
                        mm(ps[2 + t][:, h * P:(h + 1) * P], inverse_t[:, n, :], values_beta[:, n, :], start=True, stop=True)
                        last = mm(ps[4 + t][:, h * P:(h + 1) * P], keys_beta[:, n, :], inverse_t[:, n, :], start=True, stop=True)
                    last.then_inc(sem("solved"), 1)
                def fill(i, half):
                    if half == 0:
                        if i == 0:
                            pe.wait_ge(sem("w_copied"), at(l, "w_copied", 1))
                        if i == 2:
                            pe.wait_ge(sem("new_values"), at(l, "new_values", 1))
                        if i % 2 == 0:
                            unit_in(l, 6 + i // 2)
                    last = channels(6, 2 * i, 4 + i, half=half) if i < 2 else tokens(7, i - 2, i, half=half)
                    if half:
                        last.then_inc(sem("projected"), 1)

                fill(0, 0)
                pe.wait_ge(sem("queries_decayed"), at(l, "queries_decayed", 1))
                for c in range(S // CHUNK):
                    t, lo = c // 2, CHUNK * (c % 2)
                    rows_ = slice(lo, lo + CHUNK)
                    if c:
                        pe.wait_ge(sem("state_updated"), at(l, "state_updated", c))
                        for h in range(H):
                            last = mm(ps[6][rows_, h * P:(h + 1) * P], w_t[:, 4 * t + h, rows_], state[:, h, :], start=True, stop=True)
                        last.then_inc(sem("predicted"), 1)
                        fill(c, 0)
                    pe.wait_ge(sem("new_values"), at(l, "new_values", c + 1))
                    if c < 3:
                        for h in range(H):
                            last = mm(ps[1][:, h * P:(h + 1) * P], keys_end[rows_, 4 * t + h, :], v_new[rows_, 4 * t + h, :], start=True, stop=True)
                        last.then_inc(sem("state_product"), 1)
                    for h in range(H):
                        o_ = ps[7 * (1 - t)][rows_, h * P:(h + 1) * P]
                        if c:
                            mm(o_, qkv[:, h, c * CHUNK:(c + 1) * CHUNK], state[:, h, :], start=True, stop=False)
                        last = mm(o_, intra[rows_, 4 * t + h, rows_], v_new[rows_, 4 * t + h, :], start=(c == 0), stop=True)
                    last.then_inc(sem("output_step"), 1)
                    fill(c, 1)
                    if c == 2:
                        pe.wait_ge(sem("projection_read"), at(l, "projection_read", 6))
                        for i in range(2):
                            mm(ps[4 + i][:, :], table("rot"), att_k[:, 2 * i:2 * i + 2, :].rearrange("p x y -> p (x y)"), start=True, stop=True).then_inc(sem("k_swapped"), 1)
                pe.wait_ge(sem("projection_read"), at(l, "projection_read", 8))
                pe.wait_ge(sem("q_rotated"), at(l, "q_rotated", 1))
                pe.wait_ge(sem("k_rotated"), at(l, "k_rotated", 2))

                def outputs_transposed(t):
                    pe.wait_ge(sem("output_rows"), at(l, "output_rows", t + 1))
                    for h in range(H):
                        last = tr(ps[O_BANKS[t]][:, h * P:(h + 1) * P], u_rows[:, 4 * t + h, :], ident)
                    last.then_inc(sem("output_transposed"), 1)

                def second_outputs():
                    outputs_transposed(1)
                    pe.wait_ge(sem("output_mixed"), at(l, "output_mixed", 1))

                outputs_transposed(0)
                attention(l, LAYER_PAIRS, {2: second_outputs, 7: lambda: pe.wait_ge(sem("output_mixed"), at(l, "output_mixed", 2))})
                rows_product(l, mixT, U_OUT, [4, 4], lambda k: k >= 4 and pe.wait_ge(sem("attended_read"), at(l, "attended_read", k - 3)),
                             lambda: first_tile(at(l, "x_rows", 3)))
                def up(j, t=None):
                    return channels(U_UP + j // 2, j % 2, UP_BANKS[j % 4], t=t, step=2)

                pe.wait_ge(sem("x0_copied"), at(l, "x0_copied", 2))
                for j in range(AHEAD):
                    if j % 2 == 0:
                        unit_in(l, U_UP + j // 2)
                    up(j, 0)
                second_tile(l, 1)
                for j in range(AHEAD):
                    up(j, 1).then_inc(sem("up_product"), 1)
                for j in range(AHEAD, FT):
                    if j % 2 == 0:
                        unit_in(l, U_UP + j // 2)
                    if j >= 4:
                        pe.wait_ge(sem("up_convolved"), at(l, "up_convolved", j - 3))
                    up(j).then_inc(sem("up_product"), 1)
                rows_product(l, hidT, U_DOWN, DOWN_TILES, lambda k: pe.wait_ge(sem("hidden_ready"), at(l, "hidden_ready", k + 1)),
                             lambda: first_tile(at(l, "x_rows", 5)))
            L = DEPTH
            pe.wait_ge(sem("h1_rows"), 1)
            transpose_x(normed_rows, 0, "x0_transposed")
            pe.wait_ge(sem("x0_copied"), at(L, "x0_copied", 2))
            for n in range(AHEAD):
                if n % 2 == 0:
                    unit_in(L, n // 2)
                channels(n // 2, 2 * (n % 2), SECOND_BANKS[n], t=0)
            pe.wait_ge(sem("h1_rows"), 2)
            transpose_x(normed_rows, 1, "x1_transposed")
            pe.wait_ge(sem("x1_copied"), at(L, "x1_copied", 2))
            def project(n):
                u, i = n // 2, n % 2
                if n < AHEAD:
                    last = channels(u, 2 * i, SECOND_BANKS[n], t=1)
                else:
                    if i == 0:
                        unit_in(L, u)
                    if n in SECOND_BANKS_AFTER:
                        pe.wait_ge(sem("projected_2_read"), SECOND_BANKS_AFTER[n])
                    last = tokens(u, i, SECOND_BANKS[n]) if u in (2, 5) else channels(u, 2 * i, SECOND_BANKS[n])
                last.then_inc(sem("projected_2"), 1)

            for n in range(6):
                project(n)
            pe.wait_ge(sem("projected_2_read"), 6)
            steps = {i: lambda n=5 + i: project(n) for i in range(1, 7)}
            attention(L, SECOND_PAIRS, steps | {7: lambda: pe.wait_ge(sem("projected_2_read"), 12)})

            def dilated_then_differential(k):
                if k < 4:
                    pe.wait_ge(sem("attended_read"), at(L, "attended_read", k + 1))
                if k == 4:
                    pe.wait_ge(sem("diff_rows"), 4)
                    for t in range(T):
                        for h in range(H):
                            last = tr(ps[t][:, h * P:(h + 1) * P], diff_out[:, t, h * P:(h + 1) * P], ident)
                    last.then_inc(sem("diff_transposed"), 1)
                    pe.wait_ge(sem("diff_mixed"), 2)
            rows_product(L, mixT, 6, [4, 4], dilated_then_differential, k_first=4)
            for t in range(T):
                pe.wait_ge(sem("h2_rows"), t + 1)
                for kh in range(2):
                    for k in range(4):
                        last = tr(ps[H2_BANKS[2 * t + kh]][:, k * P:(k + 1) * P], normed_rows[:, t, (4 * kh + k) * P:(4 * kh + k + 1) * P], ident)
                    last.then_inc(sem("h2_transposed"), 1)
                pe.wait_ge(sem("h2_copied"), 2 * t + 2)
                for k in range(KT):
                    last = mm(ps[2 + t][:, 0:NE], xT[:, k, t * P:(t + 1) * P], router_w[:, k, :], start=(k == 0), stop=(k == KT - 1))
                last.then_inc(sem("logits"), 1)
            pe.wait_ge(sem("affinities"), 1)
            for t in range(T):
                last = tr(ps[3][0:NE, t * P:(t + 1) * P], router[:, t, :], ident)
            last.then_inc(sem("affinities_transposed"), 1)
            pe.wait_ge(sem("chosen"), 1)
            mm(ps[6][:, :], ones[0:NE, :], spread, start=True, stop=True)
            mm(ps[7][:, 0:NE], rep[:, 0:P], ident[0:NE, 0:NE], start=True, stop=True)
            mm(ps[7][:, NE:2 * NE], rep[:, P:2 * P], ident[0:NE, 0:NE], start=True, stop=True).then_inc(sem("choice_spread"), 1)
            pe.wait_ge(sem("one_hot"), 1)
            for k in range(KT):
                for t in range(T):
                    last = mm(ps[4 + k // 4][:, (k % 4) * P:(k % 4 + 1) * P], normed_rows[:, t, k * P:(k + 1) * P], one_hot[:, t, 0:FIRST], start=(t == 0), stop=(t == T - 1))
                if k % 4 == 3:
                    last.then_inc(sem("chosen_tokens"), 1)

            def other_experts_tokens():
                pe.wait_ge(sem("chosen_tokens_copied"), 2)
                for k in range(KT):
                    if k >= 4:
                        pe.wait_ge(sem("chosen_tokens_copied"), 2 + k - 3)
                    for t in range(T):
                        last = mm(ps[XE_BANKS[k % 4]][:, 0:NE * CAP - FIRST], normed_rows[:, t, k * P:(k + 1) * P], one_hot[:, t, FIRST:NE * CAP], start=(t == 0), stop=(t == T - 1))
                    last.then_inc(sem("chosen_tokens"), 1)

            def expert(e, between=None):
                pe.wait_ge(sem("expert_tokens"), e + 1)
                for k in range(KT):
                    if k == GU_RING and between:
                        between()
                    s_ = k % GU_RING
                    pe.wait_ge(sem(f"gu_in{s_}"), e * (KT // GU_RING * 32) + 32 * (k // GU_RING + 1))
                    for b, (c0, n) in enumerate(PIECES):
                        for q in range(4):
                            c = (q % 2) * HALF + c0
                            last = mm(ps[b][32 * q:32 * q + 32, 0:n], expert_x[:, k, :], gate_up_ring[:, s_, q // 2, c:c + n], start=(k == 0), stop=(k == KT - 1))
                    last.then_inc(sem("gate_up_free"), 1)
                if between:
                    pe.wait_ge(sem("chosen_tokens_copied"), 2 + KT)
                for b, (c0, n) in enumerate(PIECES):
                    pe.wait_ge(sem("expert_hidden"), e * 3 + b + 1)
                    for m in (2 * b, 2 * b + 1):
                        last = tr(ps[HID_BANKS[b]][:, (m % 2) * P:(m % 2 + 1) * P], hidden[:, m, :], ident)
                    last.then_inc(sem("expert_hidden_transposed"), 1)
                for k in range(FT):
                    pe.wait_ge(sem("expert_hidden_copied"), e * 3 + (k // 4 + 1 if k < HT else 3))
                    pe.wait_ge(sem(f"d_in{k % D_RING}"), e * (FT // D_RING * 16) + 16 * (k // D_RING + 1))
                    for q in range(4):
                        last = mm(ps[5][32 * q:32 * q + 32, 0:256], hidden_t[:, k % HT, 32 * (k // HT):32 * (k // HT) + 32], down_ring[:, k % D_RING, 256 * q:256 * q + 256],
                                  start=(k == 0), stop=(k == FT - 1))
                    last.then_inc(sem("down_free"), 1)
                pe.wait_ge(sem("expert_out"), 2 * e + 2)
                for t in range(T):
                    for nh in range(2):
                        last = mm(ps[OUT_BANKS[2 * t + nh]][:, :], placing[:, t * P:(t + 1) * P], out_quarters[:, nh * 512:(nh + 1) * 512], start=True, stop=True)
                    last.then_inc(sem("expert_placed"), 1)

            expert(0, other_experts_tokens)
            with pe.Fori(1, NE) as e:
                expert(e)

        @block.scalar
        def _(act):
            f = nc.scalar.activation

            def copy_x1T(l, n):
                act.wait_ge(sem("x1_transposed"), at(l, "x1_transposed", 2 * n + 2))
                f(xT[:, 4:8, P:2 * P], ps[7][:, :].rearrange("p (x y) -> p x y", y=P), ACT.Copy).then_inc(sem("x1_copied"), 1)

            def attention(l, pairs, at_step={}):
                n = 2 * len(pairs)
                for i in range(n + 5):
                    if i < n:
                        E = attention_operands(pairs[i // 2][0])[3]
                        act.wait_ge(sem("scores_biased"), at(l, "scores_biased", i + 1))
                        n_ = keys(pairs[i // 2][0], i % 2)
                        for m in range(2):
                            last = f(E[:, i % 4, m, 0:n_], E[:, i % 4, m, 0:n_], ACT.Exp, bias=neg_max[:, i % 4, m:m + 1], accum_out=exp_sum[:, i % 4, m:m + 1])
                        last.then_inc(sem("exps"), 1)
                    if i in at_step:
                        at_step[i]()
                    if 2 <= i < n + 2:
                        b = i - 2
                        kind, pr = pairs[b // 2]
                        PT = attention_operands(kind)[4]
                        act.wait_ge(sem("probs_transposed"), at(l, "probs_transposed", b + 1))
                        if b // 2 >= 2:
                            act.wait_ge(sem("attended"), at(l, "attended", b // 2 - 1))
                        w = 2 if kind == "diff" else 4
                        kts = T * P // keys(kind, b % 2)
                        f(PT[:, b // 2 % 2, 0:w:kts, (b % 2) * P:(b % 2 + 1) * P],
                          ps[TR[b % 2]][:, 0:w * P].rearrange("p (x y) -> p x y", y=P)[:, ::kts, :], ACT.Copy).then_inc(sem("probs_copied"), 1)
                    if i >= 6 and i % 2 == 0:
                        pi = (i - 6) // 2
                        kind, pr = pairs[pi]
                        if kind != "diff":
                            act.wait_ge(sem("attended"), at(l, "attended", pi + 1))
                            f(mixT[:, 4 + pr, :], ps[PV[pi % 2]][:, 0:S], ACT.Copy).then_inc(sem("attended_read"), 1)

            with act.Fori(0, DEPTH) as l:
                copy_x1T(l, 0)
                act.wait_ge(sem("conv_weights"), at(l, "conv_weights", 1))
                for i in range(7):
                    if i < 6:
                        act.wait_ge(sem("projected"), at(l, "projected", i + 1))
                        for j in range(2):
                            c = 2 * i + j
                            last = f(qkv[:, c, :], ps[IN_BANKS[i]][:, j * S:(j + 1) * S], ACT.Copy, scale=conv_w[:, 36 + c:37 + c])
                        last.then_inc(sem("last_tap"), 1)
                    if i:
                        act.wait_ge(sem("convolved"), at(l, "convolved", i))
                        v = qkv[:, 2 * i - 2:2 * i, :]
                        f(v, v, ACT.Silu).then_inc(sem("channels_silu"), 1)
                for i in range(4):
                    act.wait_ge(sem("channels_silu"), at(l, "channels_silu", i + 1))
                    f(qk_squares[:, i, :], qkv[:, 2 * i:2 * i + 2, :].rearrange("p x y -> p (x y)"), ACT.Square).then_inc(sem("squares"), 1)
                for i in (6, 7):
                    act.wait_ge(sem("projected"), at(l, "projected", i + 1))
                    f(z_gate[:, i % 2, :], ps[IN_BANKS[i]][:, :], ACT.Silu).then_inc(sem("projection_read"), 1)
                act.wait_ge(sem("gate_inputs"), at(l, "gate_inputs", 1))
                act.wait_ge(sem("small_in"), l * 48 + 48)
                f(exp_neg_b, b_logit, ACT.Exp, scale=-1.0)
                f(exp_neg_abs_a, neg_abs_a, ACT.Exp)
                f(exp_a_log, a_log, ACT.Exp)
                act.drain()
                f(log1p_a, exp_neg_abs_a, ACT.Ln, bias=1.0).then_inc(sem("gate_exps"), 1)
                act.wait_ge(sem("norm_sums_read"), at(l, "norm_sums_read", 1))
                f(norm_log, norm_sq, ACT.Ln).then_inc(sem("norm_logs"), 1)
                def copy_qb(i):
                    act.wait_ge(sem("projected"), at(l, "projected", i + 1))
                    f(att_q[:, 2 * (i % 2):2 * (i % 2) + 2, :].rearrange("p x y -> p (x y)"), ps[IN_BANKS[i]][:, :], ACT.Copy).then_inc(sem("projection_read"), 1)
                copy_qb(8)
                act.wait_ge(sem("decay_arguments"), at(l, "decay_arguments", 1))
                for t in range(T):
                    last = f(query_decay[:, 4 * t:4 * t + 4, :].rearrange("p x y -> p (x y)"), ps[t][:, :], ACT.Exp)
                last.then_inc(sem("query_decays"), 1)
                f(key_decay, decay_arg, ACT.Exp)
                f(chunk_decay, chunk_sum, ACT.Exp)
                f(end_decay, end_arg, ACT.Exp).then_inc(sem("token_decays"), 1)
                for n in range(8):
                    last = f(decay[:, n, :], decay[:, n, :], ACT.Exp, bias=decay_arg[:, n:n + 1])
                last.then_inc(sem("pair_decays"), 1)
                copy_qb(9)
                for n in range(8):
                    last = f(decay_t[:, n, :], decay_t[:, n, :], ACT.Exp, bias=decay_t_arg[:, n:n + 1])
                last.then_inc(sem("pair_decays"), 1)
                act.wait_ge(sem("decay_logs"), at(l, "decay_logs", 1))
                for t in range(T):
                    act.wait_ge(sem("kv_rows"), at(l, "kv_rows", t + 3))
                    for h in range(H):
                        last = f(values_beta[:, 4 * t + h, :], ps[4 + t][:, h * P:(h + 1) * P], ACT.Copy, scale=beta[:, t, h:h + 1])
                last.then_inc(sem("values_scaled"), 1)
                for lv in range(1, 6):
                    if lv == 3:
                        for i in range(2):
                            act.wait_ge(sem("q_swapped"), at(l, "q_swapped", 1))
                            last = f(q_swapped[:, i, :], ps[2 + i][:, :], ACT.Copy)
                        last.then_inc(sem("q_swapped_read"), 1)
                    for t in range(T):
                        n = 2 * lv + t
                        act.wait_ge(sem("x_product"), at(l, "x_product", n + 1))
                        f(half_product[:, 4 * t:4 * t + 4, :].rearrange("p x y -> p (x y)"), ps[4 + t][:, :], ACT.Copy).then_inc(sem("x_copied"), 1)
                for t in range(T):
                    act.wait_ge(sem("solved"), at(l, "solved", t + 1))
                    last = f(w_t[:, 4 * t:4 * t + 4, :].rearrange("p x y -> p (x y)"), ps[4 + t][:, :], ACT.Copy)
                last.then_inc(sem("w_copied"), 1)
                for i in (10, 11):
                    act.wait_ge(sem("projected"), at(l, "projected", i + 1))
                    f(att_k[:, 2 * (i % 2):2 * (i % 2) + 2, :].rearrange("p x y -> p (x y)"), ps[4 + i % 2][:, :], ACT.Copy).then_inc(sem("projection_read"), 1)
                for t in range(T):
                    act.wait_ge(sem("output_step"), at(l, "output_step", 2 * t + 2))
                    for h in range(H):
                        n = 4 * t + h
                        f(half_product[:, n, :], ps[7 * (1 - t)][:, h * P:(h + 1) * P], ACT.Square, accum_out=out_sq[:, n:n + 1])
                    act.drain()
                    f(out_root[:, 4 * t:4 * t + 4], out_sq[:, 4 * t:4 * t + 4], ACT.Sqrt, scale=1.0 / DK, bias=norm_eps).then_inc(sem("output_root"), 1)
                    if t == 0:
                        for i in (12, 13):
                            act.wait_ge(sem("projected"), at(l, "projected", i + 1))
                            f(att_v[:, i % 2, :], ps[2 + i % 2][:, :], ACT.Copy).then_inc(sem("projection_read"), 1)

                def outputs_copied(t):
                    act.wait_ge(sem("output_transposed"), at(l, "output_transposed", t + 1))
                    f(mixT[:, 0:4, t * P:(t + 1) * P], ps[O_BANKS[t]][:, :].rearrange("p (x y) -> p x y", y=P), ACT.Copy).then_inc(sem("output_mixed"), 1)
                outputs_copied(0)
                attention(l, LAYER_PAIRS, {2: lambda: outputs_copied(1)})

                def layer_norm_root(n, t):
                    act.wait_ge(sem("norm_stats"), at(l, "norm_stats", 2 * n + t + 1))
                    f(inv_std[:, t, :], mean_var[:, t, 1:2], ACT.Sqrt, bias=ln_eps).then_inc(sem("norm_root"), 1)
                for t in range(T):
                    layer_norm_root(0, t)
                copy_x1T(l, 1)
                for j in range(FT + 1):
                    if j < FT:
                        act.wait_ge(sem("up_product"), at(l, "up_product", j + 1))
                        if j >= 3:
                            act.wait_ge(sem("hidden_ready"), at(l, "hidden_ready", j - 2))
                        for gv in range(2):
                            c = gv * FT + j
                            last = f(ff_conv[:, j % 3, gv, :], ps[UP_BANKS[j % 4]][:, gv * S:(gv + 1) * S], ACT.Identity,
                                     scale=conv_w[:, 136 + c:137 + c], bias=conv_w[:, 180 + c:181 + c])
                        last.then_inc(sem("up_last_tap"), 1)
                    if j:
                        act.wait_ge(sem("up_convolved"), at(l, "up_convolved", j))
                        f(ff_conv[:, (j - 1) % 3, 0, :], ff_conv[:, (j - 1) % 3, 0, :], ACT.Silu).then_inc(sem("gate_silu"), 1)
                for t in range(T):
                    layer_norm_root(1, t)
            L = DEPTH
            def rms(n, t):
                if n == 0:
                    act.wait_ge(sem("x_rows"), at(L, "x_rows", t + 1))
                elif n == 1:
                    act.wait_ge(sem("second_rows"), t + 1)
                else:
                    act.wait_ge(sem("expert_added"), NE * T - T + t + 1)
                squares = (xT if (n, t) == (1, 0) else mixT).rearrange("p x y -> p (x y)")[:, 0:D]
                f(squares, x[:, t, :], ACT.Square, accum_out=sum_sq[:, t:t + 1])
                act.drain()
                f(inv_rms[:, t:t + 1], sum_sq[:, t:t + 1], ACT.Sqrt, scale=1.0 / D, bias=norm_eps).then_inc(sem("rms_root"), 1)
            for t in range(T):
                rms(0, t)
            copy_x1T(L, 0)
            def copy_projected(n):
                u, i = n // 2, n % 2
                dst = (qaT, kaT, va, qdT, kdT, vd)[u]
                act.wait_ge(sem("projected_2"), n + 1)
                d_ = dst[:, i, :] if u in (2, 5) else dst[:, 2 * i:2 * i + 2, :].rearrange("p x y -> p (x y)")
                f(d_, ps[SECOND_BANKS[n]][:, :], ACT.Copy).then_inc(sem("projected_2_read"), 1)

            for n in range(6):
                copy_projected(n)
            act.wait_ge(sem("lambda_dots"), 1)
            f(lambda_parts[:, 2:4], lambda_parts[:, 0:2], ACT.Exp).then_inc(sem("lambda_exps"), 1)
            attention(L, SECOND_PAIRS, {i: lambda n=4 + i: copy_projected(n) for i in range(2, 8)})
            act.wait_ge(sem("diff_sums"), 1)
            f(lambda_parts, lambda_parts, ACT.Sqrt, scale=1.0 / P, bias=subln_eps).then_inc(sem("diff_root"), 1)
            for t in range(T):
                act.wait_ge(sem("diff_transposed"), 1)
                f(mixT[:, 0:4, t * P:(t + 1) * P], ps[t][:, :].rearrange("p (x y) -> p x y", y=P), ACT.Copy).then_inc(sem("diff_mixed"), 1)
            for t in range(T):
                rms(1, t)
                for kh in range(2):
                    act.wait_ge(sem("h2_transposed"), 2 * t + kh + 1)
                    f(xT[:, 4 * kh:4 * kh + 4, t * P:(t + 1) * P], ps[H2_BANKS[2 * t + kh]][:, :].rearrange("p (x y) -> p x y", y=P), ACT.Copy).then_inc(sem("h2_copied"), 1)
            act.wait_ge(sem("router_rows"), 1)
            for t in range(T):
                last = f(router[:, t, :], router[:, t, :], ACT.Exp, bias=rmax[:, t:t + 1], accum_out=rsum[:, t:t + 1])
            last.then_inc(sem("router_exps"), 1)
            for i in range(2):
                act.wait_ge(sem("chosen_tokens"), i + 1)
                f(chosen_x_t[:, 4 * i:4 * i + 4, 0:FIRST], ps[4 + i][:, :].rearrange("p (x y) -> p x y", y=P), ACT.Copy).then_inc(sem("chosen_tokens_copied"), 1)
            for k in range(KT):
                act.wait_ge(sem("chosen_tokens"), 2 + k + 1)
                f(chosen_x_t[:, k, FIRST:NE * CAP], ps[XE_BANKS[k % 4]][:, 0:NE * CAP - FIRST], ACT.Copy).then_inc(sem("chosen_tokens_copied"), 1)
            with act.Fori(0, NE) as e:
                for b, (c0, n) in enumerate(PIECES):
                    act.wait_ge(sem("gate_up_free"), GU_RING + e * KT + KT)
                    f(expert_gate[0:64, c0:c0 + n], ps[b][0:64, 0:n], ACT.Silu).then_inc(sem("expert_silu"), 1)
                for b, (c0, n) in enumerate(PIECES):
                    act.wait_ge(sem("expert_hidden_transposed"), e * 3 + b + 1)
                    last = f(hidden_t[:, 4 * b:4 * b + 4, :], ps[HID_BANKS[b]][:, 0:S].rearrange("p (x y) -> p x y", y=64), ACT.Copy)
                    last.then_inc(sem("expert_hidden_copied"), 1)
                act.wait_ge(sem("down_free"), e * FT + FT + D_RING)
                for q in range(2):
                    last = f(out_quarters[32 * q:32 * q + 32, 256 * q:256 * q + 256], ps[5][32 * q:32 * q + 32, 0:256], ACT.Copy)
                last.then_inc(sem("expert_out"), 1)
            for t in range(T):
                rms(2, t)

        @block.vector
        def _(v):
            w = nc.vector

            def attention(l, pairs, at_step={}):
                n = 2 * len(pairs)
                for i in range(n + 5):
                    if i in at_step:
                        at_step[i]()
                    if i < n:
                        kind, pr = pairs[i // 2]
                        E, t = attention_operands(kind)[3], i % 2
                        v.wait_ge(sem("scores"), at(l, "scores", i + 1))
                        if i >= 4:
                            v.wait_ge(sem("probs_transposed"), at(l, "probs_transposed", i - 3))
                        n_ = keys(kind, t)
                        for m in range(2):
                            if kind == "causal":
                                bias = table("causal")
                            else:
                                bias = bias12[:, pr if kind == "diff" else H + 2 * pr + m, :]
                            w.scalar_tensor_tensor(E[:, i % 4, m, 0:n_], ps[score_banks(kind, i)[m]][:, 0:n_], DH ** -0.5, bias[:, P - P * t:P - P * t + n_], ALU.mult, ALU.add)
                        v.drain()
                        w.tensor_reduce(neg_max[:, i % 4, :], E[:, i % 4, :, 0:n_], AX.X, ALU.max, negate=True).then_inc(sem("scores_biased"), 1)
                    if 1 <= i <= n:
                        b = i - 1
                        kind, pr = pairs[b // 2]
                        E = attention_operands(kind)[3]
                        v.wait_ge(sem("exps"), at(l, "exps", b + 1))
                        w.reciprocal(inv_sum[:, b % 4, :], exp_sum[:, b % 4, :])
                        v.drain()
                        if kind == "diff":
                            w.tensor_scalar(inv_sum[:, b % 4, 1:2], inv_sum[:, b % 4, 1:2], neg_lambda, None, ALU.mult)
                            v.drain()
                            w.tensor_scalar(E[:, b % 4, 1, :], E[:, b % 4, 1, :], inv_sum[:, b % 4, 1:2], None, ALU.mult)
                            v.drain()
                            w.scalar_tensor_tensor(E[:, b % 4, 0, :], E[:, b % 4, 0, :], inv_sum[:, b % 4, 0:1], E[:, b % 4, 1, :], ALU.mult, ALU.add).then_inc(sem("probs"), 1)
                        else:
                            n_ = keys(kind, b % 2)
                            for m in range(2):
                                last = w.tensor_scalar(E[:, b % 4, m, 0:n_], E[:, b % 4, m, 0:n_], inv_sum[:, b % 4, m:m + 1], None, ALU.mult)
                            last.then_inc(sem("probs"), 1)
                    if i >= 6 and i % 2 == 0:
                        pi = (i - 6) // 2
                        kind, pr = pairs[pi]
                        if kind == "diff":
                            v.wait_ge(sem("attended"), at(l, "attended", pi + 1))
                            w.tensor_copy(diff_out[:, :, pr * P:(pr + 1) * P], ps[PV[pi % 2]][:, 0:S].rearrange("p (t n) -> p t n", n=P)).then_inc(sem("diff_read"), 1)

            v.wait_ge(sem("bias_product"), 1)
            w.tensor_copy(distance_bias[0:BIAS_HEADS, :], ps[3][0:BIAS_HEADS, :]).then_inc(sem("bias_copied"), 1)
            v.wait_ge(sem("x_in"), 16)
            v.nop().then_inc(sem("x_rows"), 2)

            def copy_x0T(value):
                v.wait_ge(sem("x0_transposed"), value)
                for kh in range(2):
                    last = w.tensor_copy(xT[:, 4 * kh:4 * kh + 4, 0:P], ps[4 + kh][:, :].rearrange("p (x y) -> p x y", y=P))
                last.then_inc(sem("x0_copied"), 1)

            def copy_x1T(l, n):
                v.wait_ge(sem("x1_transposed"), at(l, "x1_transposed", 2 * n + 1))
                w.tensor_copy(xT[:, 0:4, P:2 * P], ps[6][:, :].rearrange("p (x y) -> p x y", y=P)).then_inc(sem("x1_copied"), 1)

            def layer_norm(l, n):
                v.wait_ge(sem(("ln1_in", "ln2_in")[n]), l * 32 + 32)
                for t in range(T):
                    if t == 0:
                        v.wait_ge(sem("rows_t0"), at(l, "rows_t0", n + 1))
                    else:
                        v.wait_ge(sem("rows_used"), (l + 1) * ROW_UNITS + (ROW_UNITS if n else 2))
                    for nh in range(2):
                        xs = x[:, t, nh * 512:(nh + 1) * 512]
                        w.scalar_tensor_tensor(xs, xs, ALPHA, ps[ROWS_BANKS[2 * t + nh]][:, :], ALU.mult, ALU.add)
                    v.drain()
                    for nh in range(2):
                        w.bn_stats(stats[:, t, nh, :], x[:, t, nh * 512:(nh + 1) * 512])
                    v.drain()
                    w.bn_aggr(mean_var[:, t, :], stats[:, t, :, :]).then_inc(sem("norm_stats"), 1)
                    v.drain()
                    w.scalar_tensor_tensor(x[:, t, :], x[:, t, :], mean_var[:, t, 0:1], ln_g, ALU.subtract, ALU.mult)
                    v.wait_ge(sem("norm_root"), at(l, "norm_root", 2 * n + t + 1))
                    w.reciprocal(inv_std[:, t, :], inv_std[:, t, :])
                    v.drain()
                    w.scalar_tensor_tensor(x[:, t, :], x[:, t, :], inv_std[:, t, :], ln_b, ALU.mult, ALU.add).then_inc(sem("x_rows"), 1)
                    if t == 0:
                        copy_x0T(at(l, "x0_transposed", n + 2))

            copy_x0T(1)
            with v.Fori(0, DEPTH) as l:
                copy_x1T(l, 0)
                v.wait_ge(sem("conv_transposed"), at(l, "conv_transposed", 1))
                w.tensor_copy(conv_w, ps[2][:, 0:224]).then_inc(sem("conv_weights"), 1)
                v.drain()
                for i in range(6):
                    v.wait_ge(sem("last_tap"), at(l, "last_tap", i + 1))
                    for s in range(1, TAPS):
                        for j in range(2):
                            c = 2 * i + j
                            last = w.scalar_tensor_tensor(qkv[:, c, s:S], ps[IN_BANKS[i]][:, j * S:(j + 1) * S - s], conv_w[:, 12 * (3 - s) + c:12 * (3 - s) + c + 1],
                                                          qkv[:, c, s:S], ALU.mult, ALU.add)
                        if s < TAPS - 1:
                            v.drain()
                    last.then_inc(sem("convolved"), 1)
                v.wait_ge(sem("const_in"), 16)
                v.wait_ge(sem("gate_logits"), at(l, "gate_logits", 1))
                v.wait_ge(sem("small_in"), l * 48 + 48)
                ab = ps[2][:, 0:16].rearrange("p (t n) -> p t n", n=8)
                w.tensor_add(a_logit, ab[:, :, 0:H], dt_bias.unsqueeze(1).broadcast_to([P, T, H]))
                w.tensor_copy(b_logit, ab[:, :, H:2 * H])
                v.drain()
                w.tensor_scalar(neg_abs_a, a_logit, -1.0, None, ALU.mult)
                v.drain()
                w.tensor_tensor(neg_abs_a, neg_abs_a, a_logit, ALU.min).then_inc(sem("gate_inputs"), 1)
                v.wait_ge(sem("norm_sums"), at(l, "norm_sums", 1))
                w.tensor_scalar(norm_sq[:, 0:8], ps[3][:, 0:8], NORM_EPS, None, ALU.add)
                w.tensor_scalar(norm_sq[:, 8:16], ps[3][:, 8:16], NORM_EPS, DK, ALU.add, ALU.mult).then_inc(sem("norm_sums_read"), 1)
                v.wait_ge(sem("gate_exps"), at(l, "gate_exps", 1))
                w.scalar_tensor_tensor(g, a_logit, 0.0, log1p_a, ALU.max, ALU.add)
                w.tensor_scalar(beta, exp_neg_b, 1.0, None, ALU.add)
                v.drain()
                w.scalar_tensor_tensor(g, g, -1.0, exp_a_log.unsqueeze(1).broadcast_to([P, T, H]), ALU.mult, ALU.mult)
                w.reciprocal(beta, beta)
                v.drain()
                w.tensor_copy(g_spread, g.rearrange("p x y -> p (x y)").unsqueeze(2).broadcast_to([P, 8, P]))
                for c in range(2):
                    w.tensor_scalar(g_by_chunk[:, c, :], g.rearrange("p x y -> p (x y)"), table("cum")[:, CHUNK * c + CHUNK - 1:CHUNK * c + CHUNK], None, ALU.mult)
                v.wait_ge(sem("norm_logs"), at(l, "norm_logs", 1))
                w.tensor_scalar(norm_log[:, 0:8], norm_log[:, 0:8], 0.5, None, ALU.mult)
                w.tensor_scalar(norm_log[:, 8:16], norm_log[:, 8:16], -0.5, None, ALU.mult)
                v.drain()
                w.tensor_copy(norm_log_spread, norm_log.unsqueeze(2).broadcast_to([P, 16, P])).then_inc(sem("decay_logs"), 1)
                v.wait_ge(sem("cumulated"), at(l, "cumulated", 1))
                w.tensor_sub(decay_arg, ps[4][:, 0:8], norm_log[:, 0:8])
                w.scalar_tensor_tensor(decay_t_arg, ps[4][:, 0:8], -1.0, norm_log[:, 0:8], ALU.mult, ALU.subtract)
                w.tensor_copy(chunk_sum, ps[4][:, 8:24])
                v.drain()
                for c in range(2):
                    lo = CHUNK * c
                    w.tensor_add(end_arg[lo:lo + CHUNK, :], chunk_sum[lo:lo + CHUNK, 8 * c:8 * c + 8], decay_t_arg[lo:lo + CHUNK, :])
                for t in range(T):
                    bias = lambda name: table(name).unsqueeze(1).broadcast_to([P, H, P])
                    w.scalar_tensor_tensor(decay[:, 4 * t:4 * t + 4, :], ps[2 + t][:, :].rearrange("p (h n) -> p h n", n=P), -1.0, bias("neg_strict"), ALU.mult, ALU.add)
                    w.tensor_add(decay_t[:, 4 * t:4 * t + 4, :], ps[t][:, :].rearrange("p (h n) -> p h n", n=P), bias("neg_incl_t"))
                v.drain().then_inc(sem("decay_arguments"), 1)
                v.wait_ge(sem("token_decays"), at(l, "token_decays", 1))
                w.tensor_mul(beta_decay, beta.rearrange("p x y -> p (x y)"), key_decay)
                v.drain()
                for n in range(8):
                    t, h = n // 4, n % 4
                    if h == 0:
                        v.wait_ge(sem("kv_rows"), at(l, "kv_rows", t + 1))
                    w.tensor_scalar(keys_end[:, n, :], ps[6 + t][:, h * P:(h + 1) * P], end_decay[:, n:n + 1], None, ALU.mult)
                    last = w.tensor_scalar(keys_beta[:, n, :], ps[6 + t][:, h * P:(h + 1) * P], beta_decay[:, n:n + 1], None, ALU.mult)
                last.then_inc(sem("keys_scaled"), 1)
                def level(lv, t):
                    w.tensor_mul(level_part[:, 4 * t:4 * t + 4, :], A_all[:, 4 * t:4 * t + 4, :], table(f"level{lv}").unsqueeze(1).broadcast_to([P, H, P])).then_inc(sem("level_masked"), 1)
                v.wait_ge(sem("pair_decays"), at(l, "pair_decays", 1))
                for t in range(T):
                    v.wait_ge(sem("key_products"), at(l, "key_products", t + 1))
                    for h in range(H):
                        n = 4 * t + h
                        w.scalar_tensor_tensor(A_all[:, n, :], ps[t][:, h * P:(h + 1) * P], beta[:, t, h:h + 1], decay[:, n, :], ALU.mult, ALU.mult)
                    v.drain()
                    level(0, t)
                def tile(y, t):
                    return y[:, 4 * t:4 * t + 4, :]

                def in_heads(bank):
                    return ps[bank][:, :].rearrange("p (h n) -> p h n", n=P)

                identities = ident.unsqueeze(1).broadcast_to([P, H, P])
                v.drain()
                for t in range(T):
                    w.tensor_sub(tile(inverse, t), identities, tile(level_part, t))
                    v.wait_ge(sem("x_product"), at(l, "x_product", t + 1))
                    w.tensor_sub(tile(inverse_t, t), identities, in_heads(4 + t)).then_inc(sem("inverse_updated"), 1)
                    v.drain()
                    level(1, t)
                v.wait_ge(sem("key_products"), at(l, "key_products", 3))
                v.wait_ge(sem("pair_decays"), at(l, "pair_decays", 2))
                for t in range(T):
                    last = w.tensor_mul(tile(decay_t, t), in_heads(2 + t), tile(decay_t, t))
                last.then_inc(sem("intra_scores"), 1)
                for lv in range(1, 6):
                    for t in range(T):
                        n = 2 * lv + t
                        if lv < 5:
                            v.wait_ge(sem("x_product"), at(l, "x_product", n + 1))
                            level(lv + 1, t)
                        v.wait_ge(sem("update_product"), at(l, "update_product", n - 1))
                        last = w.tensor_sub(tile(inverse_t, t), tile(inverse_t, t), in_heads(6 + t))
                        if lv < 5:
                            last = w.tensor_sub(tile(inverse, t), tile(inverse, t), in_heads(t))
                        last.then_inc(sem("inverse_updated"), 1)
                for t in range(T):
                    v.wait_ge(sem("solved"), at(l, "solved", t + 1))
                    last = w.tensor_copy(u_rows[:, 4 * t:4 * t + 4, :].rearrange("p x y -> p (x y)"), ps[2 + t][:, :])
                v.drain()
                for c in range(S // CHUNK):
                    t, lo = c // 2, CHUNK * (c % 2)
                    rows_ = slice(lo, lo + CHUNK)
                    if c == 0:
                        v.nop().then_inc(sem("new_values"), 1)
                    else:
                        v.wait_ge(sem("predicted"), at(l, "predicted", c))
                        vv = v_new[rows_, 4 * t:4 * t + 4, :].rearrange("p x y -> p (x y)")
                        w.tensor_sub(vv, vv, ps[6][rows_, :]).then_inc(sem("new_values"), 1)
                    if c < 3:
                        v.wait_ge(sem("state_product"), at(l, "state_product", c + 1))
                        if c:
                            v.wait_ge(sem("output_step"), at(l, "output_step", c + 1))
                            for h in range(H):
                                last = w.scalar_tensor_tensor(state[:, h, :], state[:, h, :], chunk_decay[:, 8 * (c % 2) + 4 * t + h:8 * (c % 2) + 4 * t + h + 1],
                                                              ps[1][:, h * P:(h + 1) * P], ALU.mult, ALU.add)
                        else:
                            last = w.tensor_copy(state.rearrange("p x y -> p (x y)"), ps[1][:, :])
                        last.then_inc(sem("state_updated"), 1)
                        v.drain()
                def outputs(t):
                    v.wait_ge(sem("output_root"), at(l, "output_root", t + 1))
                    w.reciprocal(out_root[:, 4 * t:4 * t + 4], out_root[:, 4 * t:4 * t + 4])
                    v.drain()
                    for h in range(H):
                        last = w.scalar_tensor_tensor(u_rows[:, 4 * t + h, :], ps[7 * (1 - t)][:, h * P:(h + 1) * P], out_root[:, 4 * t + h:4 * t + h + 1],
                                                      z_gate[:, t, h * P:(h + 1) * P], ALU.mult, ALU.mult)
                    last.then_inc(sem("output_rows"), 1)

                for i in range(2):
                    v.wait_ge(sem("k_swapped"), at(l, "k_swapped", i + 1))
                    src = att_k[:, 2 * i:2 * i + 2, :]
                    r3 = rot_tmp.rearrange("p (x y) -> p x y", y=S)
                    w.tensor_mul(r3, ps[4 + i][:, :].rearrange("p (x y) -> p x y", y=S), table("sin").unsqueeze(1).broadcast_to([P, 2, S]))
                    w.tensor_mul(src, src, table("cos").unsqueeze(1).broadcast_to([P, 2, S]))
                    v.drain()
                    w.tensor_add(src, src, r3)
                    v.drain().then_inc(sem("k_rotated"), 1)
                v.wait_ge(sem("z_gated"), at(l, "z_gated", 1))
                outputs(0)
                attention(l, LAYER_PAIRS, {1: lambda: outputs(1)})
                layer_norm(l, 0)
                copy_x1T(l, 1)
                for j in range(FT + 1):
                    if j < FT:
                        v.wait_ge(sem("up_last_tap"), at(l, "up_last_tap", j + 1))
                        for s in range(1, FTAPS):
                            for gv in range(2):
                                c = (2 - s) * 2 * FT + gv * FT + j
                                last = w.scalar_tensor_tensor(ff_conv[:, j % 3, gv, s:S], ps[UP_BANKS[j % 4]][:, gv * S:(gv + 1) * S - s], conv_w[:, 48 + c:49 + c],
                                                              ff_conv[:, j % 3, gv, s:S], ALU.mult, ALU.add)
                            if s < FTAPS - 1:
                                v.drain()
                        last.then_inc(sem("up_convolved"), 1)
                        v.drain()
                    if j:
                        v.wait_ge(sem("gate_silu"), at(l, "gate_silu", j))
                        w.tensor_mul(hidT[:, j - 1, :], ff_conv[:, (j - 1) % 3, 0, :], ff_conv[:, (j - 1) % 3, 1, :]).then_inc(sem("hidden_ready"), 1)
                layer_norm(l, 1)

            def rms(n, t, dst, done):
                if t == 0:
                    v.wait_ge(sem(f"gain_in{n + 1}"), 16)
                v.wait_ge(sem("rms_root"), 2 * n + t + 1)
                w.reciprocal(inv_rms[:, t:t + 1], inv_rms[:, t:t + 1])
                v.drain()
                w.scalar_tensor_tensor(dst[:, t, :], x[:, t, :], inv_rms[:, t:t + 1], gain, ALU.mult, ALU.mult).then_inc(sem(done), 1)

            L = DEPTH
            rms(0, 0, normed_rows, "h1_rows")
            rms(0, 1, normed_rows, "h1_rows")
            copy_x0T(at(L, "x0_transposed", 2))
            copy_x1T(L, 0)
            v.wait_ge(sem("second_small_in"), 96)
            for n in range(2):
                w.tensor_mul(lambda_vectors[:, 2 * n, :], lambda_vectors[:, 2 * n, :], lambda_vectors[:, 2 * n + 1, :])
            w.tensor_scalar(subln_gain, subln_gain, 1.0 - LAMBDA_INIT, None, ALU.mult)
            v.drain()
            for n in range(2):
                last = w.tensor_reduce(lambda_parts[:, n:n + 1], lambda_vectors[:, 2 * n, :], AX.X, ALU.add)
            last.then_inc(sem("lambda_dots"), 1)
            v.wait_ge(sem("lambda_exps"), 1)
            w.tensor_sub(neg_lambda, lambda_parts[:, 3:4], lambda_parts[:, 2:3])
            v.drain()
            w.tensor_scalar(neg_lambda, neg_lambda, -LAMBDA_INIT, None, ALU.add)
            v.drain()
            v.wait_ge(sem("bias_back"), 16 * BIAS_HEADS)
            attention(L, SECOND_PAIRS)
            diff_squares = scores_2.rearrange("p x y z -> p (x y z)")[:, 0:1024]
            diff_sq = lambda_parts
            v.wait_ge(sem("probs_transposed"), at(L, "probs_transposed", 2 * len(SECOND_PAIRS)))
            v.drain()
            w.tensor_mul(diff_squares, diff_out.rearrange("p x y -> p (x y)"), diff_out.rearrange("p x y -> p (x y)"))
            v.drain()
            w.tensor_reduce(diff_sq, diff_squares.rearrange("p (a n) -> p a n", n=P), AX.X, ALU.add).then_inc(sem("diff_sums"), 1)
            v.wait_ge(sem("diff_root"), 1)
            w.reciprocal(diff_sq, diff_sq)
            v.drain()
            for t in range(T):
                for h in range(H):
                    o_ = diff_out[:, t, h * P:(h + 1) * P]
                    last = w.scalar_tensor_tensor(o_, o_, diff_sq[:, 4 * t + h:4 * t + h + 1], subln_gain, ALU.mult, ALU.mult)
            last.then_inc(sem("diff_rows"), 4)
            for t in range(T):
                if t == 0:
                    v.wait_ge(sem("rows_t0"), at(L, "rows_t0", 1))
                else:
                    v.wait_ge(sem("rows_used"), (DEPTH + 1) * ROW_UNITS + 2)
                for nh in range(2):
                    xs = x[:, t, nh * 512:(nh + 1) * 512]
                    last = w.tensor_add(xs, xs, ps[ROWS_BANKS[2 * t + nh]][:, :])
                last.then_inc(sem("second_rows"), 1)
                v.drain()
                rms(1, t, normed_rows, "h2_rows")
            for t in range(T):
                v.wait_ge(sem("logits"), t + 1)
                lg = ps[2 + t][:, 0:NE]
                w.tensor_copy(router[:, t, :], lg)
                w.tensor_reduce(rmax[:, t:t + 1], lg, AX.X, ALU.max, negate=True)
            v.drain().then_inc(sem("router_rows"), 1)
            v.wait_ge(sem("router_exps"), 1)
            w.reciprocal(rsum, rsum)
            v.drain()
            w.tensor_mul(router, router, rsum.unsqueeze(2).broadcast_to([P, T, NE])).then_inc(sem("affinities"), 1)
            v.wait_ge(sem("affinities_transposed"), 1)
            w.tensor_copy(affT, ps[3][0:NE, 0:S])
            v.drain()
            for r in range(CAP // 8):
                cur = affT if r % 2 == 0 else affW
                nxt = affW if r % 2 == 0 else affT
                w.max(topv[:, 8 * r:8 * r + 8], cur)
                v.drain()
                w.max_index(topidx[:, 8 * r:8 * r + 8], topv[:, 8 * r:8 * r + 8], cur)
                w.match_replace(nxt, topv[:, 8 * r:8 * r + 8], cur, -1.0)
                v.drain()
            w.tensor_copy(topf, topidx)
            v.drain()
            w.tensor_mul(spread.rearrange("p (e s) -> p e s", s=CAP), topf.unsqueeze(1).broadcast_to([NE, NE, CAP]), table("own")[0:NE, :].rearrange("p (e s) -> p e s", s=CAP))
            w.tensor_copy(rep[:, 0:P].rearrange("p (q s) -> p q s", s=CAP), topf.unsqueeze(1).broadcast_to([NE, 4, CAP]))
            w.tensor_copy(rep[:, P:2 * P].rearrange("p (q s) -> p q s", s=CAP), topv.unsqueeze(1).broadcast_to([NE, 4, CAP]))
            v.drain().then_inc(sem("chosen"), 1)
            v.wait_ge(sem("choice_spread"), 1)
            for t in range(T):
                last = w.tensor_scalar(one_hot[:, t, :], ps[6][:, :], table("tok_col")[:, t:t + 1], None, ALU.is_equal)
            last.then_inc(sem("one_hot"), 1)
            w.tensor_copy(places, ps[7][:, 0:NE])
            w.tensor_copy(affinity, ps[7][:, NE:2 * NE])
            v.drain()
            def expert(e, first=False):
                v.wait_ge(sem("chosen_tokens_copied"), 2 if first else 2 + KT)
                w.tensor_copy(expert_x, chosen_x_t[:, :, bass.ds(e * CAP, CAP)])
                w.tensor_scalar(placing, table("tok_row"), places[:, bass.ds(e, 1)], affinity[:, bass.ds(e, 1)], ALU.is_equal, ALU.mult)
                v.drain().then_inc(sem("expert_tokens"), 1)
                if first:
                    v.wait_ge(sem("chosen_tokens"), 2 + KT)
                    w.memset(hidden[64:P, 5, :], 0.0)
                    w.memset(out_quarters, 0.0)
                for b, (c0, n) in enumerate(PIECES):
                    v.wait_ge(sem("expert_silu"), e * 3 + b + 1)
                    for odd in range(2):
                        m = 2 if odd == 0 or b < 2 else 1
                        blocks = lambda y: y.rearrange("p (m n) -> p m n", n=P)[:, odd::2, :][:, 0:m, :]
                        last = w.tensor_mul(hidden[64 * odd:64 * odd + 64, 2 * b:2 * b + m, :], blocks(expert_gate[0:64, c0:c0 + n]), blocks(ps[b][64:P, 0:n]))
                    last.then_inc(sem("expert_hidden"), 1)
                v.wait_ge(sem("down_free"), e * FT + FT + D_RING)
                for q in (2, 3):
                    last = w.tensor_copy(out_quarters[32 * q:32 * q + 32, 256 * q:256 * q + 256], ps[5][32 * q:32 * q + 32, 0:256])
                last.then_inc(sem("expert_out"), 1)
                for t in range(T):
                    v.wait_ge(sem("expert_placed"), e * T + t + 1)
                    for nh in range(2):
                        xs = x[:, t, nh * 512:(nh + 1) * 512]
                        last = w.tensor_add(xs, xs, ps[OUT_BANKS[2 * t + nh]][:, :])
                    last.then_inc(sem("expert_added"), 1)
                v.drain()
            expert(0, True)
            with v.Fori(1, NE) as e:
                expert(e)
            for t in range(T):
                rms(2, t, x, "final_rows")


_INS = ["x", "w_in", "gdn_conv_w", "gdn_a_log", "gdn_dt_bias", "gdn_norm_g", "w_out", "ln1_g", "ln1_b", "w_up",
        "ffn_conv_w", "ffn_conv_b", "w_down", "ln2_g", "ln2_b", "norm1_g_2", "w_in_2", "lam_q1_2", "lam_k1_2",
        "lam_q2_2", "lam_k2_2", "subln_g_2", "w_out_2", "rel_bias_2", "norm2_g_2", "w_router_2", "w_gate_2",
        "w_up_2", "w_down_2", "norm_f_g_2"]


def kernel(**inputs):
    import concourse.bacc as bacc
    from concourse.bass_utils import run_bass_kernel_spmd

    nc = bacc.Bacc("TRN2", target_bir_lowering=False, num_devices=1)
    consts, cat = constants()
    table, takes = bias_tables()
    arrays = {"consts": consts, "bias_table": table, "takes": takes}
    for name in _INS:
        v = np.ascontiguousarray(inputs[name])
        arrays[name] = v.reshape(1, -1) if v.ndim == 1 else v
    a = {name: nc.dram_tensor("in_" + name, v.shape, mybir.dt.from_np(v.dtype), kind="ExternalInput").ap() for name, v in arrays.items()}
    out = nc.dram_tensor("out", (1, S, D), F32, kind="ExternalOutput").ap()
    scratch = nc.dram_tensor("bias_rows", (BIAS_HEADS, P * 2 * S), F32, kind="Internal").ap()
    build(nc, a, out, scratch, cat)
    r = run_bass_kernel_spmd(nc, [{"in_" + name: v for name, v in arrays.items()}], core_ids=[0])
    return r.results[0]["out"]
```
